# Optimizing a Trainium2 kernel written in Bass

```python
import math
import jax, jax.numpy as jnp
from jax import lax
import numpy as np

D_MODEL = 2048
BATCH = 1
SEQ = 1024
DEPTH = 1
DEC_BATCH = 1
DEC_SEQ = 32
PAST_LEN = 512

CHUNK = 64
D_MIX = D_MODEL
D_ATT = D_MIX // 2
D_SSM = D_MIX - D_ATT
HEAD_DIM = 128
N_HEADS = D_ATT // HEAD_DIM
SSM_GROUP = 16
N_GROUPS = D_SSM // SSM_GROUP
STATE = 64
D_PLE = 256
Q_BLOCK = 128
EPS = 1e-6
NEG_INF = -1e30

OFF_K = D_ATT
OFF_V = 2 * D_ATT
OFF_F = 3 * D_ATT
OFF_GA = 3 * D_ATT + N_HEADS
OFF_U = 4 * D_ATT + N_HEADS
OFF_GS = OFF_U + D_SSM
D_IN = OFF_GS + D_SSM

kernel_name = 'fox_s5_hymba_stream_step'

def _rmsnorm(x, g):
    xf = x.astype(jnp.float32)
    y = xf * lax.rsqrt(jnp.mean(xf * xf, axis=-1, keepdims=True) + EPS)
    return (y * g.astype(jnp.float32)).astype(x.dtype)

def _fox_block(q, cq, qpos, k, v, ck_t, kpos):
    s = jnp.einsum('bthd,bshd->bhts', q, k, preferred_element_type=jnp.float32) * (HEAD_DIM ** -0.5)
    bias = jnp.transpose(cq.astype(jnp.float32), (0, 2, 1))[..., :, None] - ck_t[:, :, None, :]
    mask = kpos[None, :] <= qpos[:, None]
    s = jnp.where(mask, s + bias, NEG_INF)
    pr = jax.nn.softmax(s, axis=-1)
    return jnp.einsum('bhts,bshd->bthd', pr.astype(v.dtype), v)

def _fox_attention(q, cq, qpos, k, v, ck, kpos):
    b, t = q.shape[0], q.shape[1]
    ck_t = jnp.transpose(ck.astype(jnp.float32), (0, 2, 1))
    if t <= Q_BLOCK:
        return _fox_block(q, cq, qpos, k, v, ck_t, kpos)
    nb = t // Q_BLOCK
    qb = q.reshape(b, nb, Q_BLOCK, N_HEADS, HEAD_DIM).transpose(1, 0, 2, 3, 4)
    cqb = cq.reshape(b, nb, Q_BLOCK, N_HEADS).transpose(1, 0, 2, 3)
    pb = qpos.reshape(nb, Q_BLOCK)
    ob = lax.map(lambda a: _fox_block(a[0], a[1], a[2], k, v, ck_t, kpos), (qb, cqb, pb))
    return ob.transpose(1, 0, 2, 3, 4).reshape(b, t, N_HEADS, HEAD_DIM)

def _ssm_combine(left, right):
    a1, b1 = left
    a2, b2 = right
    return a1 * a2, a2 * b1 + b2

def _s5(u, h0_re, h0_im, a_re, a_im, log_dt, b_re, b_im, c_re, c_im, d_skip, w_glu):
    f32 = jnp.float32
    b, t, _ = u.shape
    ug = u.astype(f32).reshape(b, t, N_GROUPS, SSM_GROUP)
    lam = lax.complex(a_re.astype(f32), a_im.astype(f32))
    dt = jnp.exp(log_dt.astype(f32))[:, None]
    a_bar = jnp.exp(lam * dt)
    b_bar = ((a_bar - 1.0) / lam)[:, :, None] * lax.complex(b_re.astype(f32), b_im.astype(f32))
    bu = jnp.einsum('gpc,btgc->btgp', b_bar, ug.astype(jnp.complex64))
    if h0_re is not None:
        h0 = lax.complex(h0_re.astype(f32), h0_im.astype(f32))
        bu = bu.at[:, 0].add(a_bar * h0)
    a_seq = jnp.broadcast_to(a_bar, (1, t, N_GROUPS, STATE))
    _, hs = lax.associative_scan(_ssm_combine, (a_seq, bu), axis=1)
    c = lax.complex(c_re.astype(f32), c_im.astype(f32))
    y = jnp.real(jnp.einsum('gcp,btgp->btgc', c, hs)) + d_skip.astype(f32).reshape(N_GROUPS, SSM_GROUP) * ug
    y = jax.nn.gelu(y.reshape(b, t, D_SSM))
    y = y * jax.nn.sigmoid(y @ w_glu.astype(f32))
    h_last = hs[:, -1]
    return y.astype(u.dtype), jnp.real(h_last), jnp.imag(h_last)

def _layer(h, pe, past, g_in, w_in, b_f, a_re, a_im, log_dt, b_re, b_im, c_re, c_im,
           d_skip, w_glu, w_out, w_pe, g_pe, w_pg):
    bsz, t, _ = h.shape
    n = _rmsnorm(h, g_in)
    z = n @ w_in
    q, k, v, fl, ga, u, gs = jnp.split(z, [OFF_K, OFF_V, OFF_F, OFF_GA, OFF_U, OFF_GS], axis=-1)
    q = q.reshape(bsz, t, N_HEADS, HEAD_DIM)
    k = k.reshape(bsz, t, N_HEADS, HEAD_DIM)
    v = v.reshape(bsz, t, N_HEADS, HEAD_DIM)
    logf = jax.nn.log_sigmoid((fl + b_f).astype(jnp.float32))
    if past is None:
        k_all, v_all, logf_all, h0_re, h0_im = k, v, logf, None, None
        n_past = 0
    else:
        k_past, v_past, logf_past, h0_re, h0_im = past
        n_past = k_past.shape[1]
        k_all = jnp.concatenate([k_past.astype(k.dtype), k], axis=1)
        v_all = jnp.concatenate([v_past.astype(v.dtype), v], axis=1)
        logf_all = jnp.concatenate([logf_past.astype(jnp.float32), logf], axis=1)
    c_all = jnp.cumsum(logf_all, axis=1)
    kpos = jnp.arange(n_past + t)
    qpos = n_past + jnp.arange(t)
    att = _fox_attention(q, c_all[:, n_past:], qpos, k_all, v_all, c_all, kpos).reshape(bsz, t, D_ATT)
    ssm, s_re, s_im = _s5(u, h0_re, h0_im, a_re, a_im, log_dt, b_re, b_im, c_re, c_im, d_skip, w_glu)
    mixed = jnp.concatenate([att * jax.nn.silu(ga), ssm * jax.nn.silu(gs)], axis=-1)
    h = h + mixed @ w_out
    e = _rmsnorm(pe @ w_pe, g_pe)
    h = h + e * jax.nn.sigmoid(h @ w_pg)
    return h, k, v, logf, s_re, s_im

def _trunk(x, p, past, g_in, w_in, b_f, a_re, a_im, log_dt, b_re, b_im, c_re, c_im,
           d_skip, w_glu, w_out, w_pe, g_pe, w_pg, g_final):
    h = x
    ks, vs, lfs, srs, sis = [], [], [], [], []
    for i in range(DEPTH):
        lp = None if past is None else (past[0][i], past[1][i], past[2][i], past[3][i], past[4][i])
        h, k, v, lf, sr, si = _layer(h, p[i], lp, g_in[i], w_in[i], b_f[i], a_re[i], a_im[i], log_dt[i],
                                     b_re[i], b_im[i], c_re[i], c_im[i], d_skip[i], w_glu[i], w_out[i],
                                     w_pe[i], g_pe[i], w_pg[i])
        ks.append(k)
        vs.append(v)
        lfs.append(lf)
        srs.append(sr)
        sis.append(si)
    y = _rmsnorm(h, g_final)
    return y, jnp.stack(ks), jnp.stack(vs), jnp.stack(lfs), jnp.stack(srs), jnp.stack(sis)

def setup_inputs(seed: int = 0) -> dict:
    key = jax.random.key(seed)
    ks = jax.random.split(key, 32)
    nrm = jax.random.normal
    f32 = jnp.float32
    x_prompt = nrm(ks[0], (BATCH, SEQ, D_MODEL), f32)
    x_sample = nrm(ks[1], (DEC_BATCH, DEC_SEQ, D_MODEL), f32)
    p_prompt = nrm(ks[2], (DEPTH, BATCH, SEQ, D_PLE), f32)
    p_sample = nrm(ks[3], (DEPTH, DEC_BATCH, DEC_SEQ, D_PLE), f32)
    cache_k = nrm(ks[4], (DEPTH, DEC_BATCH, PAST_LEN, N_HEADS, HEAD_DIM), f32)
    cache_v = nrm(ks[5], (DEPTH, DEC_BATCH, PAST_LEN, N_HEADS, HEAD_DIM), f32)
    cache_logf = jax.nn.log_sigmoid(2.0 + nrm(ks[6], (DEPTH, DEC_BATCH, PAST_LEN, N_HEADS), f32))
    state_ssm_re = 0.1 * nrm(ks[7], (DEPTH, DEC_BATCH, N_GROUPS, STATE), f32)
    state_ssm_im = 0.1 * nrm(ks[8], (DEPTH, DEC_BATCH, N_GROUPS, STATE), f32)
    g_in = 1.0 + 0.02 * nrm(ks[9], (DEPTH, D_MODEL), f32)
    w_in = nrm(ks[10], (DEPTH, D_MODEL, D_IN), f32) * D_MODEL ** -0.5
    b_f = 2.0 + 0.1 * nrm(ks[11], (DEPTH, N_HEADS), f32)
    a_re = -0.5 + 0.01 * nrm(ks[12], (DEPTH, N_GROUPS, STATE), f32)
    a_im = math.pi * jnp.arange(STATE, dtype=f32) + 0.01 * nrm(ks[13], (DEPTH, N_GROUPS, STATE), f32)
    log_dt = jax.random.uniform(ks[14], (DEPTH, N_GROUPS), f32, math.log(1e-3), math.log(1e-1))
    b_re = nrm(ks[15], (DEPTH, N_GROUPS, STATE, SSM_GROUP), f32) * (2 * SSM_GROUP) ** -0.5
    b_im = nrm(ks[16], (DEPTH, N_GROUPS, STATE, SSM_GROUP), f32) * (2 * SSM_GROUP) ** -0.5
    c_re = nrm(ks[17], (DEPTH, N_GROUPS, SSM_GROUP, STATE), f32) * STATE ** -0.5
    c_im = nrm(ks[18], (DEPTH, N_GROUPS, SSM_GROUP, STATE), f32) * STATE ** -0.5
    d_skip = nrm(ks[19], (DEPTH, D_SSM), f32)
    w_glu = nrm(ks[20], (DEPTH, D_SSM, D_SSM), f32) * D_SSM ** -0.5
    w_out = nrm(ks[21], (DEPTH, D_MIX, D_MODEL), f32) * D_MIX ** -0.5
    w_pe = nrm(ks[22], (DEPTH, D_PLE, D_MODEL), f32) * D_PLE ** -0.5
    g_pe = 1.0 + 0.02 * nrm(ks[23], (DEPTH, D_MODEL), f32)
    w_pg = nrm(ks[24], (DEPTH, D_MODEL, D_MODEL), f32) * D_MODEL ** -0.5
    g_final = 1.0 + 0.02 * nrm(ks[25], (D_MODEL,), f32)
    return {'x_prompt': x_prompt, 'x_sample': x_sample, 'p_prompt': p_prompt, 'p_sample': p_sample,
            'cache_k': cache_k, 'cache_v': cache_v, 'cache_logf': cache_logf,
            'state_ssm_re': state_ssm_re, 'state_ssm_im': state_ssm_im,
            'g_in': g_in, 'w_in': w_in, 'b_f': b_f, 'a_re': a_re, 'a_im': a_im, 'log_dt': log_dt,
            'b_re': b_re, 'b_im': b_im, 'c_re': c_re, 'c_im': c_im, 'd_skip': d_skip, 'w_glu': w_glu,
            'w_out': w_out, 'w_pe': w_pe, 'g_pe': g_pe, 'w_pg': w_pg, 'g_final': g_final}

def reference(x_prompt, x_sample, p_prompt, p_sample, cache_k, cache_v, cache_logf,
              state_ssm_re, state_ssm_im, g_in, w_in, b_f, a_re, a_im, log_dt, b_re, b_im,
              c_re, c_im, d_skip, w_glu, w_out, w_pe, g_pe, w_pg, g_final):
    y_prompt, k_p, v_p, lf_p, sr_p, si_p = _trunk(
        x_prompt, p_prompt, None, g_in, w_in, b_f, a_re, a_im, log_dt, b_re, b_im, c_re, c_im,
        d_skip, w_glu, w_out, w_pe, g_pe, w_pg, g_final)
    y_sample, k_s, v_s, lf_s, sr_s, si_s = _trunk(
        x_sample, p_sample, (cache_k, cache_v, cache_logf, state_ssm_re, state_ssm_im),
        g_in, w_in, b_f, a_re, a_im, log_dt, b_re, b_im, c_re, c_im,
        d_skip, w_glu, w_out, w_pe, g_pe, w_pg, g_final)
    return (y_prompt, y_sample, k_p, v_p, lf_p, sr_p, si_p, k_s, v_s, lf_s, sr_s, si_s)


_drawn_inputs = setup_inputs


def setup_inputs(seed=0):
    import zlib

    import numpy as np

    out = dict(_drawn_inputs(seed))
    spreads = {}
    factors = {'cache_logf': 4.113,
     'g_in': 2.719,
     'a_re': 4.211,
     'c_re': 4.703,
     'c_im': 4.637,
     'g_pe': 6.106,
     'g_final': 2.713}
    for name, (base, spread) in spreads.items():
        noise = np.random.default_rng([zlib.crc32(name.encode()), seed]).standard_normal(out[name].shape)
        drawn = base * np.exp(spread * noise) if base else spread * noise
        out[name] = __import__('jax').numpy.asarray(drawn.astype(out[name].dtype))
    for name, factor in factors.items():
        out[name] = (out[name] * factor).astype(out[name].dtype)
    return out
```

```python
import math
from contextlib import ExitStack

import numpy as np

import concourse.bass as bass
from concourse import mybir
from concourse.alu_op_type import AluOpType as ALU

P = 128
F32 = mybir.dt.float32
F32R = mybir.dt.float32r
BF16 = mybir.dt.bfloat16
ACT = mybir.ActivationFunctionType
AX_X = mybir.AxisListType.X

T_PROMPT, T_SAMPLE, T_PAST = 1024, 32, 512
T = T_PROMPT + T_SAMPLE
D_MODEL = 2048
KD = D_MODEL // P
D_ATT = D_SSM = 1024
KS = D_SSM // P
HEADS, HD = 8, 128
GROUPS, GC, ST = 64, 16, 64
D_PLE = 256
KP = D_PLE // P
EPS = 1e-6
NEG = -1e30
L = 8
NJ = T // L
NJP = T_PROMPT // L
NC = 3
CH = T // NC
TT = T_PROMPT // P
OFF_F = 3 * D_ATT
OFF_GA = OFF_F + HEADS
OFF_U = OFF_GA + D_ATT
OFF_GS = OFF_U + D_SSM
PB = 4
NPB = GROUPS // PB


class Chain:

    def __init__(self, eng, sem):
        self.eng, self.sem, self.base, self.n = eng, sem, 0, 0

    def link(self, ins):
        ins.then_inc(self.sem, 1)
        self.n += 1
        self.eng.wait_ge(self.sem, self.base + self.n)

    def enter_loop(self, i, per_iteration):
        self.before = self.base + self.n
        self.base, self.n, self.per = self.before + i * per_iteration, 0, per_iteration

    def leave_loop(self, iterations):
        assert self.n == self.per, (self.n, self.per)
        self.base, self.n = self.before + iterations * self.per, 0


def allocators(nc, ctx):
    def sb(name, shape, dt=F32):
        return ctx.enter_context(nc.sbuf_tensor(name, shape, dt))

    def ps(name, shape, dt=F32):
        return ctx.enter_context(nc.psum_tensor(name, shape, dt))

    def sem(name):
        return ctx.enter_context(nc.semaphore(name))

    return sb, ps, sem


def gemm_tile(pe, acc, w_hi, w_lo, a_hi, a_lo, kt, act_ready=None, hooks=None):
    for k in range(kt):
        if act_ready is not None:
            pe.wait_ge(act_ready, k + 1)
        if hooks and k in hooks:
            hooks[k]()
        for n, (w, a) in enumerate(((w_hi, a_hi), (w_hi, a_lo), (w_lo, a_hi))):
            for c in range(NC):
                mm = pe.matmul(acc[:, c, 0:CH], w[:, k, :], a[:, k, c * CH:(c + 1) * CH],
                               start=(k == 0 and n == 0), stop=(k == kt - 1 and n == 2))
    return mm


class Weights:

    def __init__(self, sb, sem, name, kt):
        self.kt, self.kh = kt, kt // 2
        self.raw = [sb(f"{name}_raw{h}", [P, self.kh, P]) for h in range(2)]
        self.hi = [sb(f"{name}_hi{b}", [P, kt, P], F32R) for b in range(2)]
        self.lo = [sb(f"{name}_lo{b}", [P, kt, P], F32R) for b in range(2)]
        self.loaded = [sem(f"{name}_loaded{h}") for h in range(2)]
        self.hi_done = sem(f"{name}_hi_done")
        self.split = [sem(f"{name}_split{h}") for h in range(2)]
        self.gemm_done = sem(f"{name}_gemm_done")

    def load(self, sp, w, col, n):
        for h in range(2):
            sp.wait_ge(self.split[h], n)
            sp.dma_start(self.raw[h][:], w[:, h * self.kh:(h + 1) * self.kh, bass.ds(col, P)]) \
              .then_inc(self.loaded[h], 16)

    def split_tile(self, dve, nc, n, b, in_use):
        if in_use:
            dve.wait_ge(self.gemm_done, n - 1)
        for h in range(2):
            dve.wait_ge(self.loaded[h], (n + 1) * 16)
            nc.vector.tensor_copy(self.hi[b][:, h * self.kh:(h + 1) * self.kh], self.raw[h][:]) \
              .then_inc(self.hi_done, 1)
        for h in range(2):
            part = slice(h * self.kh, (h + 1) * self.kh)
            dve.wait_ge(self.hi_done, n * 2 + h + 1)
            nc.vector.tensor_tensor(self.lo[b][:, part], self.raw[h][:], self.hi[b][:, part].bitcast(F32),
                                    ALU.subtract).then_inc(self.split[h], 1)


def settle(eng, passed):
    eng.sem_inc(passed, 1)


def identity(nc, pool, ident, chain):
    chain.link(nc.gpsimd.memset(ident[:], 0.0))
    chain.link(nc.gpsimd.affine_select(out=ident[:], in_=ident[:], compare_op=ALU.not_equal, fill=1.0, base=0,
                                       pattern=[[-1, P]], channel_multiplier=1))



def stage_norm(nc, d, G):
    with ExitStack() as ctx:
        sb, ps, sem = allocators(nc, ctx)
        x_in = [sb(f"x_in{b}", [P, D_MODEL]) for b in range(2)]
        sq = sb("sq", [P, D_MODEL])
        ssq = [sb(f"ssq{b}", [P, 4]) for b in range(2)]
        rstd_rows = sb("rstd_rows", [P, P])
        rstd_bc = sb("rstd_bc", [P, P])
        ones = sb("ones", [P, P])
        xT = [sb(f"xT{b}", [P, KD, P]) for b in range(2)]
        nT = sb("nT", [P, KD, P])
        g_col = sb("g_col", [P, KD])
        zeros = sb("zeros", [P, 1024])
        xT_ps = ps("xT_ps", [P, 4, 512])
        bc_ps = ps("bc_ps", [P, 512])
        x_loaded = [sem(f"x_loaded{b}") for b in range(2)]
        x_squared, x_turned, xT_copied, xT_stored = sem("x_squared"), sem("x_turned"), sem("xT_copied"), \
            [G["sem"][f"xT_stored{b}"] for b in range(2)]
        var_done, std_done, rows_done, bc_turned, n_split, consts, g_loaded = (
            sem(n) for n in ("var_done", "std_done", "rows_done", "bc_turned", "n_split", "consts", "g_loaded"))
        dve_order, pool_order, zero_stored = sem("dve_order"), sem("pool_order"), G["sem"]["zero_stored"]
        bc_copied = sem("bc_copied")
        block = ctx.enter_context(nc.Block())
        n_hi, n_lo = G["n_hi"], G["n_lo"]
        x_tiles = d["x_prompt"].rearrange("a (i p) c -> (a i) p c", p=P)
        xT_dram = d["xT"].rearrange("(f p) t -> p f t", p=P)

        @block.sync
        def _(sp):
            with nc.allow_non_contiguous_dma("per-feature columns of the gain"):
                sp.dma_start(g_col[:], d["g_in"][0].rearrange("(k p) -> p k", p=P)).then_inc(g_loaded, 16)
            for b in range(2):
                sp.dma_start(x_in[b][:], x_tiles[b]).then_inc(x_loaded[b], 16)
            with sp.Fori(0, TT // 2 - 1) as i:
                for b in range(2):
                    sp.wait_ge(x_squared, i * 2 + b + 1)
                    sp.wait_ge(x_turned, i * 2 + b + 1)
                    sp.dma_start(x_in[b][:], x_tiles[i * 2 + (b + 2)]).then_inc(x_loaded[b], 16)
            sp.wait_ge(x_squared, TT - 1)
            sp.wait_ge(x_turned, TT - 1)
            sp.dma_start(x_in[0][0:T_SAMPLE, :], d["x_sample"][0]).then_inc(x_loaded[0], 16)

        @block.gpsimd
        def _(pool):
            chain = Chain(pool, pool_order)
            identity(nc, pool, G["ident"], chain)
            nc.gpsimd.memset(zeros[:], 0.0)
            chain.link(nc.gpsimd.memset(ones[:], 1.0))
            chain.link(nc.gpsimd.memset(G["eps"][:], EPS))
            nc.gpsimd.memset(G["ones_col"][:], 1.0).then_inc(consts, 1)
            for q in range(GROUPS * P // 1024):
                pool.dma_start(d["toep"].rearrange("p g m -> p (g m)")[:, q * 1024:(q + 1) * 1024], zeros[:]) \
                    .then_inc(zero_stored, 16)

            def store(n, b, it, width):
                pool.wait_ge(xT_copied, n * 4 + 4)
                pool.dma_start(xT_dram[:, :, bass.ds(n * P, width)], xT[b][:, :, 0:width]) \
                    .then_inc(xT_stored[b], 16)

            with pool.Fori(0, TT // 2) as i:
                for b in range(2):
                    store(i * 2 + b, b, i, P)
            store(TT, 0, TT // 2, T_SAMPLE)
            pool.wait_ge(zero_stored, 16 * GROUPS * P // 1024)
            pool.wait_ge(xT_stored[0], 16 * (TT // 2 + 1))
            pool.wait_ge(xT_stored[1], 16 * (TT // 2))

        def norm_tile_act(act, n, b, it, rows):
            act.wait_ge(x_loaded[b], it * 16 + 16)
            nc.scalar.activation(sq[0:rows, :], x_in[b][0:rows, :], ACT.Square,
                                 accum_out=ssq[b][0:rows, 0:1]).then_inc(x_squared, 1)
            act.wait_ge(var_done, n + 1)
            nc.scalar.activation(ssq[b][0:rows, 2:3], ssq[b][0:rows, 1:2], ACT.Sqrt).then_inc(std_done, 1)
            for f in range(4):
                act.wait_ge(x_turned, n + 1)
                if f == 0:
                    act.wait_ge(xT_stored[b], it * 16)
                    act.wait_ge(n_split, n)
                nc.scalar.copy(xT[b][:, 4 * f:4 * f + 4, 0:rows],
                               xT_ps[:, f, :].rearrange("p (q t) -> p q t", q=4)[:, :, 0:rows]) \
                    .then_inc(xT_copied, 1)

        @block.scalar
        def _(act):
            with act.Fori(0, TT // 2) as i:
                for b in range(2):
                    norm_tile_act(act, i * 2 + b, b, i, P)
            norm_tile_act(act, TT, 0, TT // 2, T_SAMPLE)

        def norm_tile_pe(pe, n, b, it, rows):
            pe.wait_ge(x_loaded[b], it * 16 + 16)
            pe.wait_ge(xT_copied, n * 4)
            for f in range(KD):
                tr = pe.transpose(xT_ps[:, f // 4, (f % 4) * P:(f % 4) * P + rows],
                                  x_in[b][0:rows, f * P:(f + 1) * P], G["ident"][0:rows, 0:rows])
            tr.then_inc(x_turned, 1)
            pe.wait_ge(rows_done, n + 1)
            pe.transpose(bc_ps[:, 0:rows], rstd_rows[0:rows, :], G["ident"][0:rows, 0:rows]).then_inc(bc_turned, 1)

        @block.tensor
        def _(pe):
            pe.wait_ge(consts, 1)
            with pe.Fori(0, TT // 2) as i:
                for b in range(2):
                    norm_tile_pe(pe, i * 2 + b, b, i, P)
            norm_tile_pe(pe, TT, 0, TT // 2, T_SAMPLE)

        def norm_tile_dve(dve, chain, n, b, it, rows):
            dve.wait_ge(x_squared, n + 1)
            nc.vector.tensor_scalar(ssq[b][0:rows, 1:2], ssq[b][0:rows, 0:1], 1.0 / D_MODEL, EPS, ALU.mult,
                                    ALU.add).then_inc(var_done, 1)
            dve.wait_ge(std_done, n + 1)
            chain.link(nc.vector.reciprocal(ssq[b][0:rows, 3:4], ssq[b][0:rows, 2:3]))
            nc.vector.tensor_scalar(rstd_rows[0:rows, :], ones[0:rows, :], ssq[b][0:rows, 3:4], None, ALU.mult) \
                .then_inc(rows_done, 1)
            dve.wait_ge(bc_turned, n + 1)
            chain.link(nc.vector.tensor_copy(rstd_bc[:, 0:rows], bc_ps[:, 0:rows]))
            for f in range(KD):
                if f % 4 == 0:
                    dve.wait_ge(xT_copied, n * 4 + (f // 4 + 1))
                last = nc.vector.scalar_tensor_tensor(nT[:, f, 0:rows], xT[b][:, f, 0:rows], g_col[:, f:f + 1],
                                                      rstd_bc[:, 0:rows], ALU.mult, ALU.mult)
            chain.link(last)
            chain.link(nc.vector.tensor_copy(n_hi[:, :, bass.ds(n * P, rows)], nT[:, :, 0:rows]))
            ins = nc.vector.tensor_tensor(n_lo[:, :, bass.ds(n * P, rows)], nT[:, :, 0:rows],
                                          n_hi[:, :, bass.ds(n * P, rows)].bitcast(F32), ALU.subtract)
            ins.then_inc(n_split, 1)
            dve.wait_ge(n_split, n + 1)

        @block.vector
        def _(dve):
            dve.wait_ge(consts, 1)
            dve.wait_ge(g_loaded, 16)
            chain = Chain(dve, dve_order)
            with dve.Fori(0, TT // 2) as i:
                chain.enter_loop(i, 8)
                for b in range(2):
                    norm_tile_dve(dve, chain, i * 2 + b, b, i, P)
                chain.leave_loop(TT // 2)
            norm_tile_dve(dve, chain, TT, 0, TT // 2, T_SAMPLE)



def stage_project(nc, d, G):
    tiles = 6 * D_ATT // P
    with ExitStack() as ctx:
        sb, ps, sem = allocators(nc, ctx)
        W = Weights(sb, sem, "w_in", KD)
        acc = [ps(f"acc{b}", [P, NC, 512]) for b in range(2)]
        bank_c = ps("bank_c", [P, 512])
        bank_w = ps("bank_w", [P, 512])
        z_out = sb("z_out", [P, T])
        evacuated = [sem(f"evacuated{b}") for b in range(2)]
        z_stored = sem("z_stored")
        v_swapped, y_stored, hl_stored, const_stored, gate_stored = (
            G["sem"][n] for n in ("v_swapped", "y_stored", "hl_stored", "const_stored", "gate_stored"))

        h0, carry = (sb(n, [P, 2, GROUPS]) for n in ("h0", "carry"))
        rho, turn = sb("rho", [P, GROUPS]), sb("turn", [P, 2, GROUPS])
        h_last = sb("h_last", [P, 2, GROUPS])

        arena = nc.sbuf_base
        a_raw = sb("a_raw", [GROUPS, 4, 2, ST])
        sgn = sb("sgn", [P, 2])
        lam_re, lam_im, dt, ang, mag, q_re, q_im = (
            sb(n, [P, GROUPS]) for n in ("lam_re", "lam_im", "dt", "ang", "mag", "q_re", "q_im"))
        rate = dt
        tmp = [sb(f"tmp{i}", [P, GROUPS]) for i in range(3)]
        pw_re, pw_im = (sb(n, [P, GROUPS, L + 1]) for n in ("pw_re", "pw_im"))
        b_blk = sb("b_blk", [P, 2, PB, GC])
        c_blk = sb("c_blk", [PB * GC, 2, 2, ST])
        bt = sb("bt", [P, 2, PB, GC])
        ct = sb("ct", [P, 2, PB, GC])
        tmp_b = tmp[2].rearrange("p (g c) -> p g c", g=PB)
        xin = sb("xin", [P, PB, L, GC])
        tmp_c = sb("tmp_c", [P, PB, L + 1, GC])
        ca = sb("ca", [P, PB, L + 1, GC])
        w_state_s = sb("w_state_s", [P, PB, P])
        kern = sb("kern", [GC, PB, L, GC])
        d_bc = sb("d_bc", [GC, PB * GC])
        d_diag = sb("d_diag", [GC, PB, GC])
        b_f = sb("b_f_s", [HEADS, 1])
        lf = z_out[0:HEADS, :]
        gate_past = sb("gate_past", [P, T_PAST // P, HEADS])
        negs_at = (nc.sbuf_base + 31) // 32 * 32
        negs = sb("negs", [HEADS, T_PAST + T])
        assert 8 * GROUPS * L <= 4 * (T_PAST + T)
        pw_back = nc.alloc_sbuf_tensor_at("pw_back", [P, 2, GROUPS, L], F32, offset=negs_at)
        sp_part = negs[:, 0:T]
        lf_rows = w_state_s.rearrange("p g m -> p (g m)")[:, 0:(TT + 1) * HEADS] \
            .rearrange("p (i h) -> p i h", h=HEADS)

        at = [(arena + 31) // 32 * 32]

        def placed(name, shape):
            t = nc.alloc_sbuf_tensor_at(name, shape, F32, offset=at[0])
            at[0] += -(-4 * int(np.prod(shape[1:])) // 32) * 32
            assert at[0] <= nc.sbuf_usable_end
            return t

        u_in = [placed(f"u_in{b}", [P, PB, NJ]) for b in range(2)]
        ws_in, toep_in, wr_in = (placed(n, [P, PB, P]) for n in ("ws_in", "toep_in", "wr_in"))
        v, va, vb = placed("v", [P, 2, PB, NJ]), placed("va", [P, PB, NJ]), placed("vb", [P, PB, NJ])
        rot = placed("rot", [P, 2, PB, NJ])
        h_prev = placed("h_prev", [P, PB, NJ + 1])
        h_rows = placed("h_rows", [GROUPS, 2, P])

        (u_loaded0, u_loaded1, ws_loaded, ro_loaded, v_done, v_copied, v_used, h_ready, y_done,
         y_copied, rot_ready, hl_ready, hl_turned, hl_copied, arena_free, hist_zero) = (
            sem(n) for n in ("u_loaded0", "u_loaded1", "ws_loaded", "ro_loaded", "v_done", "v_copied",
                             "v_used", "h_ready", "y_done", "y_copied", "rot_ready", "hl_ready",
                             "hl_turned", "hl_copied", "arena_free", "hist_zero"))
        u_loaded = (u_loaded0, u_loaded1)
        small_loaded, b_loaded, c_loaded = sem("small_loaded"), sem("b_loaded"), sem("c_loaded")
        sgn_set, raw_turned, dve_order = sem("sgn_set"), sem("raw_turned"), sem("dve_order")
        dt_done, arg_done, mag_done, sin_done, cos_arg, cos_done = (
            sem(n) for n in ("dt_done", "arg_done", "mag_done", "sin_done", "cos_arg", "cos_done"))
        b_used, c_turned, c_taken, xin_done, w_turned, w_copied, ca_done, k_done, k_copied, d_added = (
            sem(n) for n in ("b_used", "c_turned", "c_taken", "xin_done", "w_turned", "w_copied", "ca_done",
                             "k_done", "k_copied", "d_added"))
        gate_in, gate_abs, gate_exp, gate_ln, past_turned, lf_done, lf_turned, lf_copied, negc_done = (
            sem(n) for n in ("gate_in", "gate_abs", "gate_exp", "gate_ln", "past_turned", "lf_done", "lf_turned",
                             "lf_copied", "negc_done"))
        block = ctx.enter_context(nc.Block())
        ident = G["ident"]
        n_small = 11

        w_in = d["w_in"][0].rearrange("(k p) n -> p k n", p=P)
        zT, uT = d["zT"], d["uT"].rearrange("r k j -> r (k j)")
        u_src = d["uT"][0:D_SSM].rearrange("(g c) k j -> k c g j", c=GC)
        y_dst = d["yT"].rearrange("(g c) k j -> k c g j", c=GC)
        b_re, b_im = (d[n][0].rearrange("g p c -> p g c") for n in ("b_re", "b_im"))
        c_re, c_im = (d[n][0].rearrange("g c p -> (g c) p") for n in ("c_re", "c_im"))

        @block.sync
        def _(sp):
            W.load(sp, w_in, OFF_F, 0)
            with nc.allow_non_contiguous_dma("small constants"):
                for h in range(2):
                    sp.dma_start(a_raw[:, 0, h, :], d["a_re"][0]).then_inc(small_loaded, 16)
                    sp.dma_start(a_raw[:, 1, h, :], d["a_im"][0]).then_inc(small_loaded, 16)
                    sp.dma_start(a_raw[:, 2 + h, 0, :], d["state_ssm_im" if h else "state_ssm_re"][0, 0]) \
                        .then_inc(small_loaded, 16)
                    sp.dma_start(a_raw[:, 2 + h, 1, :], d["state_ssm_re" if h else "state_ssm_im"][0, 0]) \
                        .then_inc(small_loaded, 16)
                sp.dma_start(dt[:], d["log_dt"].to_broadcast([P, GROUPS])).then_inc(small_loaded, 16)
                sp.dma_start(b_f[:], d["b_f"].rearrange("a h -> h a")).then_inc(small_loaded, 16)
                sp.dma_start(gate_past[:], d["cache_logf"][0, 0].rearrange("(i p) h -> p i h", p=P)) \
                    .then_inc(small_loaded, 16)

            def load_block(i):
                sp.wait_ge(b_used, i)
                sp.wait_ge(d_added, i)
                for part, (top, bottom) in enumerate(((b_re, b_im), (b_im, b_re))):
                    sp.dma_start(b_blk[0:ST, part], top[:, bass.ds(i * PB, PB), :]).then_inc(b_loaded, 16)
                    sp.dma_start(b_blk[ST:P, part], bottom[:, bass.ds(i * PB, PB), :]).then_inc(b_loaded, 16)
                sp.dma_start(d_bc[:], d["d_skip"][:, bass.ds(i * PB * GC, PB * GC)].to_broadcast([GC, PB * GC])) \
                    .then_inc(b_loaded, 16)
                sp.wait_ge(c_turned, i)
                for part, (left, right) in enumerate(((c_re, c_im), (c_im, c_re))):
                    sp.dma_start(c_blk[:, part, 0], left[bass.ds(i * PB * GC, PB * GC)]).then_inc(c_loaded, 16)
                    sp.dma_start(c_blk[:, part, 1], right[bass.ds(i * PB * GC, PB * GC)]).then_inc(c_loaded, 16)

            with nc.allow_non_contiguous_dma("64-byte rows of B"):
                with sp.Fori(0, 8) as i:
                    W.load(sp, w_in, i * (2 * P) + OFF_U, i * 2 + 1)
                    load_block(i)
                    W.load(sp, w_in, i * (2 * P) + (OFF_U + P), i * 2 + 2)
                with sp.Fori(8, NPB) as i:
                    W.load(sp, w_in, i * (2 * P) - 16 * P, i * 2 + 1)
                    load_block(i)
                    W.load(sp, w_in, i * (2 * P) - 15 * P, i * 2 + 2)

            def load_u(q, b):
                for k in range(L):
                    sp.dma_start(u_in[b][k * GC:(k + 1) * GC], u_src[k][:, bass.ds(q * PB, PB), :]) \
                        .then_inc(u_loaded[b], 16)

            def load_state(q):
                sp.wait_ge(v_done, q)
                sp.dma_start(ws_in[:], d["w_state"][:, bass.ds(q * PB, PB), :]).then_inc(ws_loaded, 16)

            def load_readout(q):
                sp.wait_ge(y_done, q)
                sp.dma_start(toep_in[:], d["toep"][:, bass.ds(q * PB, PB), :]).then_inc(ro_loaded, 16)
                sp.dma_start(wr_in[:], d["w_read"][:, bass.ds(q * PB, PB), :]).then_inc(ro_loaded, 16)

            n0 = 2 * NPB + 1
            W.load(sp, w_in, 2 * D_ATT, n0)
            sp.wait_ge(z_stored, 16 * (n0 - 1))
            sp.wait_ge(arena_free, 1)
            load_u(0, 0)
            load_state(0)
            W.load(sp, w_in, 2 * D_ATT + P, n0 + 1)
            load_readout(0)
            load_u(1, 1)
            load_state(1)

            def recur_loads(i, col):
                for b in range(2):
                    q = i * 2 + b
                    W.load(sp, w_in, col + b * P, q + n0)
                    load_readout(q - 1)
                    sp.wait_ge(y_stored, (q - 1) * 128)
                    load_u(q, b)
                    load_state(q)

            with sp.Fori(1, 4) as i:
                recur_loads(i, i * (2 * P) + 2 * D_ATT)
            with sp.Fori(4, 8) as i:
                recur_loads(i, i * (2 * P) + (OFF_GA - 8 * P))
            load_readout(NPB - 1)

        @block.gpsimd
        def _(pool):
            nc.gpsimd.memset(sgn[0:ST, 0:1], -1.0)
            nc.gpsimd.memset(sgn[ST:P, 0:1], 1.0)
            nc.gpsimd.memset(sgn[0:ST, 1:2], 1.0)
            nc.gpsimd.memset(sgn[ST:P, 1:2], -1.0).then_inc(sgn_set, 1)
            pool.wait_ge(negc_done, 1)
            pool.dma_start(d["negc"][:, 0:T_PROMPT], negs[:, 0:T_PROMPT]).then_inc(gate_stored, 16)
            pool.dma_start(d["negc"][:, T_PROMPT:], negs[:, T_PROMPT:]).then_inc(gate_stored, 16)
            pool.wait_ge(lf_copied, 1)
            pool.dma_start(d["logf_prompt"][0, 0].rearrange("(i p) h -> p i h", p=P), lf_rows[:, 0:TT]) \
                .then_inc(gate_stored, 16)
            pool.dma_start(d["logf_sample"][0, 0], lf_rows[0:T_SAMPLE, TT]).then_inc(gate_stored, 16)
            with pool.Fori(0, NPB) as i:
                pool.wait_ge(w_copied, i + 1)
                pool.dma_start(d["w_state"][:, bass.ds(i * PB, PB), :], w_state_s[:]).then_inc(const_stored, 16)
                pool.wait_ge(ca_done, i + 1)
                settle(pool, G["passed"])
                pool.dma_start(d["w_read"][:, bass.ds(i * PB, PB), :],
                               ca[:, :, 1:, :].rearrange("p g k c -> p g (k c)")).then_inc(const_stored, 16)
                pool.wait_ge(d_added, i + 1)
                settle(pool, G["passed"])
                for k in range(L):
                    pool.dma_start(d["toep"][k * GC:(k + 1) * GC, bass.ds(i * PB, PB), k * GC:],
                                   kern[:, :, 0:L - k, :].rearrange("p g k c -> p g (k c)")) \
                        .then_inc(const_stored, 16)
            pool.wait_ge(const_stored, 16 * (2 + L) * NPB)
            pool.wait_ge(gate_stored, 64)
            pool.wait_ge(d_added, NPB)
            pool.wait_ge(c_turned, NPB)
            pool.wait_ge(k_done, NPB)
            pool.wait_ge(z_stored, 16 * 2 * NPB)
            nc.gpsimd.memset(h_prev[:, :, 0:1], 0.0).then_inc(arena_free, 1)

            def swap(q):
                pool.wait_ge(v_copied, q * 2 + 2)
                pool.wait_ge(v_used, q)
                settle(pool, G["passed"])
                pool.dma_start(v[0:ST, 1], v[ST:P, 0]).then_inc(v_swapped, 16)
                pool.dma_start(v[ST:P, 1], v[0:ST, 0]).then_inc(v_swapped, 16)

            def store_y(q, b):
                pool.wait_ge(y_copied, q * 2 + 2)
                for k in range(L):
                    pool.dma_start(y_dst[k][:, bass.ds(q * PB, PB), :], u_in[b][k * GC:(k + 1) * GC]) \
                        .then_inc(y_stored, 16)

            swap(0)
            store_y(0, 0)
            swap(1)
            with pool.Fori(1, NPB // 2) as i:
                for b in range(2):
                    store_y(i * 2 + (b - 1), 1 - b)
                    swap(i * 2 + b)
            store_y(NPB - 1, 1)
            pool.wait_ge(hl_copied, 1)
            for s, names in enumerate((("ssm_re_prompt", "ssm_im_prompt"), ("ssm_re_sample", "ssm_im_sample"))):
                for h, name in enumerate(names):
                    pool.dma_start(d[name][0, 0], h_rows[:, s, h * ST:(h + 1) * ST]).then_inc(hl_stored, 16)
            pool.wait_ge(hl_stored, 64)
            pool.wait_ge(y_stored, 128 * NPB)

        @block.tensor
        def _(pe):
            def tile(n, b, it, hooks=None):
                pe.wait_ge(W.split[1], n + 1)
                pe.wait_ge(evacuated[b], it)
                gemm_tile(pe, acc[b], W.hi[b], W.lo[b], G["n_hi"], G["n_lo"], KD, hooks=hooks) \
                    .then_inc(W.gemm_done, 1)

            def turn_raw():
                pe.wait_ge(small_loaded, 16 * n_small)
                for q in range(4):
                    tr = pe.transpose(bank_c[:, q * GROUPS:(q + 1) * GROUPS],
                                      a_raw[:, q].rearrange("g h p -> g (h p)"), ident[0:GROUPS, 0:GROUPS])
                tr.then_inc(raw_turned, 1)
                for q in range(T_PAST // P):
                    tr = pe.transpose(bank_w[0:HEADS, q * P:(q + 1) * P], gate_past[:, q, :], ident[:])
                tr.then_inc(past_turned, 1)

            tile(0, 0, 0, {KD // 2: turn_raw})

            def turn_gates():
                pe.wait_ge(lf_done, 1)
                for q in range(TT + 1):
                    rows = P if q < TT else T_SAMPLE
                    tr = pe.transpose(bank_w[0:rows, q * HEADS:(q + 1) * HEADS], lf[:, q * P:q * P + rows],
                                      ident[0:HEADS, 0:HEADS])
                tr.then_inc(lf_turned, 1)

            def iteration(i, first=False):
                def turn_c():
                    pe.wait_ge(c_loaded, i * 64 + 64)
                    pe.wait_ge(k_copied, i)
                    settle(pe, G["passed"])
                    for q in range(2):
                        tr = pe.transpose(bank_c[:, q * PB * GC:(q + 1) * PB * GC],
                                          c_blk[:, q].rearrange("r h p -> r (h p)"),
                                          ident[0:PB * GC, 0:PB * GC])
                    tr.then_inc(c_turned, 1)

                def turn_state():
                    pe.wait_ge(xin_done, i + 1)
                    pe.wait_ge(w_copied, i)
                    pe.wait_ge(lf_copied, 1)
                    for g in range(PB):
                        tr = pe.transpose(bank_w[:, g * P:(g + 1) * P],
                                          xin[:, g].rearrange("p k c -> p (k c)"), ident[:])
                    tr.then_inc(w_turned, 1)

                def kernels():
                    pe.wait_ge(ca_done, i + 1)
                    for g in range(PB):
                        mm = pe.matmul(bank_c[0:GC, g * P:(g + 1) * P], bt[:, 0, g, :],
                                       ca[:, g, 0:L, :].rearrange("p k c -> p (k c)"), start=True, stop=True)
                    mm.then_inc(k_done, 1)
                return {2: turn_c, 11: turn_state}, {4: kernels}

            tile(1, 1, 0, {KD - 1: turn_gates})
            h2 = iteration(0)

            tile(2, 0, 1, {0: h2[0][2], 8: h2[0][11], 13: h2[1][4]})
            with pe.Fori(1, NPB) as i:
                first, second = iteration(i)
                tile(i * 2 + 1, 1, i, first)
                tile(i * 2 + 2, 0, i + 1, second)

            def states(q, b):
                pe.wait_ge(u_loaded[b], (q - b) * 64 + 128)
                pe.wait_ge(ws_loaded, q * 16 + 16)
                for g in range(PB):
                    if g % 2 == 0:
                        pe.wait_ge(y_copied, q * 2)
                    mm = pe.matmul((bank_c, bank_w)[g // 2][:, g % 2 * NJ:(g % 2 + 1) * NJ], ws_in[:, g],
                                   u_in[b][:, g], start=True, stop=True)
                mm.then_inc(v_done, 1)

            def readout(q, b):
                pe.wait_ge(h_ready, q + 1)
                pe.wait_ge(ro_loaded, q * 32 + 32)
                pe.wait_ge(v_copied, q * 2 + 2)
                for g in range(PB):
                    out = (bank_c, bank_w)[g // 2][:, g % 2 * NJ:(g % 2 + 1) * NJ]
                    pe.matmul(out, toep_in[:, g], u_in[b][:, g], start=True, stop=False)
                    mm = pe.matmul(out, wr_in[:, g], h_prev[:, g, 0:NJ], start=False, stop=True)
                mm.then_inc(y_done, 1)

            def recur_hooks(q, b, first=False):
                hooks = {5: lambda: states(q, b)}
                if not first:
                    hooks[1] = lambda: readout(q - 1, 1 - b)
                return hooks

            first_states = {5: lambda: (pe.wait_ge(arena_free, 1), states(0, 0))}
            tile(2 * NPB + 1, 1, NPB, first_states)
            tile(2 * NPB + 2, 0, NPB + 1, recur_hooks(1, 1))
            with pe.Fori(1, NPB // 2) as i:
                tile(i * 2 + (2 * NPB + 1), 1, i + NPB, recur_hooks(i * 2, 0))
                tile(i * 2 + (2 * NPB + 2), 0, i + (NPB + 1), recur_hooks(i * 2 + 1, 1))
            readout(NPB - 1, 1)
            pe.wait_ge(hl_ready, 1)
            pe.wait_ge(y_copied, NPB * 2)
            for s in range(2):
                tr = pe.transpose(bank_c[0:GROUPS, s * P:(s + 1) * P], h_last[:, s], ident[:])
            tr.then_inc(hl_turned, 1)

        @block.scalar
        def _(act):
            act.wait_ge(small_loaded, 16 * n_small)
            nc.scalar.activation(dt[:], dt[:], ACT.Exp).then_inc(dt_done, 1)
            act.wait_ge(arg_done, 1)
            nc.scalar.activation(mag[:], rate[:], ACT.Exp).then_inc(mag_done, 1)
            nc.scalar.activation(q_im[:], ang[:], ACT.Sin).then_inc(sin_done, 1)
            act.wait_ge(cos_arg, 1)
            nc.scalar.activation(q_re[:], tmp[0][:], ACT.Sin).then_inc(cos_done, 1)
            act.wait_ge(gate_abs, 1)
            nc.scalar.activation(sp_part[:], sp_part[:], ACT.Exp, scale=-1.0).then_inc(gate_exp, 1)
            act.wait_ge(gate_exp, 1)
            nc.scalar.activation(sp_part[:], sp_part[:], ACT.Ln, bias=G["ones_col"][0:HEADS, :]).then_inc(gate_ln, 1)

            def evacuate(n, b, it, func, dst, row, permuted):
                act.wait_ge(W.gemm_done, n + 1)
                act.wait_ge(z_stored, (n - 1) * 16)
                src = acc[b][:, :, 0:CH]
                if permuted:
                    nc.scalar.activation(
                        z_out.rearrange("p (k c j) -> p k c j", k=L, c=NC),
                        src.rearrange("p c (j k) -> p k c j", k=L), func).then_inc(evacuated[b], 1)
                else:
                    nc.scalar.activation(z_out.rearrange("p (c t) -> p c t", c=NC), src, func) \
                        .then_inc(evacuated[b], 1)
                act.wait_ge(evacuated[b], it + 1)
                act.dma_start(dst[bass.ds(row, P)], z_out[:]).then_inc(z_stored, 16)

            def copy_state(i):
                act.wait_ge(w_turned, i + 1)
                act.wait_ge(const_stored, i * (16 * (2 + L)))
                nc.scalar.copy(w_state_s.rearrange("p g m -> p (g m)"), bank_w[:]).then_inc(w_copied, 1)

            def copy_kernels(i):
                act.wait_ge(k_done, i + 1)
                nc.scalar.copy(kern.rearrange("p g k c -> p (g k c)"), bank_c[0:GC, :]).then_inc(k_copied, 1)

            act.wait_ge(lf_turned, 1)
            nc.scalar.copy(lf_rows[:, 0:TT].rearrange("p i h -> p (i h)"), bank_w[:, 0:TT * HEADS])
            nc.scalar.copy(lf_rows[0:T_SAMPLE, TT], bank_w[0:T_SAMPLE, TT * HEADS:(TT + 1) * HEADS]) \
                .then_inc(lf_copied, 1)
            act.wait_ge(negc_done, 1)
            evacuate(1, 1, 0, ACT.Copy, uT, 0, True)
            act.wait_ge(gate_stored, 64)
            copy_state(0)
            copy_kernels(0)
            evacuate(2, 0, 1, ACT.Copy, uT, P, True)

            def section(lo, hi, func, dst, row0, permuted):
                with act.Fori(lo, hi) as i:
                    copy_state(i)
                    evacuate(i * 2 + 1, 1, i, func, dst, i * (2 * P) - row0, permuted)
                    copy_kernels(i)
                    evacuate(i * 2 + 2, 0, i + 1, func, dst, i * (2 * P) + (P - row0), permuted)

            section(1, 4, ACT.Copy, uT, 0, True)
            section(4, 8, ACT.Silu, uT, 0, True)
            section(8, NPB, ACT.Copy, zT, 8 * 2 * P, False)

            def copy_v(q):
                for h, bank in enumerate((bank_c, bank_w)):
                    act.wait_ge(v_done, q + 1)
                    act.wait_ge(v_used, q)
                    nc.scalar.copy(v[:, 0, 2 * h:2 * h + 2], bank[:, 0:2 * NJ].rearrange("p (g j) -> p g j", g=2)) \
                        .then_inc(v_copied, 1)

            def gelu_y(q, b):
                for h, bank in enumerate((bank_c, bank_w)):
                    act.wait_ge(y_done, q + 1)
                    nc.scalar.activation(u_in[b][:, 2 * h:2 * h + 2],
                                         bank[:, 0:2 * NJ].rearrange("p (g j) -> p g j", g=2),
                                         ACT.Gelu_apprx_tanh).then_inc(y_copied, 1)

            def recur_tile(q, b, it, func, row, first=False):
                if not first:
                    gelu_y(q - 1, 1 - b)
                copy_v(q)
                evacuate(q + (2 * NPB + 1), 1 - b, it, func, zT, row, False)

            act.wait_ge(arena_free, 1)
            recur_tile(0, 0, NPB, ACT.Copy, 16 * P, True)
            recur_tile(1, 1, NPB + 1, ACT.Copy, 17 * P)
            for lo, hi, func in ((1, 4, ACT.Copy), (4, 8, ACT.Silu)):
                with act.Fori(lo, hi) as i:
                    recur_tile(i * 2, 0, i + NPB, func, i * (2 * P) + 16 * P)
                    recur_tile(i * 2 + 1, 1, i + (NPB + 1), func, i * (2 * P) + 17 * P)
            gelu_y(NPB - 1, 1)
            act.wait_ge(hl_turned, 1)
            nc.scalar.copy(h_rows[:], bank_c[0:GROUPS, 0:2 * P].rearrange("g (s p) -> g s p", s=2)) \
                .then_inc(hl_copied, 1)
            act.wait_ge(z_stored, 16 * tiles)

        @block.vector
        def _(dve):
            chain = Chain(dve, dve_order)
            link = chain.link
            TS, TT_, STT = nc.vector.tensor_scalar, nc.vector.tensor_tensor, nc.vector.scalar_tensor_tensor
            W.split_tile(dve, nc, 0, 0, False)
            W.split_tile(dve, nc, 1, 1, False)

            dve.wait_ge(raw_turned, 1)
            for q, dst in enumerate((lam_re, lam_im, h0[:, 0], h0[:, 1])):
                last = nc.vector.tensor_copy(dst[:] if q < 2 else dst, bank_c[:, q * GROUPS:(q + 1) * GROUPS])
            link(last)
            dve.wait_ge(dt_done, 1)
            link(TT_(ang[:], lam_im[:], dt[:], ALU.mult))
            link(TT_(rate[:], lam_re[:], dt[:], ALU.mult))
            magic = 12582912.0
            link(TS(tmp[0][:], ang[:], 1.0 / (2 * math.pi), None, ALU.mult))
            link(TS(tmp[0][:], tmp[0][:], magic, None, ALU.add))
            link(TS(tmp[0][:], tmp[0][:], magic, None, ALU.subtract))
            hi2pi = 6.28125
            link(STT(ang[:], tmp[0][:], -hi2pi, ang[:], ALU.mult, ALU.add))
            link(STT(ang[:], tmp[0][:], -(2 * math.pi - hi2pi), ang[:], ALU.mult, ALU.add))
            pi_in = 3.1415925
            TS(ang[:], ang[:], pi_in, -pi_in, ALU.min, ALU.max).then_inc(arg_done, 1)
            dve.wait_ge(arg_done, 1)
            link(TS(tmp[1][:], ang[:], math.pi / 2, -2 * math.pi, ALU.is_gt, ALU.mult))
            link(STT(tmp[0][:], ang[:], math.pi / 2, tmp[1][:], ALU.add, ALU.add))
            TS(tmp[0][:], tmp[0][:], pi_in, -pi_in, ALU.min, ALU.max).then_inc(cos_arg, 1)
            dve.wait_ge(mag_done, 1)
            dve.wait_ge(sin_done, 1)
            dve.wait_ge(cos_done, 1)
            nc.vector.memset(pw_re[:, :, 0:1], 1.0)
            nc.vector.memset(pw_im[:, :, 0:1], 0.0)
            link(TT_(pw_re[:, :, 1], mag[:], q_re[:], ALU.mult))
            link(TT_(pw_im[:, :, 1], mag[:], q_im[:], ALU.mult))

            def power(n, m):
                ar, ai, br, bi = pw_re[:, :, n], pw_im[:, :, n], pw_re[:, :, m], pw_im[:, :, m]
                link(TT_(tmp[0][:], ar, br, ALU.mult))
                link(TT_(tmp[1][:], ai, bi, ALU.mult))
                link(TT_(pw_re[:, :, n + m], tmp[0][:], tmp[1][:], ALU.subtract))
                link(TT_(tmp[0][:], ar, bi, ALU.mult))
                link(TT_(tmp[1][:], ai, br, ALU.mult))
                link(TT_(pw_im[:, :, n + m], tmp[0][:], tmp[1][:], ALU.add))

            for n, m in ((1, 1), (2, 1), (2, 2), (4, 1), (4, 2), (4, 3), (4, 4)):
                power(n, m)
            dve.wait_ge(sgn_set, 1)
            link(TT_(rho[:], mag[:], mag[:], ALU.mult))
            link(TT_(rho[:], rho[:], rho[:], ALU.mult))
            link(TT_(rho[:], rho[:], rho[:], ALU.mult))
            link(TS(q_im[:], q_im[:], sgn[:, 0:1], None, ALU.mult))
            cr, ci = q_re[:], q_im[:]
            for n in range(3):
                link(TT_(tmp[0][:], cr, cr, ALU.mult))
                link(TT_(tmp[1][:], ci, ci, ALU.mult))
                link(TT_(tmp[2][:], cr, ci, ALU.mult))
                cr, ci = turn[:, 0], turn[:, 1]
                link(TT_(cr, tmp[0][:], tmp[1][:], ALU.subtract))
                link(TS(ci, tmp[2][:], 2.0, None, ALU.mult))
            for s in range(2):
                link(TT_(tmp[0][:], pw_re[:, :, L], h0[:, s], ALU.mult))
                link(TS(tmp[1][:], pw_im[:, :, L], sgn[:, s:s + 1], None, ALU.mult))
                link(TT_(tmp[1][:], tmp[1][:], h0[:, 1 - s], ALU.mult))
                link(TT_(carry[:, s], tmp[0][:], tmp[1][:], ALU.add))
            link(TT_(tmp[0][:], lam_re[:], lam_re[:], ALU.mult))
            link(TT_(tmp[1][:], lam_im[:], lam_im[:], ALU.mult))
            link(TT_(tmp[0][:], tmp[0][:], tmp[1][:], ALU.add))
            link(nc.vector.reciprocal(tmp[2][:], tmp[0][:]))
            link(TS(mag[:], pw_re[:, :, 1], 1.0, None, ALU.subtract))
            link(TT_(tmp[0][:], mag[:], lam_re[:], ALU.mult))
            link(TT_(tmp[1][:], pw_im[:, :, 1], lam_im[:], ALU.mult))
            link(TT_(tmp[0][:], tmp[0][:], tmp[1][:], ALU.add))
            link(TT_(q_re[:], tmp[0][:], tmp[2][:], ALU.mult))
            link(TT_(tmp[0][:], pw_im[:, :, 1], lam_re[:], ALU.mult))
            link(TT_(tmp[1][:], mag[:], lam_im[:], ALU.mult))
            link(TT_(tmp[0][:], tmp[0][:], tmp[1][:], ALU.subtract))
            link(TT_(q_im[:], tmp[0][:], tmp[2][:], ALU.mult))

            dve.wait_ge(W.gemm_done, 1)
            TS(lf.rearrange("h (c t) -> h c t", c=NC), acc[0][0:HEADS, :, 0:CH], b_f[:], None, ALU.add) \
                .then_inc(evacuated[0], 1)
            dve.wait_ge(evacuated[0], 1)
            STT(sp_part, lf, -1.0, lf, ALU.mult, ALU.max).then_inc(gate_abs, 1)
            dve.wait_ge(gate_ln, 1)
            link(TS(lf[:], lf[:], 0.0, None, ALU.min))
            link(TT_(lf[:], lf[:], sp_part[:], ALU.subtract))
            dve.wait_ge(past_turned, 1)
            TS(negs[:, T_PROMPT:T_PROMPT + T_PAST], bank_w[0:HEADS, :], -1.0, None, ALU.mult).then_inc(lf_done, 1)
            W.split_tile(dve, nc, 2, 0, True)
            dve.wait_ge(lf_done, 1)
            link(TS(negs[:, 0:T_PROMPT], lf[:, 0:T_PROMPT], -1.0, None, ALU.mult))
            link(TS(negs[:, T_PROMPT + T_PAST:], lf[:, T_PROMPT:], -1.0, None, ALU.mult))
            scan = nc.vector.tensor_tensor_scan
            ones = G["ones_col"][0:HEADS, :]
            link(scan(negs[:, 0:T_PROMPT], ones.to_broadcast([HEADS, T_PROMPT]), negs[:, 0:T_PROMPT], 0.0,
                      ALU.mult, ALU.add))
            link(scan(negs[:, T_PROMPT:], ones.to_broadcast([HEADS, T_PAST + T_SAMPLE]), negs[:, T_PROMPT:], 0.0,
                      ALU.mult, ALU.add))
            TS(negs[:], negs[:], math.sqrt(HD), None, ALU.mult).then_inc(negc_done, 1)

            def inputs(i):
                dve.wait_ge(b_loaded, i * 80 + 80)
                dve.wait_ge(k_done, i)
                qr = q_re[:, bass.ds(i * PB, PB)].unsqueeze(2).to_broadcast([P, PB, GC])
                qi = q_im[:, bass.ds(i * PB, PB)].unsqueeze(2).to_broadcast([P, PB, GC])
                link(TS(b_blk[:, 1], b_blk[:, 1], sgn[:, 0:1], None, ALU.mult))
                link(TT_(bt[:, 0], b_blk[:, 0], qr, ALU.mult))
                link(TT_(tmp_b, b_blk[:, 1], qi, ALU.mult))
                link(TT_(bt[:, 0], bt[:, 0], tmp_b, ALU.add))
                link(TT_(bt[:, 1], b_blk[:, 1], qr, ALU.mult))
                link(TT_(tmp_b, b_blk[:, 0], qi, ALU.mult))
                TT_(bt[:, 1], bt[:, 1], tmp_b, ALU.subtract).then_inc(b_used, 1)
                dve.wait_ge(b_used, i + 1)
                shape = [P, PB, L, GC]
                pr = pw_back[:, 0, bass.ds(i * PB, PB), :].unsqueeze(3).to_broadcast(shape)
                pi = pw_back[:, 1, bass.ds(i * PB, PB), :].unsqueeze(3).to_broadcast(shape)
                link(TT_(xin[:], bt[:, 0].unsqueeze(2).to_broadcast(shape), pr, ALU.mult))
                link(TT_(tmp_c[:, :, 0:L], bt[:, 1].unsqueeze(2).to_broadcast(shape), pi, ALU.mult))
                TT_(xin[:], xin[:], tmp_c[:, :, 0:L], ALU.add).then_inc(xin_done, 1)

            def outputs(i):
                dve.wait_ge(c_turned, i + 1)
                dve.wait_ge(const_stored, i * (16 * (2 + L)))
                dve.wait_ge(xin_done, i + 1)
                cs = bank_c[:, 0:2 * PB * GC].rearrange("p (q g c) -> p q g c", q=2, g=PB)
                link(TS(ct[:, 0], cs[:, 0], sgn[:, 1:2], None, ALU.mult))
                link(TS(ct[:, 1], cs[:, 1], -1.0, None, ALU.mult))
                shape = [P, PB, L + 1, GC]
                pr = pw_re[:, bass.ds(i * PB, PB), :].unsqueeze(3).to_broadcast(shape)
                pi = pw_im[:, bass.ds(i * PB, PB), :].unsqueeze(3).to_broadcast(shape)
                link(TT_(ca[:], ct[:, 0].unsqueeze(2).to_broadcast(shape), pr, ALU.mult))
                link(TT_(tmp_c[:], ct[:, 1].unsqueeze(2).to_broadcast(shape), pi, ALU.mult))
                TT_(ca[:], ca[:], tmp_c[:], ALU.add).then_inc(ca_done, 1)

            def skip(i):
                link(TT_(d_diag[:], d_bc.rearrange("p (g c) -> p g c", g=PB),
                         ident[0:GC, 0:GC].unsqueeze(1).to_broadcast([GC, PB, GC]), ALU.mult))
                dve.wait_ge(k_copied, i + 1)
                TT_(kern[:, :, 0], kern[:, :, 0], d_diag[:], ALU.add).then_inc(d_added, 1)

            dve.wait_ge(gate_stored, 64)
            for part, pw in enumerate((pw_re, pw_im)):
                for k in range(L):
                    last = nc.vector.tensor_copy(pw_back[:, part, :, k], pw[:, :, L - 1 - k])
            link(last)
            inputs(0)
            outputs(0)
            W.split_tile(dve, nc, 3, 1, True)
            skip(0)
            with dve.Fori(1, NPB) as i:
                chain.enter_loop(i - 1, 13)
                W.split_tile(dve, nc, i * 2 + 2, 0, True)
                inputs(i)
                outputs(i)
                W.split_tile(dve, nc, i * 2 + 3, 1, True)
                skip(i)
                chain.leave_loop(NPB - 1)

            def rotations(q):
                part = bass.ds(q * PB, PB)
                link(nc.vector.memset(rot[:, 0, :, 0:1], 1.0))
                link(nc.vector.memset(rot[:, 1, :, 0:1], 0.0))
                link(nc.vector.tensor_copy(rot[:, :, :, 1], turn[:, :, part]))
                m = 1
                while m < NJ - 1:
                    n = min(m, NJ - 1 - m)
                    er, ei = (rot[:, s, :, m:m + 1].to_broadcast([P, PB, n]) for s in range(2))
                    br, bi = rot[:, 0, :, 1:1 + n], rot[:, 1, :, 1:1 + n]
                    link(TT_(va[:, :, 0:n], er, br, ALU.mult))
                    link(TT_(vb[:, :, 0:n], ei, bi, ALU.mult))
                    link(TT_(rot[:, 0, :, m + 1:m + 1 + n], va[:, :, 0:n], vb[:, :, 0:n], ALU.subtract))
                    link(TT_(va[:, :, 0:n], er, bi, ALU.mult))
                    link(TT_(vb[:, :, 0:n], ei, br, ALU.mult))
                    link(TT_(rot[:, 1, :, m + 1:m + 1 + n], va[:, :, 0:n], vb[:, :, 0:n], ALU.add))
                    m *= 2

            def recur(q):
                part = bass.ds(q * PB, PB)
                dve.wait_ge(v_copied, q * 2 + 2)
                dve.wait_ge(v_swapped, q * 32 + 32)
                link(TT_(v[:, :, :, NJP], v[:, :, :, NJP], carry[:, :, part], ALU.add))
                link(TT_(va[:], rot[:, 0], v[:, 0], ALU.mult))
                link(TT_(vb[:], rot[:, 1], v[:, 1], ALU.mult))
                link(TT_(va[:], va[:], vb[:], ALU.subtract))
                link(TT_(vb[:], rot[:, 0], v[:, 1], ALU.mult))
                link(TT_(v[:, 1], rot[:, 1], v[:, 0], ALU.mult))
                link(TT_(vb[:], vb[:], v[:, 1], ALU.add))
                for src, dst in ((va, v[:, 0]), (vb, v[:, 1])):
                    for g in range(PB):
                        for lo, hi in ((0, NJP), (NJP, NJ)):
                            last = nc.vector.tensor_tensor_scan(
                                dst[:, g, lo:hi], rho[:, bass.ds(q * PB + g, 1)].to_broadcast([P, hi - lo]),
                                src[:, g, lo:hi], 0.0, ALU.mult, ALU.add)
                link(last)
                link(TT_(va[:], rot[:, 0], v[:, 0], ALU.mult))
                TT_(vb[:], rot[:, 1], v[:, 1], ALU.mult).then_inc(v_used, 1)
                dve.wait_ge(v_used, q + 1)
                dve.wait_ge(y_done, q)
                link(TT_(h_prev[:, :, 1:], va[:], vb[:], ALU.add))
                link(nc.vector.tensor_copy(h_last[:, 0, part], h_prev[:, :, NJP]))
                link(nc.vector.tensor_copy(h_last[:, 1, part], h_prev[:, :, NJ]))
                nc.vector.tensor_copy(h_prev[:, :, NJP], h0[:, 0, part]).then_inc(h_ready, 1)

            levels = len([m for m in range(9) if 2 ** m < NJ - 1])
            steps = 3 + 6 * levels + 7 + 1 + 1 + 3
            n0 = 2 * NPB + 1
            W.split_tile(dve, nc, n0 + 1, 0, True)
            dve.wait_ge(arena_free, 1)
            rotations(0)
            recur(0)
            W.split_tile(dve, nc, n0 + 2, 1, True)
            rotations(1)
            recur(1)
            with dve.Fori(1, NPB // 2 - 1) as i:
                chain.enter_loop(i - 1, 2 * steps)
                for b in range(2):
                    W.split_tile(dve, nc, i * 2 + (n0 + 1 + b), b, True)
                    rotations(i * 2 + b)
                    recur(i * 2 + b)
                chain.leave_loop(NPB // 2 - 2)
            W.split_tile(dve, nc, tiles, 0, True)
            rotations(NPB - 2)
            recur(NPB - 2)
            rotations(NPB - 1)
            recur(NPB - 1)
            dve.wait_ge(h_ready, NPB)
            nc.vector.tensor_copy(va[:, 0, 0:1], h_last[:, 0, 0:1]).then_inc(hl_ready, 1)



def stage_attention(nc, d, G):
    SCALE = HD ** -0.5
    NS = T_PAST + T_SAMPLE
    SLOTS = [[(0, 0), (1, 512)]] + [[(t, 0)] for t in range(2, TT)] + [[(TT, 0)]]
    GROUPS_OF = [[[(0, 0, 0, 1), (1, 512, 0, 2)]], [[(2, 0, 0, 3)]], [[(3, 0, 0, 4)]]] + \
        [[[(t, 0, 0, 4)], [(t, 0, 4, t - 3)]] for t in range(4, TT)] + [[[(TT, 0, 0, 5)]]]
    first_group = [sum(len(g) for g in GROUPS_OF[:s]) for s in range(9)]
    per_head = first_group[8]
    assert per_head % 2 == 0
    NB = T_PAST // P
    with ExitStack() as ctx:
        sb, ps, sem = allocators(nc, ctx)
        ident, ident_bf = G["ident"], sb("ident_bf", [P, P], BF16)
        mask_f, mask_s_f = sb("mask_f", [P, P]), sb("mask_s_f", [P, T_SAMPLE])
        mask, mask_s = sb("mask", [P, P], BF16), sb("mask_s", [P, T_SAMPLE], BF16)
        q_raw, k_raw, v_raw = (sb(n, [P, T]) for n in ("q_raw", "k_raw", "v_raw"))
        kc_raw, vc_raw = (sb(n, [P, NB, HD]) for n in ("kc_raw", "vc_raw"))
        k_tok, v_tok = (sb(n, [P, TT + 1, HD]) for n in ("k_tok", "v_tok"))

        def pair(name, shape, dt=F32R):
            return [sb(f"{name}{b}", shape, dt) for b in range(2)]

        q_hi, q_lo, k_hi, k_lo = (pair(n, [P, T]) for n in ("q_hi", "q_lo", "k_hi", "k_lo"))
        v_hi, v_lo = (pair(n, [P, TT + 1, HD]) for n in ("v_hi", "v_lo"))
        kc_hi, kc_lo = (pair(n, [P, T_PAST]) for n in ("kc_hi", "kc_lo"))
        vc_hi, vc_lo = (pair(n, [P, NB, HD]) for n in ("vc_hi", "vc_lo"))
        negc = pair("negc_bc", [P, T_PROMPT + NS], F32)
        gate = pair("gate", [P, T], F32)
        prob = pair("prob", [P, 1024], F32)
        stat = pair("stat", [P, 2, 4], F32)
        pt_hi = [sb(f"pt_hi{x}", [P, n, w], F32R) for x, n, w in ((0, 4, 512), (1, 8, 512), (2, 5, T_SAMPLE))]
        pt_lo = [sb(f"pt_lo{x}", [P, n, w], F32R) for x, n, w in ((0, 4, 512), (1, 8, 512), (2, 5, T_SAMPLE))]
        mix = sb("mix", [P, T])
        score = [ps(f"score{b}", [P, 1024]) for b in range(2)]
        turned = [ps(f"turned{b}", [P, 512]) for b in range(2)]
        att, prep = ps("att", [P, 512]), ps("prep", [P, 512])

        masks_made, masks_ready, zero_pt = sem("masks_made"), sem("masks_ready"), sem("zero_pt")
        q_loaded, k_loaded, v_loaded, c_loaded = (sem(n + "_loaded") for n in ("q", "k", "v", "c"))
        gate_loaded, negc_loaded = ([sem(f"{n}_loaded{b}") for b in range(2)] for n in ("gate", "negc"))
        q_hi_done, k_hi_done, kc_hi_done, q_lo_done, k_lo_done, kc_lo_done, v_hi_done, v_lo_done, vc_hi_done, \
            vc_lo_done = (sem(n) for n in ("q_hi_done", "k_hi_done", "kc_hi_done", "q_lo_done", "k_lo_done",
                                           "kc_lo_done", "v_hi_done", "v_lo_done", "vc_hi_done", "vc_lo_done"))
        k_turned, v_turned, kc_turned, k_copied, v_copied = (
            sem(n) for n in ("k_turned", "v_turned", "kc_turned", "k_copied", "v_copied"))
        k_stored, v_stored, mix_stored = (G["sem"][n] for n in ("k_stored", "v_stored", "mix_stored"))
        scored = [sem(f"scored{b}") for b in range(2)]
        biased = [sem(f"biased{b}") for b in range(2)]
        negmax, exped, summed, normed = (
            [sem(f"{n}{b}") for b in range(2)] for n in ("negmax", "exped", "summed", "normed"))
        p_turned = [sem(f"p_turned{b}") for b in range(2)]
        prob_free = [sem(f"prob_free{b}") for b in range(2)]
        hi_done, lo_done = ([sem(f"pt_{n}_done{b}") for b in range(2)] for n in ("hi", "lo"))
        weighed = [sem(f"weighed{x}") for x in range(3)]
        gated = sem("gated")
        block = ctx.enter_context(nc.Block())
        zT = d["zT"]
        k_cache, v_cache = (d[n][0, 0].rearrange("(i p) h c -> p i h c", p=P) for n in ("cache_k", "cache_v"))

        def taken(group, dst, bank):
            at = 0
            for t, col, j0, nj in group:
                if t < TT:
                    c = t % 4 * P
                    yield dst[:, j0:j0 + nj, c:c + P], \
                        bank[:, at:at + nj * P].rearrange("p (j t) -> p j t", j=nj)
                    at += nj * P
                else:
                    yield dst[:, 0:NB], bank[:, 0:NB * T_SAMPLE].rearrange("p (j t) -> p j t", j=NB)
                    yield dst[0:T_SAMPLE, NB], bank[0:T_SAMPLE, NB * T_SAMPLE:(NB + 1) * T_SAMPLE]

        def heads(eng, head):
            head(0, 0, 0, first=True)
            head(1, 1, 0)
            with eng.Fori(1, HEADS // 2 - 1) as i:
                head(i * 2, 0, i)
                head(i * 2 + 1, 1, i)
            head(HEADS - 2, 0, HEADS // 2 - 1)
            head(HEADS - 1, 1, HEADS // 2 - 1, last=True)

        @block.sync
        def _(sp):
            def load(h, b, it, first=False):
                if not first:
                    sp.wait_ge(k_hi_done, h)
                    sp.wait_ge(k_lo_done, h)
                    settle(sp, G["passed"])
                    sp.wait_ge(k_turned, h * 3)
                sp.dma_start(k_raw[:], zT[bass.ds(h * P + D_ATT, P)]).then_inc(k_loaded, 16)
                if not first:
                    sp.wait_ge(q_hi_done, h)
                    sp.wait_ge(q_lo_done, h)
                sp.dma_start(q_raw[:], zT[bass.ds(h * P, P)]).then_inc(q_loaded, 16)
                if not first:
                    sp.wait_ge(biased[0], (h - 1) * 4)
                    sp.wait_ge(biased[1], (h - 1) * 4)
                sp.dma_start(negc[b][:], d["negc"][bass.ds(h, 1)].to_broadcast([P, T_PROMPT + NS])) \
                    .then_inc(negc_loaded[b], 16)
                if not first:
                    sp.wait_ge(v_turned, h * 3)
                sp.dma_start(v_raw[:], zT[bass.ds(h * P + 2 * D_ATT, P)]).then_inc(v_loaded, 16)
                if not first:
                    sp.wait_ge(kc_turned, h)
                    sp.wait_ge(vc_hi_done, h)
                    sp.wait_ge(vc_lo_done, h)
                    settle(sp, G["passed"])
                sp.dma_start(kc_raw[:], k_cache[:, :, bass.ds(h, 1)].rearrange("p i h c -> p i (h c)")) \
                    .then_inc(c_loaded, 16)
                sp.dma_start(vc_raw[:], v_cache[:, :, bass.ds(h, 1)].rearrange("p i h c -> p i (h c)")) \
                    .then_inc(c_loaded, 16)
                if not first:
                    sp.wait_ge(gated, (h - 1) * 3)
                sp.dma_start(gate[b][:], zT[bass.ds(h * P + 3 * D_ATT, P)]).then_inc(gate_loaded[b], 16)

            load(0, 0, 0, first=True)

            def head(h, b, i, first=False, last=False):
                if not last:
                    load(h + 1, 1 - b, i)
            heads(sp, head)

        @block.gpsimd
        def _(pool):
            nc.gpsimd.memset(mask_f[:], 0.0)
            nc.gpsimd.memset(mask_s_f[:], 0.0).then_inc(masks_made, 1)
            pool.wait_ge(masks_made, 1)
            nc.gpsimd.affine_select(out=mask_f[:], in_=mask_f[:], compare_op=ALU.is_ge, fill=NEG, base=0,
                                    pattern=[[-1, P]], channel_multiplier=1).then_inc(masks_made, 1)
            pool.wait_ge(masks_made, 2)
            r0 = P - T_SAMPLE
            nc.gpsimd.affine_select(out=mask_s_f[r0:], in_=mask_s_f[r0:], compare_op=ALU.is_ge, fill=NEG,
                                    base=0, pattern=[[-1, T_SAMPLE]], channel_multiplier=1) \
                .then_inc(masks_made, 1)
            pool.wait_ge(masks_made, 3)
            nc.gpsimd.memset(v_tok[:, TT], 0.0)
            nc.gpsimd.tensor_copy(mask[:], mask_f[:])
            nc.gpsimd.tensor_copy(mask_s[:], mask_s_f[:])
            nc.gpsimd.tensor_copy(ident_bf[:], ident[:]).then_inc(masks_ready, 1)

            def sub(out, a, hi, done):
                nc.gpsimd.tensor_tensor(out, a, hi.bitcast(F32), ALU.subtract).then_inc(done, 1)

            def store_mix(h):
                pool.wait_ge(gated, h * 3 + 3)
                pool.dma_start(d["mixT"][bass.ds(h * P, P)], mix[:]).then_inc(mix_stored, 16)

            def prepare(h, b, mix_of=None):
                pool.wait_ge(k_hi_done, h + 1)
                sub(k_lo[b][:], k_raw[:], k_hi[b][:], k_lo_done)
                pool.wait_ge(q_hi_done, h + 1)
                sub(q_lo[b][:], q_raw[:], q_hi[b][:], q_lo_done)
                pool.wait_ge(c_loaded, h * 32 + 32)
                settle(pool, G["passed"])
                nc.gpsimd.tensor_copy(vc_hi[b][:], vc_raw[:]).then_inc(vc_hi_done, 1)
                pool.wait_ge(vc_hi_done, h + 1)
                sub(vc_lo[b][:], vc_raw[:], vc_hi[b][:], vc_lo_done)
                pool.wait_ge(k_copied, h * 3 + 3)
                for tok, src, stored in (("k", k_tok, k_stored), ("v", v_tok, v_stored)):
                    if tok == "v":
                        if mix_of is not None:
                            store_mix(mix_of)
                        pool.wait_ge(v_copied, h * 3 + 3)
                        settle(pool, G["passed"])
                        nc.gpsimd.tensor_copy(v_hi[b][:], v_tok[:]).then_inc(v_hi_done, 1)
                        pool.wait_ge(v_hi_done, h + 1)
                        sub(v_lo[b][:], v_tok[:], v_hi[b][:], v_lo_done)
                    pool.dma_start(d[tok + "_prompt"][0, 0].rearrange("(i p) h c -> p i h c", p=P)
                                   [:, :, bass.ds(h, 1)].rearrange("p i h c -> p i (h c)"), src[:, 0:TT]) \
                        .then_inc(stored, 16)
                    pool.dma_start(d[tok + "_sample"][0, 0][:, bass.ds(h, 1)].rearrange("t h c -> t (h c)"),
                                   src[0:T_SAMPLE, TT]).then_inc(stored, 16)

            prepare(0, 0)

            def head(h, b, i, first=False, last=False):
                if not first:
                    pool.wait_ge(weighed[2], h)
                if not last:
                    prepare(h + 1, 1 - b, None if first else h - 1)
                elif not first:
                    store_mix(h - 1)
            heads(pool, head)
            store_mix(HEADS - 1)
            pool.wait_ge(mix_stored, 16 * HEADS)
            pool.wait_ge(k_stored, 32 * HEADS)
            pool.wait_ge(v_stored, 32 * HEADS)

        @block.tensor
        def _(pe):
            def three(out, pairs, start, stop, lhs, rhs):
                for n, (x, y) in enumerate(((0, 0), (0, 1), (1, 0))):
                    mm = pe.matmul(out, lhs[x], rhs[y], start=(start and n == 0), stop=(stop and n == 2))
                return mm

            def turn(h, m):
                if m < 6:
                    src, loaded, done = (k_raw, k_loaded, k_turned) if m < 3 else (v_raw, v_loaded, v_turned)
                    if m == 0:
                        pe.wait_ge(kc_lo_done, h)
                    elif m <= 3:
                        pe.wait_ge(k_copied, h * 3 + m)
                    else:
                        pe.wait_ge(v_copied, h * 3 + (m - 3))
                    pe.wait_ge(loaded, h * 16 + 16)
                    for q in range(4 if m % 3 < 2 else 1):
                        t = m % 3 * 4 + q
                        rows = P if t < TT else T_SAMPLE
                        tr = pe.transpose(prep[0:rows, q * P:(q + 1) * P], src[:, t * P:t * P + rows], ident[:])
                    tr.then_inc(done, 1)
                else:
                    pe.wait_ge(v_copied, h * 3 + 3)
                    pe.wait_ge(c_loaded, h * 32 + 32)
                    for q in range(NB):
                        tr = pe.transpose(prep[:, q * P:(q + 1) * P], kc_raw[:, q], ident[:])
                    tr.then_inc(kc_turned, 1)

            def scores(h, b, it, s, hb):
                pe.wait_ge(biased[b], it)
                if s == 0:
                    pe.wait_ge(q_lo_done, h + 1)
                    pe.wait_ge(k_lo_done, h + 1)
                if s == 7:
                    pe.wait_ge(kc_lo_done, h + 1)
                    q = [x[hb][:, T - P:T] for x in (q_hi, q_lo)]
                    three(score[b][:, 0:T_PAST], 0, True, True, q, [x[hb][:] for x in (kc_hi, kc_lo)])
                    out = score[b][:, T_PAST:NS]
                    three(out, 0, True, False, q, [x[hb][:, T_PROMPT:T] for x in (k_hi, k_lo)])
                    mm = pe.matmul(out, ident_bf[:], mask_s[:], start=False, stop=True)
                else:
                    for t, col in SLOTS[s]:
                        q = [x[hb][:, t * P:(t + 1) * P] for x in (q_hi, q_lo)]
                        for lo in range(0, (t + 1) * P, 512):
                            hi = min(lo + 512, (t + 1) * P)
                            final = hi == (t + 1) * P
                            three(score[b][:, col + lo:col + hi], 0, True, not final, q,
                                  [x[hb][:, lo:hi] for x in (k_hi, k_lo)])
                        mm = pe.matmul(score[b][:, col + t * P:col + (t + 1) * P], ident_bf[:], mask[:],
                                       start=False, stop=True)
                mm.then_inc(scored[b], 1)

            def turn_probs(h, s):
                b = s % 2
                pe.wait_ge(normed[b], h * 4 + (s // 2 + 1))
                for n, group in enumerate(GROUPS_OF[s]):
                    gi = first_group[s] + n
                    bank = turned[gi % 2]
                    pe.wait_ge(lo_done[gi % 2], h * (per_head // 2) + gi // 2)
                    if group[0][0] == TT:
                        settle(pe, G["passed"])
                    at = 0
                    for t, col, j0, nj in group:
                        for j in range(j0, j0 + nj):
                            if t < TT:
                                tr = pe.transpose(bank[:, at:at + P], prob[b][:, col + j * P:col + (j + 1) * P],
                                                  ident[:])
                                at += P
                            else:
                                rows, r0 = (P if j < NB else T_SAMPLE), P - T_SAMPLE
                                tr = pe.transpose(bank[0:rows, at:at + T_SAMPLE],
                                                  prob[b][r0:P, j * P:j * P + rows], ident[r0:P, r0:P])
                                at += T_SAMPLE
                    tr.then_inc(p_turned[gi % 2], 1)
                pe.nop().then_inc(prob_free[b], 1)

            def weigh(h, x, hb):
                gi = first_group[(3, 7, 8)[x]] - 1
                for q in (gi - 1, gi):
                    pe.wait_ge(lo_done[q % 2], h * (per_head // 2) + (q // 2 + 1))
                pe.wait_ge(gated, h * 3 + x)
                if x == 0:
                    pe.wait_ge(v_lo_done, h + 1)
                if x < 2:
                    for j in range(4 * x + 4):
                        lo = max(0, j - 4 * x) * P
                        mm = three(att[:, lo:512], 0, j == 0, j == 4 * x + 3,
                                   [v[hb][:, j] for v in (v_hi, v_lo)], [p[x][:, j, lo:512] for p in (pt_hi, pt_lo)])
                else:
                    for j in range(NB):
                        three(att[:, 0:T_SAMPLE], 0, j == 0, False, [v[hb][:, j] for v in (vc_hi, vc_lo)],
                              [p[x][:, j] for p in (pt_hi, pt_lo)])
                    mm = three(att[:, 0:T_SAMPLE], 0, False, True,
                               [v[hb][0:T_SAMPLE, TT] for v in (v_hi, v_lo)],
                               [p[x][0:T_SAMPLE, NB] for p in (pt_hi, pt_lo)])
                mm.then_inc(weighed[x], 1)

            pe.wait_ge(masks_ready, 1)
            for m in range(7):
                turn(0, m)
            scores(0, 0, 0, 0, 0)
            scores(0, 1, 0, 1, 0)

            def head(h, hb, i, first=False, last=False):
                for s in range(8):
                    turn_probs(h, s)
                    if s < 6:
                        scores(h, s % 2, h * 4 + (s // 2 + 1), s + 2, hb)
                    elif not last:
                        scores(h + 1, s % 2, h * 4 + (s // 2 + 1), s - 6, 1 - hb)
                    if s == 0 and not first:
                        weigh(h - 1, 1, 1 - hb)
                    if s == 1 and not first:
                        weigh(h - 1, 2, 1 - hb)
                    if s == 4:
                        weigh(h, 0, hb)
                    if s < 7 and not last:
                        turn(h + 1, s)
            heads(pe, head)
            weigh(HEADS - 1, 1, 1)
            weigh(HEADS - 1, 2, 1)

        @block.scalar
        def _(act):
            def split_qk(h, b, which, first=False):
                hi, raw, loaded, done = ((k_hi, k_raw, k_loaded, k_hi_done),
                                         (q_hi, q_raw, q_loaded, q_hi_done))[which]
                act.wait_ge(loaded, h * 16 + 16)
                if not first:
                    act.wait_ge(scored[0], (h - 1) * 4)
                    act.wait_ge(scored[1], (h - 1) * 4)
                nc.scalar.copy(hi[b][:], raw[:]).then_inc(done, 1)

            def copy_k(h, m):
                act.wait_ge(k_turned, h * 3 + (m + 1))
                act.wait_ge(k_stored, h * 32)
                if m < 2:
                    nc.scalar.copy(k_tok[:, 4 * m:4 * m + 4].rearrange("p i c -> p (i c)"), prep[:]) \
                        .then_inc(k_copied, 1)
                else:
                    nc.scalar.copy(k_tok[0:T_SAMPLE, TT], prep[0:T_SAMPLE, 0:P]).then_inc(k_copied, 1)

            def split_kc(h, b):
                act.wait_ge(kc_turned, h + 1)
                nc.scalar.copy(kc_hi[b][:], prep[:]).then_inc(kc_hi_done, 1)

            def exponentials(h, s):
                b, it = s % 2, h * 4 + s // 2
                act.wait_ge(negmax[b], it + 1)
                for n, (t, col) in enumerate(SLOTS[s]):
                    width = (t + 1) * P if t < TT else NS
                    e = nc.scalar.activation(prob[b][:, col:col + width], prob[b][:, col:col + width], ACT.Exp,
                                             scale=SCALE, bias=stat[b][:, n, 1:2], accum_out=stat[b][:, n, 2:3])
                e.then_inc(exped[b], 1)

            def high_parts(h, s):
                for n, group in enumerate(GROUPS_OF[s]):
                    gi = first_group[s] + n
                    bank, x = turned[gi % 2], (0 if s < 3 else 1 if s < 7 else 2)
                    act.wait_ge(p_turned[gi % 2], h * (per_head // 2) + (gi // 2 + 1))
                    act.wait_ge(weighed[x], h)
                    for out, src in taken(group, pt_hi[x], bank):
                        c = nc.scalar.copy(out, src)
                    c.then_inc(hi_done[gi % 2], 1)

            split_qk(0, 0, 0, True)
            split_qk(0, 0, 1, True)
            for m in range(3):
                copy_k(0, m)
            split_kc(0, 0)
            exponentials(0, 0)

            def head(h, hb, i, first=False, last=False):
                for s in range(8):
                    if s < 7:
                        exponentials(h, s + 1)
                    elif not last:
                        exponentials(h + 1, 0)
                    high_parts(h, s)
                    if last:
                        continue
                    if s < 2:
                        split_qk(h + 1, 1 - hb, s)
                    if s < 3:
                        copy_k(h + 1, s)
                    if s == 6:
                        split_kc(h + 1, 1 - hb)
            heads(act, head)

        @block.vector
        def _(dve):
            def copy_v(h, m):
                dve.wait_ge(v_turned, h * 3 + (m + 1))
                dve.wait_ge(v_stored, h * 32)
                dve.wait_ge(v_lo_done, h)
                if m < 2:
                    nc.vector.tensor_copy(v_tok[:, 4 * m:4 * m + 4].rearrange("p i c -> p (i c)"), prep[:]) \
                        .then_inc(v_copied, 1)
                else:
                    nc.vector.tensor_copy(v_tok[0:T_SAMPLE, TT], prep[0:T_SAMPLE, 0:P]).then_inc(v_copied, 1)

            def low_kc(h, b):
                dve.wait_ge(kc_hi_done, h + 1)
                nc.vector.tensor_tensor(kc_lo[b][:], prep[:], kc_hi[b][:].bitcast(F32), ALU.subtract) \
                    .then_inc(kc_lo_done, 1)

            def bias(h, s, hb, pair):
                b, it = s % 2, h * 4 + s // 2
                dve.wait_ge(scored[b], it + 1)
                dve.wait_ge(prob_free[b], it)
                if s == 0:
                    dve.wait_ge(negc_loaded[hb], pair * 16 + 16)
                settle(dve, G["passed"])
                for n, (t, col) in enumerate(SLOTS[s]):
                    width, row = ((t + 1) * P, 0) if t < TT else (NS, T_PROMPT)
                    z = nc.vector.tensor_tensor_reduce(
                        out=prob[b][:, col:col + width], in0=score[b][:, col:col + width],
                        in1=negc[hb][:, row:row + width], scale=1.0, scalar=-3.0e38, op0=ALU.add, op1=ALU.max,
                        accum_out=stat[b][:, n, 0:1])
                z.then_inc(biased[b], 1)
                dve.wait_ge(biased[b], it + 1)
                nt = len(SLOTS[s])
                nc.vector.tensor_scalar(stat[b][:, 0:nt, 1], stat[b][:, 0:nt, 0], -SCALE, None, ALU.mult) \
                    .then_inc(negmax[b], 1)

            def normalize(h, s):
                b, it = s % 2, h * 4 + s // 2
                dve.wait_ge(exped[b], it + 1)
                nt = len(SLOTS[s])
                nc.vector.reciprocal(stat[b][:, 0:nt, 3], stat[b][:, 0:nt, 2]).then_inc(summed[b], 1)
                dve.wait_ge(summed[b], it + 1)
                for n, (t, col) in enumerate(SLOTS[s]):
                    width = (t + 1) * P if t < TT else NS
                    p = nc.vector.tensor_scalar(prob[b][:, col:col + width], prob[b][:, col:col + width],
                                                stat[b][:, n, 3:4], None, ALU.mult)
                p.then_inc(normed[b], 1)

            def low_parts(h, s):
                for n, group in enumerate(GROUPS_OF[s]):
                    gi = first_group[s] + n
                    bank, x = turned[gi % 2], (0 if s < 3 else 1 if s < 7 else 2)
                    dve.wait_ge(hi_done[gi % 2], h * (per_head // 2) + (gi // 2 + 1))
                    for (out, src), (hi, _) in zip(taken(group, pt_lo[x], bank), taken(group, pt_hi[x], bank)):
                        c = nc.vector.tensor_tensor(out, src, hi.bitcast(F32), ALU.subtract)
                    c.then_inc(lo_done[gi % 2], 1)

            def gate_out(h, x, hb, pair=None):
                cols = slice(512 * x, 512 * x + (512 if x < 2 else T_SAMPLE))
                dve.wait_ge(weighed[x], h + 1)
                if x == 0:
                    dve.wait_ge(mix_stored, h * 16)
                    dve.wait_ge(gate_loaded[hb], pair * 16 + 16)
                nc.vector.tensor_tensor(mix[:, cols], att[:, 0:cols.stop - cols.start], gate[hb][:, cols],
                                        ALU.mult).then_inc(gated, 1)

            dve.wait_ge(masks_ready, 1)
            for m in range(3):
                copy_v(0, m)
            low_kc(0, 0)
            bias(0, 0, 0, 0)

            def head(h, hb, i, first=False, last=False):
                for s in range(8):
                    if s < 7:
                        bias(h, s + 1, hb, i)
                    elif not last:
                        bias(h + 1, 0, 1 - hb, i + hb)
                    normalize(h, s)
                    if s > 0:
                        low_parts(h, s - 1)
                    elif not first:
                        low_parts(h - 1, 7)
                    if s == 1 and not first:
                        gate_out(h - 1, 1, 1 - hb)
                    if s == 2 and not first:
                        gate_out(h - 1, 2, 1 - hb)
                    if not last and 3 <= s < 6:
                        copy_v(h + 1, s - 3)
                    if not last and s == 6:
                        low_kc(h + 1, 1 - hb)
                    if s == 6:
                        gate_out(h, 0, hb, i)
            heads(dve, head)
            low_parts(HEADS - 1, 7)
            gate_out(HEADS - 1, 1, 1)
            gate_out(HEADS - 1, 2, 1)



def stage_side(nc, d, G):
    with ExitStack() as ctx:
        sb, ps, sem = allocators(nc, ctx)
        ident = G["ident"]
        WE = Weights(sb, sem, "w_pe_s", KP)
        WG = Weights(sb, sem, "w_glu_s", KS)
        p_in = [sb(f"p_in{b}", [P, D_PLE]) for b in range(2)]
        p_hi, p_lo = (sb(n, [P, KP, T], F32R) for n in ("p_hi", "p_lo"))
        e_out = [sb(f"e_out{b}", [P, T]) for b in range(2)]
        e_sq = sb("e_sq", [P, T])
        e_sum = sb("e_sum", [P, T])
        ones = sb("ones_sq", [P, P])
        y_raw = sb("y_raw", [P, KS, T])
        y_hi, y_lo = (sb(n, [P, KS, T], F32R) for n in ("y_hi", "y_lo"))
        sig = [sb(f"sig{b}", [P, T]) for b in range(2)]
        gs = [sb(f"gs{b}", [P, T]) for b in range(2)]
        out = [sb(f"mix_out{b}", [P, T]) for b in range(2)]
        acc = [ps(f"side_acc{b}", [P, NC, 512]) for b in range(2)]
        p_ps = [ps(f"p_ps{b}", [P, 512]) for b in range(2)]
        p_loaded = [sem(f"p_loaded{b}") for b in range(2)]
        gs_loaded, y_loaded = [G["sem"][f"gs_loaded{b}"] for b in range(2)], G["sem"]["y_loaded"]
        y_hi_done, y_split = sem("y_hi_done"), sem("y_split")
        p_turned, p_hi_done, p_lo_done, ones_set = (
            sem(n) for n in ("p_turned", "p_hi_done", "p_lo_done", "ones_set"))
        evacuated = [sem(f"side_evacuated{b}") for b in range(2)]
        e_stored = [sem(f"e_stored{b}") for b in range(2)]
        norm_ready, norm_std, dve_order = (sem(n) for n in ("e_norm_ready", "e_norm_std", "side_order"))
        summed = [sem(f"e_summed{b}") for b in range(2)]
        sig_done, gated_done, mix_stored = ([sem(f"{n}{b}") for b in range(2)]
                                            for n in ("sig_done", "gated_done", "glu_stored"))
        block = ctx.enter_context(nc.Block())
        w_pe = d["w_pe"][0].rearrange("(k p) n -> p k n", p=P)
        w_glu = d["w_glu"][0].rearrange("(k p) n -> p k n", p=P)
        p_tiles = d["p_prompt"][0].rearrange("a (i p) c -> (a i) p c", p=P)
        yT = d["yT"].rearrange("r k j -> r (k j)")
        uT = d["uT"].rearrange("r k j -> r (k j)")

        @block.sync
        def _(sp):
            WE.load(sp, w_pe, 0, 0)
            for n in range(TT + 1):
                b = n % 2
                sp.wait_ge(p_turned, max(n - 1, 0))
                if n < TT:
                    sp.dma_start(p_in[b][:], p_tiles[n]).then_inc(p_loaded[b], 16)
                else:
                    sp.dma_start(p_in[b][0:T_SAMPLE], d["p_sample"][0, 0]).then_inc(p_loaded[b], 16)
            with sp.Fori(1, KD) as m:
                WE.load(sp, w_pe, m * P, m)
            with sp.Fori(0, KS) as m:
                WG.load(sp, w_glu, m * P, m)

        @block.gpsimd
        def _(pool):
            nc.gpsimd.memset(ones[:], 1.0).then_inc(ones_set, 1)
            pool.dma_start(y_raw[:], yT.rearrange("(k p) t -> p k t", p=P)).then_inc(y_loaded, 16)
            with pool.Fori(0, KS // 2) as i:
                for b in range(2):
                    pool.wait_ge(gated_done[b], i)
                    pool.dma_start(gs[b][:], uT[bass.ds(i * (2 * P) + (D_SSM + b * P), P)]) \
                        .then_inc(gs_loaded[b], 16)

        @block.tensor
        def _(pe):
            for n in range(TT + 1):
                b, rows = n % 2, (P if n < TT else T_SAMPLE)
                pe.wait_ge(p_loaded[b], 16 * (n // 2 + 1))
                if n >= 2:
                    pe.wait_ge(p_lo_done, n - 1)
                for k in range(KP):
                    tr = pe.transpose(p_ps[b][:, k * P:k * P + rows], p_in[b][0:rows, k * P:(k + 1) * P],
                                      ident[0:rows, 0:rows])
                tr.then_inc(p_turned, 1)
            pe.wait_ge(p_lo_done, TT + 1)
            with pe.Fori(0, KD // 2) as i:
                for b in range(2):
                    pe.wait_ge(WE.split[1], i * 2 + (b + 1))
                    pe.wait_ge(evacuated[b], i)
                    gemm_tile(pe, acc[b], WE.hi[b], WE.lo[b], p_hi, p_lo, KP).then_inc(WE.gemm_done, 1)
            with pe.Fori(0, KS // 2) as i:
                for b in range(2):
                    pe.wait_ge(WG.split[1], i * 2 + (b + 1))
                    pe.wait_ge(evacuated[b], i + KD // 2)
                    gemm_tile(pe, acc[b], WG.hi[b], WG.lo[b], y_hi, y_lo, KS, act_ready=y_split) \
                        .then_inc(WG.gemm_done, 1)
            pe.wait_ge(ones_set, 1)
            for b in range(2):
                pe.wait_ge(summed[b], KD // 2)
            pe.wait_ge(evacuated[0], (KD + KS) // 2)
            for c in range(NC):
                mm = pe.matmul(acc[0][:, c, 0:CH], ones[:], e_sum[:, c * CH:(c + 1) * CH], start=True, stop=True)
            mm.then_inc(norm_ready, 1)

        @block.scalar
        def _(act):
            for n in range(TT + 1):
                b, rows = n % 2, (P if n < TT else T_SAMPLE)
                act.wait_ge(p_turned, n + 1)
                nc.scalar.copy(p_hi[:, :, n * P:n * P + rows],
                               p_ps[b][:, 0:2 * P].rearrange("p (k t) -> p k t", k=KP)[:, :, 0:rows]) \
                    .then_inc(p_hi_done, 1)
            with act.Fori(0, KD // 2) as i:
                for b in range(2):
                    act.wait_ge(WE.gemm_done, i * 2 + (b + 1))
                    act.wait_ge(e_stored[b], i * 16)
                    act.wait_ge(summed[b], i)
                    nc.scalar.copy(e_out[b].rearrange("p (c t) -> p c t", c=NC), acc[b][:, :, 0:CH]) \
                        .then_inc(evacuated[b], 1)
                    act.wait_ge(evacuated[b], i + 1)
                    act.dma_start(d["eT"][bass.ds(i * (2 * P) + b * P, P)], e_out[b][:]).then_inc(e_stored[b], 16)
            act.wait_ge(y_loaded, 16)
            for k in range(KS):
                nc.scalar.copy(y_hi[:, k], y_raw[:, k]).then_inc(y_hi_done, 1)
            with act.Fori(0, KS // 2) as i:
                for b in range(2):
                    act.wait_ge(WG.gemm_done, i * 2 + (b + 1))
                    act.wait_ge(gated_done[b], i)
                    nc.scalar.activation(sig[b].rearrange("p (c t) -> p c t", c=NC), acc[b][:, :, 0:CH],
                                         ACT.Sigmoid).then_inc(evacuated[b], 1)
                    act.wait_ge(gated_done[b], i + 1)
                    act.dma_start(d["mixT"][bass.ds(i * (2 * P) + (D_ATT + b * P), P)], out[b][:]) \
                        .then_inc(mix_stored[b], 16)
            act.wait_ge(norm_ready, 1)
            nc.scalar.activation(e_sum.rearrange("p (c t) -> p c t", c=NC), acc[0][:, :, 0:CH], ACT.Sqrt,
                                 scale=1.0 / D_MODEL, bias=G["eps"][:]).then_inc(norm_std, 1)
            for b in range(2):
                act.wait_ge(e_stored[b], 16 * KD // 2)
                act.wait_ge(mix_stored[b], 16 * KS // 2)

        @block.vector
        def _(dve):
            chain = Chain(dve, dve_order)
            for n in range(TT + 1):
                b, rows = n % 2, (P if n < TT else T_SAMPLE)
                dve.wait_ge(p_hi_done, n + 1)
                nc.vector.tensor_tensor(p_lo[:, :, n * P:n * P + rows],
                                        p_ps[b][:, 0:2 * P].rearrange("p (k t) -> p k t", k=KP)[:, :, 0:rows],
                                        p_hi[:, :, n * P:n * P + rows].bitcast(F32), ALU.subtract) \
                    .then_inc(p_lo_done, 1)
            chain.link(nc.vector.memset(e_sum[:], 0.0))
            WE.split_tile(dve, nc, 0, 0, False)
            WE.split_tile(dve, nc, 1, 1, False)

            def square(b, it):
                dve.wait_ge(evacuated[b], it + 1)
                chain.link(nc.vector.tensor_tensor(e_sq[:], e_out[b][:], e_out[b][:], ALU.mult))
                nc.vector.tensor_tensor(e_sum[:], e_sum[:], e_sq[:], ALU.add).then_inc(summed[b], 1)
                dve.wait_ge(summed[b], it + 1)

            with dve.Fori(0, KD // 2 - 1) as i:
                chain.enter_loop(i, 2)
                for b in range(2):
                    WE.split_tile(dve, nc, i * 2 + (b + 2), b, True)
                    square(b, i)
                chain.leave_loop(KD // 2 - 1)
            for k in range(KS):
                dve.wait_ge(y_hi_done, k + 1)
                nc.vector.tensor_tensor(y_lo[:, k], y_raw[:, k], y_hi[:, k].bitcast(F32), ALU.subtract) \
                    .then_inc(y_split, 1)
                if k == 0:
                    for b in range(2):
                        square(b, KD // 2 - 1)
                    WG.split_tile(dve, nc, 0, 0, False)
                    WG.split_tile(dve, nc, 1, 1, False)

            def gate_y(m, b, i):
                dve.wait_ge(evacuated[b], i + (KD // 2 + 1))
                dve.wait_ge(gs_loaded[b], i * 16 + 16)
                dve.wait_ge(mix_stored[b], i * 16)
                chain.link(nc.vector.tensor_tensor(sig[b][:], sig[b][:], y_raw[:, bass.ds(m, 1)]
                                                   .rearrange("p a t -> p (a t)"), ALU.mult))
                nc.vector.tensor_tensor(out[b].rearrange("p (j k) -> p k j", k=L),
                                        sig[b].rearrange("p (k j) -> p k j", k=L),
                                        gs[b].rearrange("p (k j) -> p k j", k=L), ALU.mult) \
                    .then_inc(gated_done[b], 1)

            with dve.Fori(0, KS // 2 - 1) as i:
                chain.enter_loop(i, 2)
                for b in range(2):
                    WG.split_tile(dve, nc, i * 2 + (b + 2), b, True)
                    gate_y(i * 2 + b, b, i)
                chain.leave_loop(KS // 2 - 1)
            for b in range(2):
                gate_y(KS - 2 + b, b, KS // 2 - 1)
            dve.wait_ge(norm_std, 1)
            chain.link(nc.vector.reciprocal(G["e_rstd"][:], e_sum[:]))



def stage_output(nc, d, G):
    WIDTH, BASE = (512, T - 512), (0, 512)
    ROWS = ([P] * 4, [P] * 4 + [T_SAMPLE])
    CHUNKS = ([(0, 512)], [(0, 272), (272, 272)])
    WM = max(WIDTH)
    YT = len(ROWS[1])
    RING = 4
    with ExitStack() as ctx:
        sb, ps, sem = allocators(nc, ctx)
        ident = G["ident"]
        W = Weights(sb, sem, "w_post", KD)
        hi, lo, y_tok, g_bc, mix_raw = [], [], [], [], []
        for r in range(2):
            start = (nc.sbuf_base + 31) // 32 * 32
            hi.append(sb(f"region{r}_hi", [P, KD, WM], F32R))
            lo.append(sb(f"region{r}_lo", [P, KD, WM], F32R))
            y_bytes = 4 * YT * D_MODEL
            y_tok.append(nc.alloc_sbuf_tensor_at(f"region{r}_y", [P, YT, D_MODEL], F32, offset=start))
            g_bc.append(nc.alloc_sbuf_tensor_at(f"region{r}_g", [P, D_MODEL], F32, offset=start + y_bytes))
            mix_raw.append(nc.alloc_sbuf_tensor_at(f"region{r}_raw", [P, RING, 2, WM], F32,
                                                   offset=start + y_bytes + 4 * D_MODEL))
            assert y_bytes + 4 * D_MODEL + 4 * RING * 2 * WM <= 2 * 4 * KD * WM
        side, total, sig, h2 = ([sb(f"{n}{b}", [P, WM]) for b in range(2)]
                                for n in ("side", "total", "gate_sig", "h2_"))
        junk = sb("junk", [P, YT, P])
        g_pe = sb("g_pe_s", [P, KD])
        ssq = sb("ssq_y", [P, YT, KD])
        var, std, rstd = (sb(n, [P, YT]) for n in ("var_y", "std_y", "rstd_y"))
        acc = [ps(f"post_acc{b}", [P, 2, 512]) for b in range(2)]
        tr_ps = [ps(f"y_ps{b}", [P, 2 * 512]) for b in range(2)]

        side_loaded, evacuated = ([sem(f"{n}{b}") for b in range(2)] for n in ("side_loaded", "post_evacuated"))
        mix_loaded = [sem(f"mix_loaded{s}") for s in range(RING)]
        mix_hi_done, mix_split, h_hi_done, h_split, total_done, h2_done = (
            sem(n) for n in ("mix_hi_done", "mix_split", "h_hi_done", "h_split", "total_done", "h2_done"))
        e_scaled, e_gated, ssq_zero = sem("e_scaled"), sem("e_gated"), sem("ssq_zero")
        turned, squared, y_filled, gains_loaded, g_loaded = (
            sem(n) for n in ("h2_turned", "h2_squared", "y_filled", "gains_loaded", "g_final_loaded"))
        var_summed, var_done, std_done, rstd_done, dve_scaled, act_scaled = (
            sem(n) for n in ("y_var_summed", "y_var_done", "y_std_done", "y_rstd_done", "dve_scaled", "act_scaled"))
        y_stored = [sem(f"y_stored{t}") for t in range(YT)]
        block = ctx.enter_context(nc.Block())
        w_out, w_pg = (d[n][0].rearrange("(k p) n -> p k n", p=P) for n in ("w_out", "w_pg"))
        mixT = d["mixT"].rearrange("(k p) t -> p k t", p=P)
        y_tiles = d["y_prompt"][0].rearrange("(i p) c -> i p c", p=P)
        ACT_TILES = (1, 3)

        def cols(ap, part):
            return ap[:, 0:WIDTH[part]].rearrange("p (c t) -> p c t", c=len(CHUNKS[part]))

        def acc_cols(b, part):
            return acc[b][:, 0:len(CHUNKS[part]), 0:CHUNKS[part][0][1]]

        def row(regions, part, m):
            return regions[1 - part][:, bass.ds(m, 1), 0:WIDTH[part]].rearrange("p a t -> p (a t)")

        def y_store(eng, part, t):
            rows = ROWS[part][t]
            dst = d["y_sample"][0] if rows < P else y_tiles[BASE[part] // P + t]
            eng.dma_start(dst, y_tok[part][0:rows, t]).then_inc(y_stored[t], 16)

        def stored_count(part, t):
            return 16 * sum(1 for q in range(part + 1) if t < len(ROWS[q]))

        @block.sync
        def _(sp):
            def load(phase, m, b, it):
                part, gate = phase // 2, phase % 2 == 1
                W.load(sp, w_pg if gate else w_out, m * P, m + phase * KD)
                if (gate and not isinstance(m, int)) or (not gate and isinstance(m, int) and part):
                    sp.wait_ge(e_scaled, m + (part * KD - 1))
                else:
                    sp.wait_ge(evacuated[b], it + phase * (KD // 2))
                sp.dma_start(side[b][:, 0:WIDTH[part]],
                             d["eT" if gate else "xT"][bass.ds(m * P, P), BASE[part]:BASE[part] + WIDTH[part]]) \
                  .then_inc(side_loaded[b], 16)

            for phase in range(4):
                for b in range(2):
                    load(phase, b, b, 0)
                with sp.Fori(1, KD // 2) as i:
                    for b in range(2):
                        load(phase, i * 2 + b, b, i)

        @block.gpsimd
        def _(pool):
            with nc.allow_non_contiguous_dma("per-feature columns of the gain"):
                pool.dma_start(g_pe[:], d["g_pe"][0].rearrange("(k p) -> p k", p=P)).then_inc(gains_loaded, 16)

            def load_mix(part, g):
                if g >= RING:
                    pool.wait_ge(mix_split, part * KD + 2 * (g - RING) + 2)
                raw = mix_raw[1 - part][:, g % RING, :, 0:WIDTH[part]]
                pool.dma_start(raw, mixT[:, 2 * g:2 * g + 2, BASE[part]:BASE[part] + WIDTH[part]]) \
                    .then_inc(mix_loaded[g % RING], 16)

            def rejoin(part, m, b):
                nc.gpsimd.tensor_tensor(total[b][:, 0:WIDTH[part]], row(hi, part, m).bitcast(F32),
                                        row(lo, part, m).bitcast(F32), ALU.add).then_inc(total_done, 1)

            for part in range(2):
                for g in range(0 if part == 0 else RING, KD // 2):
                    load_mix(part, g)
                if part == 1:
                    for t in range(len(ROWS[0])):
                        if t not in ACT_TILES:
                            pool.wait_ge(dve_scaled, t // 2 + 1)
                            y_store(pool, 0, t)
                pool.wait_ge(W.gemm_done, part * 2 * KD + KD)
                pool.dma_start(g_bc[part][:], d["g_final"].unsqueeze(0).to_broadcast([P, D_MODEL])) \
                    .then_inc(g_loaded, 16)
                if part == 0:
                    for g in range(RING):
                        load_mix(1, g)
                pool.wait_ge(h_split, part * KD + KD)
                for b in range(2):
                    rejoin(part, b, b)
                with pool.Fori(1, KD // 2) as i:
                    for b in range(2):
                        pool.wait_ge(h2_done, i * 2 + (part * KD + b - 1))
                        rejoin(part, i * 2 + b, b)
            for t in range(YT):
                if t not in ACT_TILES:
                    pool.wait_ge(dve_scaled, 2 + t // 2 + 1)
                    y_store(pool, 1, t)
            for t in range(YT):
                pool.wait_ge(y_stored[t], stored_count(1, t))

        @block.tensor
        def _(pe):
            def turn(part, m, b):
                pe.wait_ge(h2_done, m + (part * KD + 1))
                if part or not isinstance(m, int) or m >= 2:
                    pe.wait_ge(y_filled, m + (part * KD - 1))
                for t, rows in enumerate(ROWS[part]):
                    tr = pe.transpose(tr_ps[b][0:rows, t * P:(t + 1) * P], h2[b][:, t * P:t * P + rows], ident[:])
                tr.then_inc(turned, 1)

            def tile(phase, m, b, it, hook):
                part = phase // 2
                region = part if phase % 2 == 0 else 1 - part
                ready, base = (mix_split, part * KD) if phase % 2 == 0 else (h_split, part * KD)
                pe.wait_ge(W.split[1], m + (phase * KD + 1))
                pe.wait_ge(evacuated[b], it + phase * KD // 2)
                for k in range(KD):
                    pe.wait_ge(ready, base + k + 1)
                    if hook and k == KD // 2:
                        hook()
                    for n, (w, a) in enumerate(((W.hi[b], hi), (W.hi[b], lo), (W.lo[b], hi))):
                        for c, (start, width) in enumerate(CHUNKS[part]):
                            mm = pe.matmul(acc[b][:, c, 0:width], w[:, k, :],
                                           a[region][:, k, start:start + width],
                                           start=(k == 0 and n == 0), stop=(k == KD - 1 and n == 2))
                mm.then_inc(W.gemm_done, 1)

            with pe.Fori(0, KD // 2) as i:
                for b in range(2):
                    tile(0, i * 2 + b, b, i, None)
            for phase in range(1, 4):
                part = phase // 2
                gate = phase % 2 == 1
                tile(phase, 0, 0, 0, None if gate else (lambda: turn(part - 1, KD - 1, 1)))
                tile(phase, 1, 1, 0, (lambda: turn(part, 0, 0)) if gate else None)
                with pe.Fori(1, KD // 2) as i:
                    for b in range(2):
                        tile(phase, i * 2 + b, b, i, (lambda: turn(part, i * 2 + (b - 1), 1 - b)) if gate else None)
            turn(1, KD - 1, 1)

        @block.scalar
        def _(act):
            def high_mix(part, k):
                act.wait_ge(mix_loaded[k // 2 % RING], 16 * (part * 2 + k // 2 // RING + 1))
                if part == 1 and k == 0:
                    act.wait_ge(W.gemm_done, 2 * KD)
                    act.wait_ge(total_done, KD)
                nc.scalar.copy(hi[part][:, k, 0:WIDTH[part]],
                               mix_raw[1 - part][:, k // 2 % RING, k % 2, 0:WIDTH[part]]).then_inc(mix_hi_done, 1)

            def high_h(part, m, b, it):
                act.wait_ge(evacuated[b], it + (part * KD + 1))
                nc.scalar.copy(row(hi, part, m),
                               total[b][:, 0:WIDTH[part]]).then_inc(h_hi_done, 1)

            def sigmoid(part, m, b, it, used=True):
                act.wait_ge(W.gemm_done, m + (part * 2 * KD + KD + 1))
                if used:
                    act.wait_ge(h2_done, m + (part * KD - 1))
                nc.scalar.activation(cols(sig[b], part), acc_cols(b, part), ACT.Sigmoid).then_inc(evacuated[b], 1)

            def squares(part, m, b):
                act.wait_ge(turned, m + (part * KD + 1))
                if part or not isinstance(m, int) or m:
                    act.wait_ge(squared, m + part * KD)
                for t, rows in enumerate(ROWS[part]):
                    s = nc.scalar.activation(junk[0:rows, t], tr_ps[b][0:rows, t * P:(t + 1) * P], ACT.Square,
                                             accum_out=ssq[0:rows, t, bass.ds(m, 1)])
                s.then_inc(squared, 1)

            def tail(part):
                act.wait_ge(var_done, part + 1)
                nc.scalar.activation(std[:], var[:], ACT.Sqrt).then_inc(std_done, 1)
                act.wait_ge(rstd_done, part + 1)
                for t in ACT_TILES:
                    nc.scalar.mul(y_tok[part][:, t], y_tok[part][:, t], rstd[:, t:t + 1]) \
                        .then_inc(act_scaled, 1)
                    act.wait_ge(act_scaled, part * len(ACT_TILES) + ACT_TILES.index(t) + 1)
                    y_store(act, part, t)

            act.wait_ge(ssq_zero, 1)
            for part in range(2):
                if part == 0:
                    for k in range(KD):
                        high_mix(0, k)
                else:
                    for t in range(len(ROWS[0])):
                        act.wait_ge(y_stored[t], stored_count(0, t))
                with act.Fori(0, KD // 2) as i:
                    for b in range(2):
                        high_h(part, i * 2 + b, b, i)
                for m in range(2):
                    sigmoid(part, m, m, 0, used=part > 0)
                    squares(part, m, m)
                with act.Fori(1, KD // 2 - 1) as i:
                    for b in range(2):
                        sigmoid(part, i * 2 + b, b, i)
                        squares(part, i * 2 + b, b)
                sigmoid(part, KD - 2, 0, KD // 2 - 1)
                squares(part, KD - 2, 0)
                if part == 0:
                    for k in range(4):
                        high_mix(1, k)
                sigmoid(part, KD - 1, 1, KD // 2 - 1)
                if part == 0:
                    for k in range(4, KD):
                        high_mix(1, k)
                squares(part, KD - 1, 1)
                tail(part)

        @block.vector
        def _(dve):
            def low_mix(part, k):
                dve.wait_ge(mix_hi_done, part * KD + k + 1)
                w = WIDTH[part]
                nc.vector.tensor_tensor(lo[part][:, k, 0:w], mix_raw[1 - part][:, k // 2 % RING, k % 2, 0:w],
                                        hi[part][:, k, 0:w].bitcast(F32), ALU.subtract).then_inc(mix_split, 1)

            def residual(part, m, b, it):
                w = WIDTH[part]
                dve.wait_ge(W.gemm_done, m + (part * 2 * KD + 1))
                dve.wait_ge(side_loaded[b], it * 16 + 16 * (part * KD + 1))
                nc.vector.tensor_tensor(cols(total[b], part), acc_cols(b, part), cols(side[b], part), ALU.add) \
                    .then_inc(evacuated[b], 1)
                W.split_tile(dve, nc, m + (part * 2 * KD + 2), b, True)
                dve.wait_ge(h_hi_done, m + (part * KD + 1))
                nc.vector.tensor_tensor(row(lo, part, m), total[b][:, 0:w], row(hi, part, m).bitcast(F32),
                                        ALU.subtract).then_inc(h_split, 1)

            def gate(part, m, b, it, first=False):
                w = WIDTH[part]
                dve.wait_ge(side_loaded[b], it * 16 + 16 * (part * KD + KD // 2 + 1))
                if not first:
                    dve.wait_ge(turned, m + (part * KD - 1))
                nc.vector.scalar_tensor_tensor(
                    h2[b][:, 0:w], side[b][:, 0:w], g_pe[:, bass.ds(m, 1)],
                    G["e_rstd"][:, BASE[part]:BASE[part] + w], ALU.mult, ALU.mult).then_inc(e_scaled, 1)
                dve.wait_ge(e_scaled, m + (part * KD + 1))
                dve.wait_ge(evacuated[b], it + (part * KD + KD // 2 + 1))
                nc.vector.tensor_tensor(h2[b][:, 0:w], h2[b][:, 0:w], sig[b][:, 0:w], ALU.mult).then_inc(e_gated, 1)
                dve.wait_ge(e_gated, m + (part * KD + 1))
                dve.wait_ge(total_done, m + (part * KD + 1))
                nc.vector.tensor_tensor(h2[b][:, 0:w], h2[b][:, 0:w], total[b][:, 0:w], ALU.add) \
                    .then_inc(h2_done, 1)

            def fill(part, m, b):
                dve.wait_ge(squared, m + (part * KD + 1))
                dve.wait_ge(g_loaded, 16 * part + 16)
                full = sum(r == P for r in ROWS[part])
                span = bass.ds(m * P, P)
                f = nc.vector.tensor_tensor(y_tok[part][:, 0:full, span],
                                            tr_ps[b][:, 0:full * P].rearrange("p (i c) -> p i c", i=full),
                                            g_bc[part][:, span].unsqueeze(1).to_broadcast([P, full, P]), ALU.mult)
                if part == 1:
                    f = nc.vector.tensor_tensor(y_tok[part][0:T_SAMPLE, full, span],
                                                tr_ps[b][0:T_SAMPLE, full * P:(full + 1) * P],
                                                g_bc[part][0:T_SAMPLE, span], ALU.mult)
                f.then_inc(y_filled, 1)

            def tail(part):
                nc.vector.reduce_sum(var[:], ssq[:], axis=AX_X).then_inc(var_summed, 1)
                dve.wait_ge(var_summed, part + 1)
                nc.vector.tensor_scalar(var[:], var[:], 1.0 / D_MODEL, EPS, ALU.mult, ALU.add).then_inc(var_done, 1)
                dve.wait_ge(std_done, part + 1)
                dve.wait_ge(y_filled, part * KD + KD)
                if part:
                    dve.wait_ge(act_scaled, len(ACT_TILES))
                nc.vector.reciprocal(rstd[:], std[:]).then_inc(rstd_done, 1)
                dve.wait_ge(rstd_done, part + 1)
                for t, rows in enumerate(ROWS[part]):
                    if t not in ACT_TILES:
                        nc.vector.tensor_scalar(y_tok[part][0:rows, t], y_tok[part][0:rows, t], rstd[0:rows, t:t + 1],
                                                None, ALU.mult).then_inc(dve_scaled, 1)

            nc.vector.memset(ssq[:], 0.0).then_inc(ssq_zero, 1)
            dve.wait_ge(gains_loaded, 16)
            W.split_tile(dve, nc, 0, 0, False)
            for k in range(KD):
                low_mix(0, k)
            W.split_tile(dve, nc, 1, 1, False)
            for part in range(2):
                first_pg = part * 2 * KD + KD
                with dve.Fori(0, KD // 2) as i:
                    for b in range(2):
                        residual(part, i * 2 + b, b, i)
                for m in range(2):
                    gate(part, m, m, 0, first=part == 0)
                    W.split_tile(dve, nc, first_pg + m + 2, m, True)
                    fill(part, m, m)
                with dve.Fori(1, KD // 2 - 1) as i:
                    for b in range(2):
                        gate(part, i * 2 + b, b, i)
                        W.split_tile(dve, nc, i * 2 + (first_pg + b + 2), b, True)
                        fill(part, i * 2 + b, b)
                gate(part, KD - 2, 0, KD // 2 - 1)
                if part == 0:
                    W.split_tile(dve, nc, first_pg + KD, 0, True)
                fill(part, KD - 2, 0)
                if part == 0:
                    for k in range(4):
                        low_mix(1, k)
                gate(part, KD - 1, 1, KD // 2 - 1)
                if part == 0:
                    for k in range(4, KD):
                        low_mix(1, k)
                    W.split_tile(dve, nc, first_pg + KD + 1, 1, True)
                fill(part, KD - 1, 1)
                tail(part)



OUTS = [("y_prompt", (1, T_PROMPT, D_MODEL)), ("y_sample", (1, T_SAMPLE, D_MODEL)),
        ("k_prompt", (1, 1, T_PROMPT, HEADS, HD)), ("v_prompt", (1, 1, T_PROMPT, HEADS, HD)),
        ("logf_prompt", (1, 1, T_PROMPT, HEADS)),
        ("ssm_re_prompt", (1, 1, GROUPS, ST)), ("ssm_im_prompt", (1, 1, GROUPS, ST)),
        ("k_sample", (1, 1, T_SAMPLE, HEADS, HD)), ("v_sample", (1, 1, T_SAMPLE, HEADS, HD)),
        ("logf_sample", (1, 1, T_SAMPLE, HEADS)),
        ("ssm_re_sample", (1, 1, GROUPS, ST)), ("ssm_im_sample", (1, 1, GROUPS, ST))]
SCRATCH = [("xT", (D_MODEL, T)),
           ("zT", (4 * D_ATT, T)),
           ("uT", (2 * D_SSM, L, NJ)),
           ("toep", (P, GROUPS, P)),
           ("w_state", (P, GROUPS, P)),
           ("w_read", (P, GROUPS, P)),
           ("yT", (D_SSM, L, NJ)),
           ("negc", (HEADS, T_PROMPT + T_PAST + T_SAMPLE)),
           ("mixT", (D_MODEL, T)),
           ("eT", (D_MODEL, T))]
SCRATCH_KIND = "Internal"


def clear_semaphores(nc, first, free):
    with nc.Block() as block:
        @block.gpsimd
        def _(pool):
            nc.gpsimd.sem_clear(range(first, max(free) + 1))


def program(nc, d, stages=None):
    for name, shape in SCRATCH:
        d[name] = nc.dram_tensor(name, shape, F32, kind=SCRATCH_KIND).ap()
    with ExitStack() as ctx:
        sb, ps, sem = allocators(nc, ctx)
        pool_sems = {n: sem(n) for n in ("zero_stored", "xT_stored0", "xT_stored1", "gate_stored", "const_stored",
                                         "v_swapped", "y_stored", "hl_stored", "k_stored", "v_stored", "mix_stored",
                                         "y_loaded", "gs_loaded0", "gs_loaded1")}
        G = {"sem": pool_sems, "passed": sem("passed"), "ident": sb("ident", [P, P]), "ones_col": sb("ones_col", [P, 1]), "eps": sb("eps", [P, 1])}
        first_sem = nc.free_semaphores[0]
        with ExitStack() as ctx_n:
            sb_n, _, _ = allocators(nc, ctx_n)
            G["n_hi"] = sb_n("n_hi", [P, KD, T], F32R)
            G["n_lo"] = sb_n("n_lo", [P, KD, T], F32R)
            stage_norm(nc, d, G)
            stage_project(nc, d, G)
        stage_attention(nc, d, G)
        clear_semaphores(nc, first_sem, nc.free_semaphores)
        G["e_rstd"] = sb("e_rstd", [P, T])
        stage_side(nc, d, G)
        stage_output(nc, d, G)


INS = ("x_prompt", "x_sample", "p_prompt", "p_sample", "cache_k", "cache_v", "cache_logf", "state_ssm_re",
       "state_ssm_im", "g_in", "w_in", "b_f", "a_re", "a_im", "log_dt", "b_re", "b_im", "c_re", "c_im", "d_skip",
       "w_glu", "w_out", "w_pe", "g_pe", "w_pg", "g_final")


def kernel(**inputs):
    import concourse.bacc as bacc
    from concourse.bass_utils import run_bass_kernel_spmd

    nc = bacc.Bacc("TRN2", target_bir_lowering=False, num_devices=1)
    arrays, d = {}, {}
    for name in INS:
        a = np.ascontiguousarray(inputs[name])
        arrays[f"in_{name}_dram"] = a
        d[name] = nc.dram_tensor(f"in_{name}_dram", a.shape, mybir.dt.from_np(a.dtype), kind="ExternalInput").ap()
    for i, (name, shape) in enumerate(OUTS):
        d[name] = nc.dram_tensor(f"out_{i}_dram", shape, F32, kind="ExternalOutput").ap()
    program(nc, d)
    r = run_bass_kernel_spmd(nc, [arrays], core_ids=[0])
    return tuple(r.results[0][f"out_{i}_dram"] for i in range(len(OUTS)))
```

```python
import math
from contextlib import ExitStack

import numpy as np

import concourse.bass as bass
from concourse import mybir
from concourse.alu_op_type import AluOpType as ALU

P = 128
F32 = mybir.dt.float32
F32R = mybir.dt.float32r
BF16 = mybir.dt.bfloat16
ACT = mybir.ActivationFunctionType
AX_X = mybir.AxisListType.X

T_PROMPT, T_SAMPLE, T_PAST = 1024, 32, 512
T = T_PROMPT + T_SAMPLE
D_MODEL = 2048
KD = D_MODEL // P
D_ATT = D_SSM = 1024
KS = D_SSM // P
HEADS, HD = 8, 128
GROUPS, GC, ST = 64, 16, 64
D_PLE = 256
KP = D_PLE // P
EPS = 1e-6
NEG = -1e30
L = 8
NJ = T // L
NJP = T_PROMPT // L
NC = 3
CH = T // NC
TT = T_PROMPT // P
OFF_F = 3 * D_ATT
OFF_GA = OFF_F + HEADS
OFF_U = OFF_GA + D_ATT
OFF_GS = OFF_U + D_SSM
PB = 4
NPB = GROUPS // PB


class Chain:

    def __init__(self, eng, sem):
        self.eng, self.sem, self.base, self.n = eng, sem, 0, 0

    def link(self, ins):
        ins.then_inc(self.sem, 1)
        self.n += 1
        self.eng.wait_ge(self.sem, self.base + self.n)

    def enter_loop(self, i, per_iteration):
        self.before = self.base + self.n
        self.base, self.n, self.per = self.before + i * per_iteration, 0, per_iteration

    def leave_loop(self, iterations):
        assert self.n == self.per, (self.n, self.per)
        self.base, self.n = self.before + iterations * self.per, 0


def allocators(nc, ctx):
    def sb(name, shape, dt=F32):
        return ctx.enter_context(nc.sbuf_tensor(name, shape, dt))

    def ps(name, shape, dt=F32):
        return ctx.enter_context(nc.psum_tensor(name, shape, dt))

    def sem(name):
        return ctx.enter_context(nc.semaphore(name))

    return sb, ps, sem


def gemm_tile(pe, acc, w_hi, w_lo, a_hi, a_lo, kt, act_ready=None, hooks=None):
    for k in range(kt):
        if act_ready is not None:
            pe.wait_ge(act_ready, k + 1)
        if hooks and k in hooks:
            hooks[k]()
        for n, (w, a) in enumerate(((w_hi, a_hi), (w_hi, a_lo), (w_lo, a_hi))):
            for c in range(NC):
                mm = pe.matmul(acc[:, c, 0:CH], w[:, k, :], a[:, k, c * CH:(c + 1) * CH],
                               start=(k == 0 and n == 0), stop=(k == kt - 1 and n == 2))
    return mm


class Weights:

    def __init__(self, sb, sem, name, kt):
        self.kt, self.kh = kt, kt // 2
        self.raw = [sb(f"{name}_raw{h}", [P, self.kh, P]) for h in range(2)]
        self.hi = [sb(f"{name}_hi{b}", [P, kt, P], F32R) for b in range(2)]
        self.lo = [sb(f"{name}_lo{b}", [P, kt, P], F32R) for b in range(2)]
        self.loaded = [sem(f"{name}_loaded{h}") for h in range(2)]
        self.hi_done = sem(f"{name}_hi_done")
        self.split = [sem(f"{name}_split{h}") for h in range(2)]
        self.gemm_done = sem(f"{name}_gemm_done")

    def load(self, sp, w, col, n):
        for h in range(2):
            sp.wait_ge(self.split[h], n)
            sp.dma_start(self.raw[h][:], w[:, h * self.kh:(h + 1) * self.kh, bass.ds(col, P)]) \
              .then_inc(self.loaded[h], 16)

    def split_tile(self, dve, nc, n, b, in_use):
        if in_use:
            dve.wait_ge(self.gemm_done, n - 1)
        for h in range(2):
            dve.wait_ge(self.loaded[h], (n + 1) * 16)
            nc.vector.tensor_copy(self.hi[b][:, h * self.kh:(h + 1) * self.kh], self.raw[h][:]) \
              .then_inc(self.hi_done, 1)
        for h in range(2):
            part = slice(h * self.kh, (h + 1) * self.kh)
            dve.wait_ge(self.hi_done, n * 2 + h + 1)
            nc.vector.tensor_tensor(self.lo[b][:, part], self.raw[h][:], self.hi[b][:, part].bitcast(F32),
                                    ALU.subtract).then_inc(self.split[h], 1)


def settle(eng, passed):
    eng.sem_inc(passed, 1)


def identity(nc, pool, ident, chain):
    chain.link(nc.gpsimd.memset(ident[:], 0.0))
    chain.link(nc.gpsimd.affine_select(out=ident[:], in_=ident[:], compare_op=ALU.not_equal, fill=1.0, base=0,
                                       pattern=[[-1, P]], channel_multiplier=1))



def stage_norm(nc, d, G):
    with ExitStack() as ctx:
        sb, ps, sem = allocators(nc, ctx)
        x_in = [sb(f"x_in{b}", [P, D_MODEL]) for b in range(2)]
        n_rows = [sb(f"n_rows{b}", [P, D_MODEL]) for b in range(2)]
        g_bc = sb("g_bc", [P, D_MODEL])
        stat = [sb(f"x_stat{b}", [P, 3]) for b in range(2)]
        xT = [sb(f"xT{b}", [P, KD, P]) for b in range(2)]
        x_ps, n_ps = ps("x_ps", [P, 4, 512]), ps("n_ps", [P, 4, 512])
        x_loaded = [sem(f"x_loaded{b}") for b in range(2)]
        xT_stored = [G["sem"][f"xT_stored{b}"] for b in range(2)]
        x_squared, std_done, rstd_done, n_ready, x_turned, n_turned, consts, g_loaded = (
            sem(n) for n in ("x_squared", "x_std_done", "x_rstd_done", "n_ready", "x_turned", "n_turned", "consts",
                             "g_loaded"))
        xT_act, xT_dve, n_hi_done, n_split, pool_order = (
            sem(n) for n in ("xT_act", "xT_dve", "n_hi_done", "n_split", "pool_order"))
        block = ctx.enter_context(nc.Block())
        n_hi, n_lo = G["n_hi"], G["n_lo"]
        x_tiles = d["x_prompt"].rearrange("a (i p) c -> (a i) p c", p=P)
        xT_dram = d["xT"].rearrange("(f p) t -> p f t", p=P)
        ACT_BANKS = 3

        def tiles(eng, body):
            with eng.Fori(0, TT // 2) as i:
                for b in range(2):
                    body(i * 2 + b, b, i, P)
            body(TT, 0, TT // 2, T_SAMPLE)

        def blocks(bank, rows):
            return bank.rearrange("p (q t) -> p q t", q=4)[:, :, 0:rows]

        @block.sync
        def _(sp):
            for b in range(2):
                sp.dma_start(x_in[b][:], x_tiles[b]).then_inc(x_loaded[b], 16)
                if b == 0:
                    sp.dma_start(g_bc[:], d["g_in"].to_broadcast([P, D_MODEL])).then_inc(g_loaded, 16)

            def free(n):
                sp.wait_ge(x_turned, n + 1)
                sp.wait_ge(n_ready, n + 1)

            with sp.Fori(0, TT // 2 - 1) as i:
                for b in range(2):
                    free(i * 2 + b)
                    sp.dma_start(x_in[b][:], x_tiles[i * 2 + (b + 2)]).then_inc(x_loaded[b], 16)
            free(TT - 2)
            sp.dma_start(x_in[0][0:T_SAMPLE, :], d["x_sample"][0]).then_inc(x_loaded[0], 16)

        @block.gpsimd
        def _(pool):
            chain = Chain(pool, pool_order)
            identity(nc, pool, G["ident"], chain)
            chain.link(nc.gpsimd.memset(G["eps"][:], EPS))
            nc.gpsimd.memset(G["ones_col"][:], 1.0).then_inc(consts, 1)

            def store(n, b, it, rows):
                pool.wait_ge(xT_act, n + 1)
                pool.wait_ge(xT_dve, n + 1)
                pool.dma_start(xT_dram[:, :, bass.ds(n * P, rows)], xT[b][:, :, 0:rows]).then_inc(xT_stored[b], 16)
            tiles(pool, store)
            pool.wait_ge(xT_stored[0], 16 * (TT // 2 + 1))
            pool.wait_ge(xT_stored[1], 16 * (TT // 2))

        @block.tensor
        def _(pe):
            pe.wait_ge(consts, 1)

            def turn(n, b, it, rows):
                pe.wait_ge(x_loaded[b], it * 16 + 16)
                pe.wait_ge(xT_act, n)
                pe.wait_ge(xT_dve, n)
                for f in range(KD):
                    tr = pe.transpose(x_ps[:, f // 4, (f % 4) * P:(f % 4) * P + rows],
                                      x_in[b][0:rows, f * P:(f + 1) * P], G["ident"][0:rows, 0:rows])
                tr.then_inc(x_turned, 1)
                pe.wait_ge(n_ready, n + 1)
                pe.wait_ge(n_split, n)
                for f in range(KD):
                    tr = pe.transpose(n_ps[:, f // 4, (f % 4) * P:(f % 4) * P + rows],
                                      n_rows[b][0:rows, f * P:(f + 1) * P], G["ident"][0:rows, 0:rows])
                tr.then_inc(n_turned, 1)
            tiles(pe, turn)

        @block.scalar
        def _(act):
            act.wait_ge(consts, 1)

            def squares(n, b, it, rows, first=False):
                act.wait_ge(x_loaded[b], it * 16 + 16)
                if not first:
                    act.wait_ge(n_turned, n - 1)
                nc.scalar.activation(n_rows[b][0:rows, :], x_in[b][0:rows, :], ACT.Square,
                                     accum_out=stat[b][0:rows, 0:1]).then_inc(x_squared, 1)
                act.wait_ge(x_squared, n + 1)
                nc.scalar.activation(stat[b][0:rows, 1:2], stat[b][0:rows, 0:1], ACT.Sqrt, scale=1.0 / D_MODEL,
                                     bias=G["eps"][0:rows]).then_inc(std_done, 1)

            def copies(n, b, it, rows):
                act.wait_ge(x_turned, n + 1)
                act.wait_ge(xT_stored[b], it * 16)
                for f in range(ACT_BANKS):
                    c = nc.scalar.copy(xT[b][:, 4 * f:4 * f + 4, 0:rows], blocks(x_ps[:, f, :], rows))
                c.then_inc(xT_act, 1)
                act.wait_ge(n_turned, n + 1)
                for f in range(4):
                    nc.scalar.copy(n_hi[:, 4 * f:4 * f + 4, bass.ds(n * P, rows)], blocks(n_ps[:, f, :], rows)) \
                        .then_inc(n_hi_done, 1)

            squares(0, 0, 0, P, first=True)
            squares(1, 1, 0, P, first=True)
            copies(0, 0, 0, P)
            with act.Fori(1, TT // 2) as i:
                squares(i * 2, 0, i, P)
                copies(i * 2 - 1, 1, i - 1, P)
                squares(i * 2 + 1, 1, i, P)
                copies(i * 2, 0, i, P)
            squares(TT, 0, TT // 2, T_SAMPLE)
            copies(TT - 1, 1, TT // 2 - 1, P)
            copies(TT, 0, TT // 2, T_SAMPLE)

        @block.vector
        def _(dve):
            dve.wait_ge(g_loaded, 16)

            def normalize(n, b, it, rows):
                dve.wait_ge(std_done, n + 1)
                nc.vector.reciprocal(stat[b][0:rows, 2:3], stat[b][0:rows, 1:2]).then_inc(rstd_done, 1)
                dve.wait_ge(rstd_done, n + 1)
                nc.vector.scalar_tensor_tensor(n_rows[b][0:rows, :], x_in[b][0:rows, :], stat[b][0:rows, 2:3],
                                               g_bc[0:rows, :], ALU.mult, ALU.mult).then_inc(n_ready, 1)

            def lows(n, b, it, rows):
                dve.wait_ge(x_turned, n + 1)
                dve.wait_ge(xT_stored[b], it * 16)
                for f in range(ACT_BANKS, 4):
                    c = nc.vector.tensor_copy(xT[b][:, 4 * f:4 * f + 4, 0:rows], blocks(x_ps[:, f, :], rows))
                c.then_inc(xT_dve, 1)
                for f in range(4):
                    dve.wait_ge(n_hi_done, n * 4 + (f + 1))
                    c = nc.vector.tensor_tensor(
                        n_lo[:, 4 * f:4 * f + 4, bass.ds(n * P, rows)], blocks(n_ps[:, f, :], rows),
                        n_hi[:, 4 * f:4 * f + 4, bass.ds(n * P, rows)].bitcast(F32), ALU.subtract)
                c.then_inc(n_split, 1)

            normalize(0, 0, 0, P)
            with dve.Fori(1, TT // 2) as i:
                normalize(i * 2 - 1, 1, i - 1, P)
                lows(i * 2 - 2, 0, i - 1, P)
                normalize(i * 2, 0, i, P)
                lows(i * 2 - 1, 1, i - 1, P)
            normalize(TT - 1, 1, TT // 2 - 1, P)
            lows(TT - 2, 0, TT // 2 - 1, P)
            normalize(TT, 0, TT // 2, T_SAMPLE)
            lows(TT - 1, 1, TT // 2 - 1, P)
            lows(TT, 0, TT // 2, T_SAMPLE)



def stage_project(nc, d, G):
    tiles = 6 * D_ATT // P
    with ExitStack() as ctx:
        sb, ps, sem = allocators(nc, ctx)
        W = Weights(sb, sem, "w_in", KD)
        acc = [ps(f"acc{b}", [P, NC, 512]) for b in range(2)]
        bank_c = ps("bank_c", [P, 512])
        bank_w = ps("bank_w", [P, 512])
        z_out = sb("z_out", [P, T])
        evacuated = [sem(f"evacuated{b}") for b in range(2)]
        z_stored = sem("z_stored")
        v_swapped, y_stored, hl_stored, const_stored, gate_stored = (
            G["sem"][n] for n in ("v_swapped", "y_stored", "hl_stored", "const_stored", "gate_stored"))

        h0, carry = (sb(n, [P, 2, GROUPS]) for n in ("h0", "carry"))
        rho, turn = sb("rho", [P, GROUPS]), sb("turn", [P, 2, GROUPS])
        h_last = sb("h_last", [P, 2, GROUPS])

        arena = nc.sbuf_base
        sgn = sb("sgn", [P, 2])
        lam_re, lam_im, dt, ang, mag, q_re, q_im = (
            sb(n, [P, GROUPS]) for n in ("lam_re", "lam_im", "dt", "ang", "mag", "q_re", "q_im"))
        rate = dt
        tmp = [sb(f"tmp{i}", [P, GROUPS]) for i in range(3)]
        pw_re, pw_im = (sb(n, [P, GROUPS, L + 1]) for n in ("pw_re", "pw_im"))
        b_blk = sb("b_blk", [P, 2, PB, GC])
        c_blk = sb("c_blk", [PB * GC, 2, 2, ST])
        bt = sb("bt", [P, 2, PB, GC])
        ct = sb("ct", [P, 2, PB, GC])
        tmp_b = tmp[2].rearrange("p (g c) -> p g c", g=PB)
        xin = sb("xin", [P, PB, L, GC])
        tmp_c = sb("tmp_c", [P, PB, L + 1, GC])
        ca = sb("ca", [P, PB, L + 1, GC])
        w_state_s = sb("w_state_s", [P, PB, P])
        kern_at = (nc.sbuf_base + 31) // 32 * 32
        kern = sb("kern", [GC, PB, 2 * L - 1, GC])
        assert 4 * 4 * 2 * ST <= 4 * PB * (2 * L - 1) * GC
        a_raw = nc.alloc_sbuf_tensor_at("a_raw", [GROUPS, 4, 2, ST], F32, offset=kern_at)
        d_bc = sb("d_bc", [GC, PB * GC])
        d_diag = sb("d_diag", [GC, PB, GC])
        b_f = sb("b_f_s", [HEADS, 1])
        lf = z_out[0:HEADS, :]
        gate_past = sb("gate_past", [P, T_PAST // P, HEADS])
        negs_at = (nc.sbuf_base + 31) // 32 * 32
        negs = sb("negs", [HEADS, T_PAST + T])
        assert 8 * GROUPS * L <= 4 * (T_PAST + T)
        pw_back = nc.alloc_sbuf_tensor_at("pw_back", [P, 2, GROUPS, L], F32, offset=negs_at)
        sp_part = negs[:, 0:T]
        lf_rows = w_state_s.rearrange("p g m -> p (g m)")[:, 0:(TT + 1) * HEADS] \
            .rearrange("p (i h) -> p i h", h=HEADS)

        at = [(arena + 31) // 32 * 32]

        def placed(name, shape):
            t = nc.alloc_sbuf_tensor_at(name, shape, F32, offset=at[0])
            at[0] += -(-4 * int(np.prod(shape[1:])) // 32) * 32
            assert at[0] <= nc.sbuf_usable_end
            return t

        u_in = [placed(f"u_in{b}", [P, PB, NJ]) for b in range(2)]
        ws_in, toep_in, wr_in = (placed(n, [P, PB, P]) for n in ("ws_in", "toep_in", "wr_in"))
        v, va, vb = placed("v", [P, 2, PB, NJ]), placed("va", [P, PB, NJ]), placed("vb", [P, PB, NJ])
        rot = placed("rot", [P, 2, PB, NJ])
        h_prev = placed("h_prev", [P, PB, NJ + 1])
        h_rows = placed("h_rows", [GROUPS, 2, P])

        (u_loaded0, u_loaded1, ws_loaded, ro_loaded, v_done, v_copied, v_used, h_ready, y_done,
         y_copied, rot_ready, hl_ready, hl_turned, hl_copied, arena_free, hist_zero) = (
            sem(n) for n in ("u_loaded0", "u_loaded1", "ws_loaded", "ro_loaded", "v_done", "v_copied",
                             "v_used", "h_ready", "y_done", "y_copied", "rot_ready", "hl_ready",
                             "hl_turned", "hl_copied", "arena_free", "hist_zero"))
        u_loaded = (u_loaded0, u_loaded1)
        small_loaded, b_loaded, c_loaded = sem("small_loaded"), sem("b_loaded"), sem("c_loaded")
        sgn_set, raw_turned, dve_order = sem("sgn_set"), sem("raw_turned"), sem("dve_order")
        dt_done, arg_done, mag_done, sin_done, cos_arg, cos_done = (
            sem(n) for n in ("dt_done", "arg_done", "mag_done", "sin_done", "cos_arg", "cos_done"))
        b_used, c_turned, c_taken, xin_done, w_turned, w_copied, ca_done, k_done, k_copied, d_added = (
            sem(n) for n in ("b_used", "c_turned", "c_taken", "xin_done", "w_turned", "w_copied", "ca_done",
                             "k_done", "k_copied", "d_added"))
        gate_in, gate_abs, gate_exp, gate_ln, past_turned, lf_done, lf_turned, lf_copied, negc_done = (
            sem(n) for n in ("gate_in", "gate_abs", "gate_exp", "gate_ln", "past_turned", "lf_done", "lf_turned",
                             "lf_copied", "negc_done"))
        block = ctx.enter_context(nc.Block())
        ident = G["ident"]
        n_small = 11

        w_in = d["w_in"][0].rearrange("(k p) n -> p k n", p=P)
        zT, uT = d["zT"], d["uT"].rearrange("r k j -> r (k j)")
        u_src = d["uT"][0:D_SSM].rearrange("(g c) k j -> k c g j", c=GC)
        y_dst = d["yT"].rearrange("(g c) k j -> k c g j", c=GC)
        b_re, b_im = (d[n][0].rearrange("g p c -> p g c") for n in ("b_re", "b_im"))
        c_re, c_im = (d[n][0].rearrange("g c p -> (g c) p") for n in ("c_re", "c_im"))

        @block.sync
        def _(sp):
            W.load(sp, w_in, OFF_F, 0)
            with nc.allow_non_contiguous_dma("small constants"):
                for h in range(2):
                    sp.dma_start(a_raw[:, 0, h, :], d["a_re"][0]).then_inc(small_loaded, 16)
                    sp.dma_start(a_raw[:, 1, h, :], d["a_im"][0]).then_inc(small_loaded, 16)
                    sp.dma_start(a_raw[:, 2 + h, 0, :], d["state_ssm_im" if h else "state_ssm_re"][0, 0]) \
                        .then_inc(small_loaded, 16)
                    sp.dma_start(a_raw[:, 2 + h, 1, :], d["state_ssm_re" if h else "state_ssm_im"][0, 0]) \
                        .then_inc(small_loaded, 16)
                sp.dma_start(dt[:], d["log_dt"].to_broadcast([P, GROUPS])).then_inc(small_loaded, 16)
                sp.dma_start(b_f[:], d["b_f"].rearrange("a h -> h a")).then_inc(small_loaded, 16)
                sp.dma_start(gate_past[:], d["cache_logf"][0, 0].rearrange("(i p) h -> p i h", p=P)) \
                    .then_inc(small_loaded, 16)

            def load_block(i):
                sp.wait_ge(b_used, i)
                sp.wait_ge(d_added, i)
                for part, (top, bottom) in enumerate(((b_re, b_im), (b_im, b_re))):
                    sp.dma_start(b_blk[0:ST, part], top[:, bass.ds(i * PB, PB), :]).then_inc(b_loaded, 16)
                    sp.dma_start(b_blk[ST:P, part], bottom[:, bass.ds(i * PB, PB), :]).then_inc(b_loaded, 16)
                sp.dma_start(d_bc[:], d["d_skip"][:, bass.ds(i * PB * GC, PB * GC)].to_broadcast([GC, PB * GC])) \
                    .then_inc(b_loaded, 16)
                sp.wait_ge(c_turned, i)
                for part, (left, right) in enumerate(((c_re, c_im), (c_im, c_re))):
                    sp.dma_start(c_blk[:, part, 0], left[bass.ds(i * PB * GC, PB * GC)]).then_inc(c_loaded, 16)
                    sp.dma_start(c_blk[:, part, 1], right[bass.ds(i * PB * GC, PB * GC)]).then_inc(c_loaded, 16)

            with nc.allow_non_contiguous_dma("64-byte rows of B"):
                with sp.Fori(0, 8) as i:
                    W.load(sp, w_in, i * (2 * P) + OFF_U, i * 2 + 1)
                    load_block(i)
                    W.load(sp, w_in, i * (2 * P) + (OFF_U + P), i * 2 + 2)
                with sp.Fori(8, NPB) as i:
                    W.load(sp, w_in, i * (2 * P) - 16 * P, i * 2 + 1)
                    load_block(i)
                    W.load(sp, w_in, i * (2 * P) - 15 * P, i * 2 + 2)

            def load_u(q, b):
                for k in range(L):
                    sp.dma_start(u_in[b][k * GC:(k + 1) * GC], u_src[k][:, bass.ds(q * PB, PB), :]) \
                        .then_inc(u_loaded[b], 16)

            def load_state(q):
                sp.wait_ge(v_done, q)
                sp.dma_start(ws_in[:], d["w_state"][:, bass.ds(q * PB, PB), :]).then_inc(ws_loaded, 16)

            def load_readout(q):
                sp.wait_ge(y_done, q)
                sp.dma_start(toep_in[:], d["toep"][:, bass.ds(q * PB, PB), :]).then_inc(ro_loaded, 16)
                sp.dma_start(wr_in[:], d["w_read"][:, bass.ds(q * PB, PB), :]).then_inc(ro_loaded, 16)

            n0 = 2 * NPB + 1
            W.load(sp, w_in, 2 * D_ATT, n0)
            sp.wait_ge(z_stored, 16 * (n0 - 1))
            sp.wait_ge(arena_free, 1)
            load_u(0, 0)
            load_state(0)
            W.load(sp, w_in, 2 * D_ATT + P, n0 + 1)
            load_readout(0)
            load_u(1, 1)
            load_state(1)

            def recur_loads(i, col):
                for b in range(2):
                    q = i * 2 + b
                    W.load(sp, w_in, col + b * P, q + n0)
                    load_readout(q - 1)
                    sp.wait_ge(y_stored, (q - 1) * 128)
                    load_u(q, b)
                    load_state(q)

            with sp.Fori(1, 4) as i:
                recur_loads(i, i * (2 * P) + 2 * D_ATT)
            with sp.Fori(4, 8) as i:
                recur_loads(i, i * (2 * P) + (OFF_GA - 8 * P))
            load_readout(NPB - 1)

        @block.gpsimd
        def _(pool):
            nc.gpsimd.memset(sgn[0:ST, 0:1], -1.0)
            nc.gpsimd.memset(sgn[ST:P, 0:1], 1.0)
            nc.gpsimd.memset(sgn[0:ST, 1:2], 1.0)
            nc.gpsimd.memset(sgn[ST:P, 1:2], -1.0).then_inc(sgn_set, 1)
            pool.wait_ge(negc_done, 1)
            pool.dma_start(d["negc"][:, 0:T_PROMPT], negs[:, 0:T_PROMPT]).then_inc(gate_stored, 16)
            pool.dma_start(d["negc"][:, T_PROMPT:], negs[:, T_PROMPT:]).then_inc(gate_stored, 16)
            pool.wait_ge(lf_copied, 1)
            pool.dma_start(d["logf_prompt"][0, 0].rearrange("(i p) h -> p i h", p=P), lf_rows[:, 0:TT]) \
                .then_inc(gate_stored, 16)
            pool.dma_start(d["logf_sample"][0, 0], lf_rows[0:T_SAMPLE, TT]).then_inc(gate_stored, 16)
            with pool.Fori(0, NPB) as i:
                pool.wait_ge(w_copied, i + 1)
                pool.dma_start(d["w_state"][:, bass.ds(i * PB, PB), :], w_state_s[:]).then_inc(const_stored, 16)
                pool.wait_ge(ca_done, i + 1)
                settle(pool, G["passed"])
                pool.dma_start(d["w_read"][:, bass.ds(i * PB, PB), :],
                               ca[:, :, 1:, :].rearrange("p g k c -> p g (k c)")).then_inc(const_stored, 16)
                pool.wait_ge(d_added, i + 1)
                settle(pool, G["passed"])
                for k in range(L):
                    pool.dma_start(d["toep"][k * GC:(k + 1) * GC, bass.ds(i * PB, PB), :],
                                   kern[:, :, L - 1 - k:2 * L - 1 - k, :].rearrange("p g k c -> p g (k c)")) \
                        .then_inc(const_stored, 16)
            pool.wait_ge(const_stored, 16 * (2 + L) * NPB)
            pool.wait_ge(gate_stored, 64)
            pool.wait_ge(d_added, NPB)
            pool.wait_ge(c_turned, NPB)
            pool.wait_ge(k_done, NPB)
            pool.wait_ge(z_stored, 16 * 2 * NPB)
            nc.gpsimd.memset(h_prev[:, :, 0:1], 0.0).then_inc(arena_free, 1)

            def swap(q):
                pool.wait_ge(v_copied, q * 2 + 2)
                pool.wait_ge(v_used, q)
                settle(pool, G["passed"])
                pool.dma_start(v[0:ST, 1], v[ST:P, 0]).then_inc(v_swapped, 16)
                pool.dma_start(v[ST:P, 1], v[0:ST, 0]).then_inc(v_swapped, 16)

            def store_y(q, b):
                pool.wait_ge(y_copied, q * 2 + 2)
                for k in range(L):
                    pool.dma_start(y_dst[k][:, bass.ds(q * PB, PB), :], u_in[b][k * GC:(k + 1) * GC]) \
                        .then_inc(y_stored, 16)

            swap(0)
            store_y(0, 0)
            swap(1)
            with pool.Fori(1, NPB // 2) as i:
                for b in range(2):
                    store_y(i * 2 + (b - 1), 1 - b)
                    swap(i * 2 + b)
            store_y(NPB - 1, 1)
            pool.wait_ge(hl_copied, 1)
            for s, names in enumerate((("ssm_re_prompt", "ssm_im_prompt"), ("ssm_re_sample", "ssm_im_sample"))):
                for h, name in enumerate(names):
                    pool.dma_start(d[name][0, 0], h_rows[:, s, h * ST:(h + 1) * ST]).then_inc(hl_stored, 16)
            pool.wait_ge(hl_stored, 64)
            pool.wait_ge(y_stored, 128 * NPB)

        @block.tensor
        def _(pe):
            def tile(n, b, it, hooks=None):
                pe.wait_ge(W.split[1], n + 1)
                pe.wait_ge(evacuated[b], it)
                gemm_tile(pe, acc[b], W.hi[b], W.lo[b], G["n_hi"], G["n_lo"], KD, hooks=hooks) \
                    .then_inc(W.gemm_done, 1)

            def turn_raw():
                pe.wait_ge(small_loaded, 16 * n_small)
                for q in range(4):
                    tr = pe.transpose(bank_c[:, q * GROUPS:(q + 1) * GROUPS],
                                      a_raw[:, q].rearrange("g h p -> g (h p)"), ident[0:GROUPS, 0:GROUPS])
                tr.then_inc(raw_turned, 1)
                for q in range(T_PAST // P):
                    tr = pe.transpose(bank_w[0:HEADS, q * P:(q + 1) * P], gate_past[:, q, :], ident[:])
                tr.then_inc(past_turned, 1)

            tile(0, 0, 0, {KD // 2: turn_raw})

            def turn_gates():
                pe.wait_ge(lf_done, 1)
                for q in range(TT + 1):
                    rows = P if q < TT else T_SAMPLE
                    tr = pe.transpose(bank_w[0:rows, q * HEADS:(q + 1) * HEADS], lf[:, q * P:q * P + rows],
                                      ident[0:HEADS, 0:HEADS])
                tr.then_inc(lf_turned, 1)

            def iteration(i, first=False):
                def turn_c():
                    pe.wait_ge(c_loaded, i * 64 + 64)
                    pe.wait_ge(k_copied, i)
                    settle(pe, G["passed"])
                    for q in range(2):
                        tr = pe.transpose(bank_c[:, q * PB * GC:(q + 1) * PB * GC],
                                          c_blk[:, q].rearrange("r h p -> r (h p)"),
                                          ident[0:PB * GC, 0:PB * GC])
                    tr.then_inc(c_turned, 1)

                def turn_state():
                    pe.wait_ge(xin_done, i + 1)
                    pe.wait_ge(w_copied, i)
                    pe.wait_ge(lf_copied, 1)
                    for g in range(PB):
                        tr = pe.transpose(bank_w[:, g * P:(g + 1) * P],
                                          xin[:, g].rearrange("p k c -> p (k c)"), ident[:])
                    tr.then_inc(w_turned, 1)

                def kernels():
                    pe.wait_ge(ca_done, i + 1)
                    for g in range(PB):
                        mm = pe.matmul(bank_c[0:GC, g * P:(g + 1) * P], bt[:, 0, g, :],
                                       ca[:, g, 0:L, :].rearrange("p k c -> p (k c)"), start=True, stop=True)
                    mm.then_inc(k_done, 1)
                return {2: turn_c, 11: turn_state}, {4: kernels}

            tile(1, 1, 0, {KD - 1: turn_gates})
            h2 = iteration(0)

            tile(2, 0, 1, {0: h2[0][2], 8: h2[0][11], 13: h2[1][4]})
            with pe.Fori(1, NPB) as i:
                first, second = iteration(i)
                tile(i * 2 + 1, 1, i, first)
                tile(i * 2 + 2, 0, i + 1, second)

            def states(q, b):
                pe.wait_ge(u_loaded[b], (q - b) * 64 + 128)
                pe.wait_ge(ws_loaded, q * 16 + 16)
                for g in range(PB):
                    if g % 2 == 0:
                        pe.wait_ge(y_copied, q * 2)
                    mm = pe.matmul((bank_c, bank_w)[g // 2][:, g % 2 * NJ:(g % 2 + 1) * NJ], ws_in[:, g],
                                   u_in[b][:, g], start=True, stop=True)
                mm.then_inc(v_done, 1)

            def readout(q, b):
                pe.wait_ge(h_ready, q + 1)
                pe.wait_ge(ro_loaded, q * 32 + 32)
                pe.wait_ge(v_copied, q * 2 + 2)
                for g in range(PB):
                    out = (bank_c, bank_w)[g // 2][:, g % 2 * NJ:(g % 2 + 1) * NJ]
                    pe.matmul(out, toep_in[:, g], u_in[b][:, g], start=True, stop=False)
                    mm = pe.matmul(out, wr_in[:, g], h_prev[:, g, 0:NJ], start=False, stop=True)
                mm.then_inc(y_done, 1)

            def recur_hooks(q, b, first=False):
                hooks = {6: lambda: states(q, b)}
                if not first:
                    hooks[2] = lambda: readout(q - 1, 1 - b)
                return hooks

            first_states = {5: lambda: (pe.wait_ge(arena_free, 1), states(0, 0))}
            tile(2 * NPB + 1, 1, NPB, first_states)
            tile(2 * NPB + 2, 0, NPB + 1, recur_hooks(1, 1))
            with pe.Fori(1, NPB // 2) as i:
                tile(i * 2 + (2 * NPB + 1), 1, i + NPB, recur_hooks(i * 2, 0))
                tile(i * 2 + (2 * NPB + 2), 0, i + (NPB + 1), recur_hooks(i * 2 + 1, 1))
            readout(NPB - 1, 1)
            pe.wait_ge(hl_ready, 1)
            pe.wait_ge(y_copied, NPB * 2)
            for s in range(2):
                tr = pe.transpose(bank_c[0:GROUPS, s * P:(s + 1) * P], h_last[:, s], ident[:])
            tr.then_inc(hl_turned, 1)

        @block.scalar
        def _(act):
            act.wait_ge(small_loaded, 16 * n_small)
            nc.scalar.activation(dt[:], dt[:], ACT.Exp).then_inc(dt_done, 1)
            act.wait_ge(arg_done, 1)
            nc.scalar.activation(mag[:], rate[:], ACT.Exp).then_inc(mag_done, 1)
            nc.scalar.activation(q_im[:], ang[:], ACT.Sin).then_inc(sin_done, 1)
            act.wait_ge(cos_arg, 1)
            nc.scalar.activation(q_re[:], tmp[0][:], ACT.Sin).then_inc(cos_done, 1)
            act.wait_ge(gate_abs, 1)
            nc.scalar.activation(sp_part[:], sp_part[:], ACT.Exp, scale=-1.0).then_inc(gate_exp, 1)
            act.wait_ge(gate_exp, 1)
            nc.scalar.activation(sp_part[:], sp_part[:], ACT.Ln, bias=G["ones_col"][0:HEADS, :]).then_inc(gate_ln, 1)

            def evacuate(n, b, it, func, dst, row, permuted):
                act.wait_ge(W.gemm_done, n + 1)
                act.wait_ge(z_stored, (n - 1) * 16)
                src = acc[b][:, :, 0:CH]
                if permuted:
                    nc.scalar.activation(
                        z_out.rearrange("p (k c j) -> p k c j", k=L, c=NC),
                        src.rearrange("p c (j k) -> p k c j", k=L), func).then_inc(evacuated[b], 1)
                else:
                    nc.scalar.activation(z_out.rearrange("p (c t) -> p c t", c=NC), src, func) \
                        .then_inc(evacuated[b], 1)
                act.wait_ge(evacuated[b], it + 1)
                act.dma_start(dst[bass.ds(row, P)], z_out[:]).then_inc(z_stored, 16)

            def copy_state(i):
                act.wait_ge(w_turned, i + 1)
                act.wait_ge(const_stored, i * (16 * (2 + L)))
                nc.scalar.copy(w_state_s.rearrange("p g m -> p (g m)"), bank_w[:]).then_inc(w_copied, 1)

            def copy_kernels(i):
                act.wait_ge(k_done, i + 1)
                nc.scalar.copy(kern[:, :, L - 1:, :].rearrange("p g k c -> p g (k c)"),
                               bank_c[0:GC, :].rearrange("p (g x) -> p g x", g=PB)).then_inc(k_copied, 1)

            act.wait_ge(lf_turned, 1)
            nc.scalar.copy(lf_rows[:, 0:TT].rearrange("p i h -> p (i h)"), bank_w[:, 0:TT * HEADS])
            nc.scalar.copy(lf_rows[0:T_SAMPLE, TT], bank_w[0:T_SAMPLE, TT * HEADS:(TT + 1) * HEADS]) \
                .then_inc(lf_copied, 1)
            act.wait_ge(negc_done, 1)
            evacuate(1, 1, 0, ACT.Copy, uT, 0, True)
            act.wait_ge(gate_stored, 64)
            copy_state(0)
            copy_kernels(0)
            evacuate(2, 0, 1, ACT.Copy, uT, P, True)

            def section(lo, hi, func, dst, row0, permuted):
                with act.Fori(lo, hi) as i:
                    copy_state(i)
                    evacuate(i * 2 + 1, 1, i, func, dst, i * (2 * P) - row0, permuted)
                    copy_kernels(i)
                    evacuate(i * 2 + 2, 0, i + 1, func, dst, i * (2 * P) + (P - row0), permuted)

            section(1, 4, ACT.Copy, uT, 0, True)
            section(4, 8, ACT.Silu, uT, 0, True)
            section(8, NPB, ACT.Copy, zT, 8 * 2 * P, False)

            def copy_v(q):
                for h, bank in enumerate((bank_c, bank_w)):
                    act.wait_ge(v_done, q + 1)
                    act.wait_ge(v_used, q)
                    nc.scalar.copy(v[:, 0, 2 * h:2 * h + 2], bank[:, 0:2 * NJ].rearrange("p (g j) -> p g j", g=2)) \
                        .then_inc(v_copied, 1)

            def gelu_y(q, b):
                for h, bank in enumerate((bank_c, bank_w)):
                    act.wait_ge(y_done, q + 1)
                    nc.scalar.activation(u_in[b][:, 2 * h:2 * h + 2],
                                         bank[:, 0:2 * NJ].rearrange("p (g j) -> p g j", g=2),
                                         ACT.Gelu_apprx_tanh).then_inc(y_copied, 1)

            def recur_tile(q, b, it, func, row, first=False):
                if not first:
                    gelu_y(q - 1, 1 - b)
                copy_v(q)
                evacuate(q + (2 * NPB + 1), 1 - b, it, func, zT, row, False)

            act.wait_ge(arena_free, 1)
            recur_tile(0, 0, NPB, ACT.Copy, 16 * P, True)
            recur_tile(1, 1, NPB + 1, ACT.Copy, 17 * P)
            for lo, hi, func in ((1, 4, ACT.Copy), (4, 8, ACT.Silu)):
                with act.Fori(lo, hi) as i:
                    recur_tile(i * 2, 0, i + NPB, func, i * (2 * P) + 16 * P)
                    recur_tile(i * 2 + 1, 1, i + (NPB + 1), func, i * (2 * P) + 17 * P)
            gelu_y(NPB - 1, 1)
            act.wait_ge(hl_turned, 1)
            nc.scalar.copy(h_rows[:], bank_c[0:GROUPS, 0:2 * P].rearrange("g (s p) -> g s p", s=2)) \
                .then_inc(hl_copied, 1)
            act.wait_ge(z_stored, 16 * tiles)

        @block.vector
        def _(dve):
            chain = Chain(dve, dve_order)
            link = chain.link
            TS, TT_, STT = nc.vector.tensor_scalar, nc.vector.tensor_tensor, nc.vector.scalar_tensor_tensor
            W.split_tile(dve, nc, 0, 0, False)
            W.split_tile(dve, nc, 1, 1, False)

            dve.wait_ge(raw_turned, 1)
            nc.vector.memset(kern[:, :, 0:L - 1, :], 0.0)
            for q, dst in enumerate((lam_re, lam_im, h0[:, 0], h0[:, 1])):
                last = nc.vector.tensor_copy(dst[:] if q < 2 else dst, bank_c[:, q * GROUPS:(q + 1) * GROUPS])
            link(last)
            dve.wait_ge(dt_done, 1)
            link(TT_(ang[:], lam_im[:], dt[:], ALU.mult))
            link(TT_(rate[:], lam_re[:], dt[:], ALU.mult))
            magic = 12582912.0
            link(TS(tmp[0][:], ang[:], 1.0 / (2 * math.pi), None, ALU.mult))
            link(TS(tmp[0][:], tmp[0][:], magic, None, ALU.add))
            link(TS(tmp[0][:], tmp[0][:], magic, None, ALU.subtract))
            hi2pi = 6.28125
            link(STT(ang[:], tmp[0][:], -hi2pi, ang[:], ALU.mult, ALU.add))
            link(STT(ang[:], tmp[0][:], -(2 * math.pi - hi2pi), ang[:], ALU.mult, ALU.add))
            pi_in = 3.1415925
            TS(ang[:], ang[:], pi_in, -pi_in, ALU.min, ALU.max).then_inc(arg_done, 1)
            dve.wait_ge(arg_done, 1)
            link(TS(tmp[1][:], ang[:], math.pi / 2, -2 * math.pi, ALU.is_gt, ALU.mult))
            link(STT(tmp[0][:], ang[:], math.pi / 2, tmp[1][:], ALU.add, ALU.add))
            TS(tmp[0][:], tmp[0][:], pi_in, -pi_in, ALU.min, ALU.max).then_inc(cos_arg, 1)
            dve.wait_ge(mag_done, 1)
            dve.wait_ge(sin_done, 1)
            dve.wait_ge(cos_done, 1)
            nc.vector.memset(pw_re[:, :, 0:1], 1.0)
            nc.vector.memset(pw_im[:, :, 0:1], 0.0)
            link(TT_(pw_re[:, :, 1], mag[:], q_re[:], ALU.mult))
            link(TT_(pw_im[:, :, 1], mag[:], q_im[:], ALU.mult))

            def power(n, m):
                ar, ai, br, bi = pw_re[:, :, n], pw_im[:, :, n], pw_re[:, :, m], pw_im[:, :, m]
                link(TT_(tmp[0][:], ar, br, ALU.mult))
                link(TT_(tmp[1][:], ai, bi, ALU.mult))
                link(TT_(pw_re[:, :, n + m], tmp[0][:], tmp[1][:], ALU.subtract))
                link(TT_(tmp[0][:], ar, bi, ALU.mult))
                link(TT_(tmp[1][:], ai, br, ALU.mult))
                link(TT_(pw_im[:, :, n + m], tmp[0][:], tmp[1][:], ALU.add))

            for n, m in ((1, 1), (2, 1), (2, 2), (4, 1), (4, 2), (4, 3), (4, 4)):
                power(n, m)
            dve.wait_ge(sgn_set, 1)
            link(TT_(rho[:], mag[:], mag[:], ALU.mult))
            link(TT_(rho[:], rho[:], rho[:], ALU.mult))
            link(TT_(rho[:], rho[:], rho[:], ALU.mult))
            link(TS(q_im[:], q_im[:], sgn[:, 0:1], None, ALU.mult))
            cr, ci = q_re[:], q_im[:]
            for n in range(3):
                link(TT_(tmp[0][:], cr, cr, ALU.mult))
                link(TT_(tmp[1][:], ci, ci, ALU.mult))
                link(TT_(tmp[2][:], cr, ci, ALU.mult))
                cr, ci = turn[:, 0], turn[:, 1]
                link(TT_(cr, tmp[0][:], tmp[1][:], ALU.subtract))
                link(TS(ci, tmp[2][:], 2.0, None, ALU.mult))
            for s in range(2):
                link(TT_(tmp[0][:], pw_re[:, :, L], h0[:, s], ALU.mult))
                link(TS(tmp[1][:], pw_im[:, :, L], sgn[:, s:s + 1], None, ALU.mult))
                link(TT_(tmp[1][:], tmp[1][:], h0[:, 1 - s], ALU.mult))
                link(TT_(carry[:, s], tmp[0][:], tmp[1][:], ALU.add))
            link(TT_(tmp[0][:], lam_re[:], lam_re[:], ALU.mult))
            link(TT_(tmp[1][:], lam_im[:], lam_im[:], ALU.mult))
            link(TT_(tmp[0][:], tmp[0][:], tmp[1][:], ALU.add))
            link(nc.vector.reciprocal(tmp[2][:], tmp[0][:]))
            link(TS(mag[:], pw_re[:, :, 1], 1.0, None, ALU.subtract))
            link(TT_(tmp[0][:], mag[:], lam_re[:], ALU.mult))
            link(TT_(tmp[1][:], pw_im[:, :, 1], lam_im[:], ALU.mult))
            link(TT_(tmp[0][:], tmp[0][:], tmp[1][:], ALU.add))
            link(TT_(q_re[:], tmp[0][:], tmp[2][:], ALU.mult))
            link(TT_(tmp[0][:], pw_im[:, :, 1], lam_re[:], ALU.mult))
            link(TT_(tmp[1][:], mag[:], lam_im[:], ALU.mult))
            link(TT_(tmp[0][:], tmp[0][:], tmp[1][:], ALU.subtract))
            link(TT_(q_im[:], tmp[0][:], tmp[2][:], ALU.mult))

            dve.wait_ge(W.gemm_done, 1)
            TS(lf.rearrange("h (c t) -> h c t", c=NC), acc[0][0:HEADS, :, 0:CH], b_f[:], None, ALU.add) \
                .then_inc(evacuated[0], 1)
            dve.wait_ge(evacuated[0], 1)
            STT(sp_part, lf, -1.0, lf, ALU.mult, ALU.max).then_inc(gate_abs, 1)
            dve.wait_ge(gate_ln, 1)
            link(TS(lf[:], lf[:], 0.0, None, ALU.min))
            link(TT_(lf[:], lf[:], sp_part[:], ALU.subtract))
            dve.wait_ge(past_turned, 1)
            TS(negs[:, T_PROMPT:T_PROMPT + T_PAST], bank_w[0:HEADS, :], -1.0, None, ALU.mult).then_inc(lf_done, 1)
            W.split_tile(dve, nc, 2, 0, True)
            dve.wait_ge(lf_done, 1)
            link(TS(negs[:, 0:T_PROMPT], lf[:, 0:T_PROMPT], -1.0, None, ALU.mult))
            link(TS(negs[:, T_PROMPT + T_PAST:], lf[:, T_PROMPT:], -1.0, None, ALU.mult))
            scan = nc.vector.tensor_tensor_scan
            ones = G["ones_col"][0:HEADS, :]
            link(scan(negs[:, 0:T_PROMPT], ones.to_broadcast([HEADS, T_PROMPT]), negs[:, 0:T_PROMPT], 0.0,
                      ALU.mult, ALU.add))
            link(scan(negs[:, T_PROMPT:], ones.to_broadcast([HEADS, T_PAST + T_SAMPLE]), negs[:, T_PROMPT:], 0.0,
                      ALU.mult, ALU.add))
            TS(negs[:], negs[:], math.sqrt(HD), None, ALU.mult).then_inc(negc_done, 1)

            def inputs(i):
                dve.wait_ge(b_loaded, i * 80 + 80)
                dve.wait_ge(k_done, i)
                qr = q_re[:, bass.ds(i * PB, PB)].unsqueeze(2).to_broadcast([P, PB, GC])
                qi = q_im[:, bass.ds(i * PB, PB)].unsqueeze(2).to_broadcast([P, PB, GC])
                link(TS(b_blk[:, 1], b_blk[:, 1], sgn[:, 0:1], None, ALU.mult))
                link(TT_(bt[:, 0], b_blk[:, 0], qr, ALU.mult))
                link(TT_(tmp_b, b_blk[:, 1], qi, ALU.mult))
                link(TT_(bt[:, 0], bt[:, 0], tmp_b, ALU.add))
                link(TT_(bt[:, 1], b_blk[:, 1], qr, ALU.mult))
                link(TT_(tmp_b, b_blk[:, 0], qi, ALU.mult))
                TT_(bt[:, 1], bt[:, 1], tmp_b, ALU.subtract).then_inc(b_used, 1)
                dve.wait_ge(b_used, i + 1)
                shape = [P, PB, L, GC]
                pr = pw_back[:, 0, bass.ds(i * PB, PB), :].unsqueeze(3).to_broadcast(shape)
                pi = pw_back[:, 1, bass.ds(i * PB, PB), :].unsqueeze(3).to_broadcast(shape)
                link(TT_(xin[:], bt[:, 0].unsqueeze(2).to_broadcast(shape), pr, ALU.mult))
                link(TT_(tmp_c[:, :, 0:L], bt[:, 1].unsqueeze(2).to_broadcast(shape), pi, ALU.mult))
                TT_(xin[:], xin[:], tmp_c[:, :, 0:L], ALU.add).then_inc(xin_done, 1)

            def outputs(i):
                dve.wait_ge(c_turned, i + 1)
                dve.wait_ge(const_stored, i * (16 * (2 + L)))
                dve.wait_ge(xin_done, i + 1)
                cs = bank_c[:, 0:2 * PB * GC].rearrange("p (q g c) -> p q g c", q=2, g=PB)
                link(TS(ct[:, 0], cs[:, 0], sgn[:, 1:2], None, ALU.mult))
                link(TS(ct[:, 1], cs[:, 1], -1.0, None, ALU.mult))
                shape = [P, PB, L + 1, GC]
                pr = pw_re[:, bass.ds(i * PB, PB), :].unsqueeze(3).to_broadcast(shape)
                pi = pw_im[:, bass.ds(i * PB, PB), :].unsqueeze(3).to_broadcast(shape)
                link(TT_(ca[:], ct[:, 0].unsqueeze(2).to_broadcast(shape), pr, ALU.mult))
                link(TT_(tmp_c[:], ct[:, 1].unsqueeze(2).to_broadcast(shape), pi, ALU.mult))
                TT_(ca[:], ca[:], tmp_c[:], ALU.add).then_inc(ca_done, 1)

            def skip(i):
                link(TT_(d_diag[:], d_bc.rearrange("p (g c) -> p g c", g=PB),
                         ident[0:GC, 0:GC].unsqueeze(1).to_broadcast([GC, PB, GC]), ALU.mult))
                dve.wait_ge(k_copied, i + 1)
                TT_(kern[:, :, L - 1], kern[:, :, L - 1], d_diag[:], ALU.add).then_inc(d_added, 1)

            dve.wait_ge(gate_stored, 64)
            for part, pw in enumerate((pw_re, pw_im)):
                for k in range(L):
                    last = nc.vector.tensor_copy(pw_back[:, part, :, k], pw[:, :, L - 1 - k])
            link(last)
            inputs(0)
            outputs(0)
            W.split_tile(dve, nc, 3, 1, True)
            skip(0)
            with dve.Fori(1, NPB) as i:
                chain.enter_loop(i - 1, 13)
                W.split_tile(dve, nc, i * 2 + 2, 0, True)
                inputs(i)
                outputs(i)
                W.split_tile(dve, nc, i * 2 + 3, 1, True)
                skip(i)
                chain.leave_loop(NPB - 1)

            def rotations(q):
                part = bass.ds(q * PB, PB)
                nc.vector.memset(rot[:, 0, :, 0:1], 1.0)
                nc.vector.memset(rot[:, 1, :, 0:1], 0.0)
                link(nc.vector.tensor_copy(rot[:, :, :, 1], turn[:, :, part]))
                m, half = 1, NJ // 2
                while m < NJ - 1:
                    n = min(m, NJ - 1 - m)
                    er, ei = (rot[:, s, :, m:m + 1].to_broadcast([P, PB, n]) for s in range(2))
                    br, bi = rot[:, 0, :, 1:1 + n], rot[:, 1, :, 1:1 + n]
                    rr, ii, ri, ir = va[:, :, 0:n], vb[:, :, 0:n], va[:, :, half:half + n], vb[:, :, half:half + n]
                    TT_(rr, er, br, ALU.mult)
                    TT_(ii, ei, bi, ALU.mult)
                    TT_(ri, er, bi, ALU.mult)
                    link(TT_(ir, ei, br, ALU.mult))
                    TT_(rot[:, 0, :, m + 1:m + 1 + n], rr, ii, ALU.subtract)
                    link(TT_(rot[:, 1, :, m + 1:m + 1 + n], ri, ir, ALU.add))
                    m *= 2

            def recur(q):
                part = bass.ds(q * PB, PB)
                dve.wait_ge(v_copied, q * 2 + 2)
                dve.wait_ge(v_swapped, q * 32 + 32)
                link(TT_(v[:, :, :, NJP], v[:, :, :, NJP], carry[:, :, part], ALU.add))
                TT_(va[:], rot[:, 0], v[:, 0], ALU.mult)
                link(TT_(vb[:], rot[:, 1], v[:, 1], ALU.mult))
                TT_(va[:], va[:], vb[:], ALU.subtract)
                TT_(v[:, 0], rot[:, 1], v[:, 0], ALU.mult)
                link(TT_(v[:, 1], rot[:, 0], v[:, 1], ALU.mult))
                link(TT_(vb[:], v[:, 0], v[:, 1], ALU.add))
                for src, dst in ((va, v[:, 0]), (vb, v[:, 1])):
                    for g in range(PB):
                        for lo, hi in ((0, NJP), (NJP, NJ)):
                            last = nc.vector.tensor_tensor_scan(
                                dst[:, g, lo:hi], rho[:, bass.ds(q * PB + g, 1)].to_broadcast([P, hi - lo]),
                                src[:, g, lo:hi], 0.0, ALU.mult, ALU.add)
                link(last)
                TT_(va[:], rot[:, 0], v[:, 0], ALU.mult)
                TT_(vb[:], rot[:, 1], v[:, 1], ALU.mult).then_inc(v_used, 1)
                dve.wait_ge(v_used, q + 1)
                dve.wait_ge(y_done, q)
                link(TT_(h_prev[:, :, 1:], va[:], vb[:], ALU.add))
                nc.vector.tensor_copy(h_last[:, 0, part], h_prev[:, :, NJP])
                link(nc.vector.tensor_copy(h_last[:, 1, part], h_prev[:, :, NJ]))
                nc.vector.tensor_copy(h_prev[:, :, NJP], h0[:, 0, part]).then_inc(h_ready, 1)

            levels = len([m for m in range(9) if 2 ** m < NJ - 1])
            steps = 1 + 2 * levels + 7
            n0 = 2 * NPB + 1
            W.split_tile(dve, nc, n0 + 1, 0, True)
            dve.wait_ge(arena_free, 1)
            rotations(0)
            recur(0)
            W.split_tile(dve, nc, n0 + 2, 1, True)
            rotations(1)
            recur(1)
            with dve.Fori(1, NPB // 2 - 1) as i:
                chain.enter_loop(i - 1, 2 * steps)
                for b in range(2):
                    W.split_tile(dve, nc, i * 2 + (n0 + 1 + b), b, True)
                    rotations(i * 2 + b)
                    recur(i * 2 + b)
                chain.leave_loop(NPB // 2 - 2)
            W.split_tile(dve, nc, tiles, 0, True)
            rotations(NPB - 2)
            recur(NPB - 2)
            rotations(NPB - 1)
            recur(NPB - 1)
            dve.wait_ge(h_ready, NPB)
            nc.vector.tensor_copy(va[:, 0, 0:1], h_last[:, 0, 0:1]).then_inc(hl_ready, 1)



def stage_attention(nc, d, G):
    SCALE = HD ** -0.5
    NS = T_PAST + T_SAMPLE
    SLOTS = [[(0, 0), (1, 512)]] + [[(t, 0)] for t in range(2, TT)] + [[(TT, 0)]]
    GROUPS_OF = [[[(0, 0, 0, 1), (1, 512, 0, 2)]], [[(2, 0, 0, 3)]], [[(3, 0, 0, 4)]]] + \
        [[[(t, 0, 0, 4)], [(t, 0, 4, t - 3)]] for t in range(4, TT)] + [[[(TT, 0, 0, 5)]]]
    first_group = [sum(len(g) for g in GROUPS_OF[:s]) for s in range(9)]
    per_head = first_group[8]
    assert per_head % 2 == 0
    NB = T_PAST // P
    with ExitStack() as ctx:
        sb, ps, sem = allocators(nc, ctx)
        ident, ident_bf = G["ident"], sb("ident_bf", [P, P], BF16)
        mask_f, mask_s_f = sb("mask_f", [P, P]), sb("mask_s_f", [P, T_SAMPLE])
        mask, mask_s = sb("mask", [P, P], BF16), sb("mask_s", [P, T_SAMPLE], BF16)
        q_raw, k_raw, v_raw = (sb(n, [P, T]) for n in ("q_raw", "k_raw", "v_raw"))
        kc_raw, vc_raw = (sb(n, [P, NB, HD]) for n in ("kc_raw", "vc_raw"))
        k_tok, v_tok = (sb(n, [P, TT + 1, HD]) for n in ("k_tok", "v_tok"))

        def pair(name, shape, dt=F32R):
            return [sb(f"{name}{b}", shape, dt) for b in range(2)]

        q_hi, q_lo, k_hi, k_lo = (pair(n, [P, T]) for n in ("q_hi", "q_lo", "k_hi", "k_lo"))
        v_hi, v_lo = (pair(n, [P, TT + 1, HD]) for n in ("v_hi", "v_lo"))
        kc_hi, kc_lo = (pair(n, [P, T_PAST]) for n in ("kc_hi", "kc_lo"))
        vc_hi, vc_lo = (pair(n, [P, NB, HD]) for n in ("vc_hi", "vc_lo"))
        negc = pair("negc_bc", [P, T_PROMPT + NS], F32)
        gate = pair("gate", [P, T], F32)
        prob = [sb(f"prob{n}", [P, 1024]) for n in range(4)]
        stat = pair("stat", [P, 2, 4], F32)
        pt_hi = [sb(f"pt_hi{x}", [P, n, w], F32R) for x, n, w in ((0, 4, 512), (1, 8, 512), (2, 5, T_SAMPLE))]
        pt_lo = [sb(f"pt_lo{x}", [P, n, w], F32R) for x, n, w in ((0, 4, 512), (1, 8, 512), (2, 5, T_SAMPLE))]
        mix = sb("mix", [P, T])
        score = [ps(f"score{b}", [P, 1024]) for b in range(2)]
        turned = [ps(f"turned{b}", [P, 512]) for b in range(2)]
        att, prep = ps("att", [P, 512]), ps("prep", [P, 512])

        masks_made, masks_ready, zero_pt = sem("masks_made"), sem("masks_ready"), sem("zero_pt")
        q_loaded, k_loaded, v_loaded, c_loaded = (sem(n + "_loaded") for n in ("q", "k", "v", "c"))
        gate_loaded, negc_loaded = ([sem(f"{n}_loaded{b}") for b in range(2)] for n in ("gate", "negc"))
        q_hi_done, k_hi_done, kc_hi_done, q_lo_done, k_lo_done, kc_lo_done, v_hi_done, v_lo_done, vc_hi_done, \
            vc_lo_done = (sem(n) for n in ("q_hi_done", "k_hi_done", "kc_hi_done", "q_lo_done", "k_lo_done",
                                           "kc_lo_done", "v_hi_done", "v_lo_done", "vc_hi_done", "vc_lo_done"))
        k_turned, v_turned, kc_turned, k_copied, v_copied = (
            sem(n) for n in ("k_turned", "v_turned", "kc_turned", "k_copied", "v_copied"))
        k_stored, v_stored, mix_stored = (G["sem"][n] for n in ("k_stored", "v_stored", "mix_stored"))
        scored = [sem(f"scored{b}") for b in range(2)]
        biased = [sem(f"biased{b}") for b in range(2)]
        negmax, exped, summed, normed = (
            [sem(f"{n}{b}") for b in range(2)] for n in ("negmax", "exped", "summed", "normed"))
        p_turned = [sem(f"p_turned{b}") for b in range(2)]
        prob_free = [sem(f"prob_free{b}") for b in range(2)]
        hi_done, lo_done = ([sem(f"pt_{n}_done{b}") for b in range(2)] for n in ("hi", "lo"))
        weighed = [sem(f"weighed{x}") for x in range(3)]
        gated = sem("gated")
        block = ctx.enter_context(nc.Block())
        zT = d["zT"]
        k_cache, v_cache = (d[n][0, 0].rearrange("(i p) h c -> p i h c", p=P) for n in ("cache_k", "cache_v"))

        def taken(group, dst, bank):
            at = 0
            for t, col, j0, nj in group:
                if t < TT:
                    c = t % 4 * P
                    yield dst[:, j0:j0 + nj, c:c + P], \
                        bank[:, at:at + nj * P].rearrange("p (j t) -> p j t", j=nj)
                    at += nj * P
                else:
                    yield dst[:, 0:NB], bank[:, 0:NB * T_SAMPLE].rearrange("p (j t) -> p j t", j=NB)
                    yield dst[0:T_SAMPLE, NB], bank[0:T_SAMPLE, NB * T_SAMPLE:(NB + 1) * T_SAMPLE]

        def heads(eng, head):
            head(0, 0, 0, first=True)
            head(1, 1, 0)
            with eng.Fori(1, HEADS // 2 - 1) as i:
                head(i * 2, 0, i)
                head(i * 2 + 1, 1, i)
            head(HEADS - 2, 0, HEADS // 2 - 1)
            head(HEADS - 1, 1, HEADS // 2 - 1, last=True)

        @block.sync
        def _(sp):
            def load(h, b, it, first=False):
                if not first:
                    sp.wait_ge(k_hi_done, h)
                    sp.wait_ge(k_lo_done, h)
                    settle(sp, G["passed"])
                    sp.wait_ge(k_turned, h * 3)
                sp.dma_start(k_raw[:], zT[bass.ds(h * P + D_ATT, P)]).then_inc(k_loaded, 16)
                if not first:
                    sp.wait_ge(q_hi_done, h)
                    sp.wait_ge(q_lo_done, h)
                sp.dma_start(q_raw[:], zT[bass.ds(h * P, P)]).then_inc(q_loaded, 16)
                if not first:
                    sp.wait_ge(biased[0], (h - 1) * 4)
                    sp.wait_ge(biased[1], (h - 1) * 4)
                sp.dma_start(negc[b][:], d["negc"][bass.ds(h, 1)].to_broadcast([P, T_PROMPT + NS])) \
                    .then_inc(negc_loaded[b], 16)
                if not first:
                    sp.wait_ge(v_turned, h * 3)
                sp.dma_start(v_raw[:], zT[bass.ds(h * P + 2 * D_ATT, P)]).then_inc(v_loaded, 16)
                if not first:
                    sp.wait_ge(kc_turned, h)
                    sp.wait_ge(vc_hi_done, h)
                    sp.wait_ge(vc_lo_done, h)
                    settle(sp, G["passed"])
                sp.dma_start(kc_raw[:], k_cache[:, :, bass.ds(h, 1)].rearrange("p i h c -> p i (h c)")) \
                    .then_inc(c_loaded, 16)
                sp.dma_start(vc_raw[:], v_cache[:, :, bass.ds(h, 1)].rearrange("p i h c -> p i (h c)")) \
                    .then_inc(c_loaded, 16)
                if not first:
                    sp.wait_ge(gated, (h - 1) * 3)
                sp.dma_start(gate[b][:], zT[bass.ds(h * P + 3 * D_ATT, P)]).then_inc(gate_loaded[b], 16)

            load(0, 0, 0, first=True)

            def head(h, b, i, first=False, last=False):
                if not last:
                    load(h + 1, 1 - b, i)
            heads(sp, head)

        @block.gpsimd
        def _(pool):
            nc.gpsimd.memset(mask_f[:], 0.0)
            nc.gpsimd.memset(mask_s_f[:], 0.0).then_inc(masks_made, 1)
            pool.wait_ge(masks_made, 1)
            nc.gpsimd.affine_select(out=mask_f[:], in_=mask_f[:], compare_op=ALU.is_ge, fill=NEG, base=0,
                                    pattern=[[-1, P]], channel_multiplier=1).then_inc(masks_made, 1)
            pool.wait_ge(masks_made, 2)
            r0 = P - T_SAMPLE
            nc.gpsimd.affine_select(out=mask_s_f[r0:], in_=mask_s_f[r0:], compare_op=ALU.is_ge, fill=NEG,
                                    base=0, pattern=[[-1, T_SAMPLE]], channel_multiplier=1) \
                .then_inc(masks_made, 1)
            pool.wait_ge(masks_made, 3)
            nc.gpsimd.memset(v_tok[:, TT], 0.0)
            nc.gpsimd.tensor_copy(mask[:], mask_f[:])
            nc.gpsimd.tensor_copy(mask_s[:], mask_s_f[:])
            nc.gpsimd.tensor_copy(ident_bf[:], ident[:]).then_inc(masks_ready, 1)

            def sub(out, a, hi, done):
                nc.gpsimd.tensor_tensor(out, a, hi.bitcast(F32), ALU.subtract).then_inc(done, 1)

            def store_mix(h):
                pool.wait_ge(gated, h * 3 + 3)
                pool.dma_start(d["mixT"][bass.ds(h * P, P)], mix[:]).then_inc(mix_stored, 16)

            def prepare(h, b, mix_of=None):
                pool.wait_ge(k_hi_done, h + 1)
                sub(k_lo[b][:], k_raw[:], k_hi[b][:], k_lo_done)
                pool.wait_ge(q_hi_done, h + 1)
                sub(q_lo[b][:], q_raw[:], q_hi[b][:], q_lo_done)
                pool.wait_ge(c_loaded, h * 32 + 32)
                settle(pool, G["passed"])
                nc.gpsimd.tensor_copy(vc_hi[b][:], vc_raw[:]).then_inc(vc_hi_done, 1)
                pool.wait_ge(vc_hi_done, h + 1)
                sub(vc_lo[b][:], vc_raw[:], vc_hi[b][:], vc_lo_done)
                pool.wait_ge(k_copied, h * 3 + 3)
                for tok, src, stored in (("k", k_tok, k_stored), ("v", v_tok, v_stored)):
                    if tok == "v":
                        if mix_of is not None:
                            store_mix(mix_of)
                        pool.wait_ge(v_copied, h * 3 + 3)
                        settle(pool, G["passed"])
                        nc.gpsimd.tensor_copy(v_hi[b][:], v_tok[:]).then_inc(v_hi_done, 1)
                        pool.wait_ge(v_hi_done, h + 1)
                        sub(v_lo[b][:], v_tok[:], v_hi[b][:], v_lo_done)
                    pool.dma_start(d[tok + "_prompt"][0, 0].rearrange("(i p) h c -> p i h c", p=P)
                                   [:, :, bass.ds(h, 1)].rearrange("p i h c -> p i (h c)"), src[:, 0:TT]) \
                        .then_inc(stored, 16)
                    pool.dma_start(d[tok + "_sample"][0, 0][:, bass.ds(h, 1)].rearrange("t h c -> t (h c)"),
                                   src[0:T_SAMPLE, TT]).then_inc(stored, 16)

            prepare(0, 0)

            def head(h, b, i, first=False, last=False):
                if not first:
                    pool.wait_ge(weighed[2], h)
                if not last:
                    prepare(h + 1, 1 - b, None if first else h - 1)
                elif not first:
                    store_mix(h - 1)
            heads(pool, head)
            store_mix(HEADS - 1)
            pool.wait_ge(mix_stored, 16 * HEADS)
            pool.wait_ge(k_stored, 32 * HEADS)
            pool.wait_ge(v_stored, 32 * HEADS)

        @block.tensor
        def _(pe):
            def three(out, pairs, start, stop, lhs, rhs):
                for n, (x, y) in enumerate(((0, 0), (0, 1), (1, 0))):
                    mm = pe.matmul(out, lhs[x], rhs[y], start=(start and n == 0), stop=(stop and n == 2))
                return mm

            def turn(h, m):
                if m < 6:
                    src, loaded, done = (k_raw, k_loaded, k_turned) if m < 3 else (v_raw, v_loaded, v_turned)
                    if m == 0:
                        pe.wait_ge(kc_lo_done, h)
                    elif m <= 3:
                        pe.wait_ge(k_copied, h * 3 + m)
                    else:
                        pe.wait_ge(v_copied, h * 3 + (m - 3))
                    pe.wait_ge(loaded, h * 16 + 16)
                    for q in range(4 if m % 3 < 2 else 1):
                        t = m % 3 * 4 + q
                        rows = P if t < TT else T_SAMPLE
                        tr = pe.transpose(prep[0:rows, q * P:(q + 1) * P], src[:, t * P:t * P + rows], ident[:])
                    tr.then_inc(done, 1)
                else:
                    pe.wait_ge(v_copied, h * 3 + 3)
                    pe.wait_ge(c_loaded, h * 32 + 32)
                    for q in range(NB):
                        tr = pe.transpose(prep[:, q * P:(q + 1) * P], kc_raw[:, q], ident[:])
                    tr.then_inc(kc_turned, 1)

            def scores(h, b, it, s, hb):
                pe.wait_ge(biased[b], it)
                if s == 0:
                    pe.wait_ge(q_lo_done, h + 1)
                    pe.wait_ge(k_lo_done, h + 1)
                if s == 7:
                    pe.wait_ge(kc_lo_done, h + 1)
                    q = [x[hb][:, T - P:T] for x in (q_hi, q_lo)]
                    three(score[b][:, 0:T_PAST], 0, True, True, q, [x[hb][:] for x in (kc_hi, kc_lo)])
                    out = score[b][:, T_PAST:NS]
                    three(out, 0, True, False, q, [x[hb][:, T_PROMPT:T] for x in (k_hi, k_lo)])
                    mm = pe.matmul(out, ident_bf[:], mask_s[:], start=False, stop=True)
                else:
                    for t, col in SLOTS[s]:
                        q = [x[hb][:, t * P:(t + 1) * P] for x in (q_hi, q_lo)]
                        for lo in range(0, (t + 1) * P, 512):
                            hi = min(lo + 512, (t + 1) * P)
                            final = hi == (t + 1) * P
                            three(score[b][:, col + lo:col + hi], 0, True, not final, q,
                                  [x[hb][:, lo:hi] for x in (k_hi, k_lo)])
                        mm = pe.matmul(score[b][:, col + t * P:col + (t + 1) * P], ident_bf[:], mask[:],
                                       start=False, stop=True)
                mm.then_inc(scored[b], 1)

            def turn_probs(h, s):
                b = s % 2
                pe.wait_ge(normed[b], h * 4 + (s // 2 + 1))
                for n, group in enumerate(GROUPS_OF[s]):
                    gi = first_group[s] + n
                    bank = turned[gi % 2]
                    pe.wait_ge(lo_done[gi % 2], h * (per_head // 2) + gi // 2)
                    if group[0][0] == TT:
                        settle(pe, G["passed"])
                    at = 0
                    for t, col, j0, nj in group:
                        for j in range(j0, j0 + nj):
                            if t < TT:
                                tr = pe.transpose(bank[:, at:at + P], prob[s % 4][:, col + j * P:col + (j + 1) * P],
                                                  ident[:])
                                at += P
                            else:
                                rows, r0 = (P if j < NB else T_SAMPLE), P - T_SAMPLE
                                tr = pe.transpose(bank[0:rows, at:at + T_SAMPLE],
                                                  prob[s % 4][r0:P, j * P:j * P + rows], ident[r0:P, r0:P])
                                at += T_SAMPLE
                    tr.then_inc(p_turned[gi % 2], 1)
                pe.nop().then_inc(prob_free[b], 1)

            def weigh(h, x, hb, half=None):
                if half != 1:
                    gi = first_group[(3, 7, 8)[x]] - 1
                    for q in (gi - 1, gi):
                        pe.wait_ge(lo_done[q % 2], h * (per_head // 2) + (q // 2 + 1))
                    pe.wait_ge(gated, h * 3 + x)
                if x == 0:
                    pe.wait_ge(v_lo_done, h + 1)
                if x < 2:
                    for j in range(4 * x + 4) if half is None else range(4 * half, 4 * half + 4):
                        lo = max(0, j - 4 * x) * P
                        mm = three(att[:, lo:512], 0, j == 0, j == 4 * x + 3,
                                   [v[hb][:, j] for v in (v_hi, v_lo)], [p[x][:, j, lo:512] for p in (pt_hi, pt_lo)])
                else:
                    for j in range(NB):
                        three(att[:, 0:T_SAMPLE], 0, j == 0, False, [v[hb][:, j] for v in (vc_hi, vc_lo)],
                              [p[x][:, j] for p in (pt_hi, pt_lo)])
                    mm = three(att[:, 0:T_SAMPLE], 0, False, True,
                               [v[hb][0:T_SAMPLE, TT] for v in (v_hi, v_lo)],
                               [p[x][0:T_SAMPLE, NB] for p in (pt_hi, pt_lo)])
                if half != 0:
                    mm.then_inc(weighed[x], 1)

            pe.wait_ge(masks_ready, 1)
            for m in range(7):
                turn(0, m)
            scores(0, 0, 0, 0, 0)
            scores(0, 1, 0, 1, 0)

            def head(h, hb, i, first=False, last=False):
                for s in range(8):
                    if s < 6:
                        scores(h, s % 2, h * 4 + (s // 2 + 1), s + 2, hb)
                    elif not last:
                        scores(h + 1, s % 2, h * 4 + (s // 2 + 1), s - 6, 1 - hb)
                    if s < 7 and not last:
                        turn(h + 1, s)
                    turn_probs(h, s)
                    if s == 0 and not first:
                        weigh(h - 1, 1, 1 - hb, 1)
                    if s == 1 and not first:
                        weigh(h - 1, 2, 1 - hb)
                    if s == 5:
                        weigh(h, 0, hb)
                    if s == 7:
                        weigh(h, 1, hb, 0)
            heads(pe, head)
            weigh(HEADS - 1, 1, 1, 1)
            weigh(HEADS - 1, 2, 1)

        @block.scalar
        def _(act):
            def split_qk(h, b, which, first=False):
                hi, raw, loaded, done = ((k_hi, k_raw, k_loaded, k_hi_done),
                                         (q_hi, q_raw, q_loaded, q_hi_done))[which]
                act.wait_ge(loaded, h * 16 + 16)
                if not first:
                    act.wait_ge(scored[0], (h - 1) * 4)
                    act.wait_ge(scored[1], (h - 1) * 4)
                nc.scalar.copy(hi[b][:], raw[:]).then_inc(done, 1)

            def copy_k(h, m):
                act.wait_ge(k_turned, h * 3 + (m + 1))
                act.wait_ge(k_stored, h * 32)
                if m < 2:
                    nc.scalar.copy(k_tok[:, 4 * m:4 * m + 4].rearrange("p i c -> p (i c)"), prep[:]) \
                        .then_inc(k_copied, 1)
                else:
                    nc.scalar.copy(k_tok[0:T_SAMPLE, TT], prep[0:T_SAMPLE, 0:P]).then_inc(k_copied, 1)

            def split_kc(h, b):
                act.wait_ge(kc_turned, h + 1)
                nc.scalar.copy(kc_hi[b][:], prep[:]).then_inc(kc_hi_done, 1)

            def exponentials(h, s):
                b, it = s % 2, h * 4 + s // 2
                act.wait_ge(negmax[b], it + 1)
                for n, (t, col) in enumerate(SLOTS[s]):
                    width = (t + 1) * P if t < TT else NS
                    e = nc.scalar.activation(prob[s % 4][:, col:col + width], prob[s % 4][:, col:col + width], ACT.Exp,
                                             scale=SCALE, bias=stat[b][:, n, 1:2], accum_out=stat[b][:, n, 2:3])
                e.then_inc(exped[b], 1)

            def high_parts(h, s):
                for n, group in enumerate(GROUPS_OF[s]):
                    gi = first_group[s] + n
                    bank, x = turned[gi % 2], (0 if s < 3 else 1 if s < 7 else 2)
                    act.wait_ge(p_turned[gi % 2], h * (per_head // 2) + (gi // 2 + 1))
                    act.wait_ge(weighed[x], h)
                    for out, src in taken(group, pt_hi[x], bank):
                        c = nc.scalar.copy(out, src)
                    c.then_inc(hi_done[gi % 2], 1)

            split_qk(0, 0, 0, True)
            split_qk(0, 0, 1, True)
            for m in range(3):
                copy_k(0, m)
            split_kc(0, 0)
            exponentials(0, 0)

            def head(h, hb, i, first=False, last=False):
                for s in range(8):
                    if s < 7:
                        exponentials(h, s + 1)
                    elif not last:
                        exponentials(h + 1, 0)
                    high_parts(h, s)
                    if last:
                        continue
                    if s < 2:
                        split_qk(h + 1, 1 - hb, s)
                    if s < 3:
                        copy_k(h + 1, s)
                    if s == 6:
                        split_kc(h + 1, 1 - hb)
            heads(act, head)

        @block.vector
        def _(dve):
            def copy_v(h, m):
                dve.wait_ge(v_turned, h * 3 + (m + 1))
                dve.wait_ge(v_stored, h * 32)
                dve.wait_ge(v_lo_done, h)
                if m < 2:
                    nc.vector.tensor_copy(v_tok[:, 4 * m:4 * m + 4].rearrange("p i c -> p (i c)"), prep[:]) \
                        .then_inc(v_copied, 1)
                else:
                    nc.vector.tensor_copy(v_tok[0:T_SAMPLE, TT], prep[0:T_SAMPLE, 0:P]).then_inc(v_copied, 1)

            def low_kc(h, b):
                dve.wait_ge(kc_hi_done, h + 1)
                nc.vector.tensor_tensor(kc_lo[b][:], prep[:], kc_hi[b][:].bitcast(F32), ALU.subtract) \
                    .then_inc(kc_lo_done, 1)

            def bias(h, s, hb, pair):
                b, it = s % 2, h * 4 + s // 2
                dve.wait_ge(scored[b], it + 1)
                if not isinstance(h, int) or it > 1:
                    dve.wait_ge(prob_free[b], h * 4 + (s // 2 - 1))
                if s == 0:
                    dve.wait_ge(negc_loaded[hb], pair * 16 + 16)
                settle(dve, G["passed"])
                for n, (t, col) in enumerate(SLOTS[s]):
                    width, row = ((t + 1) * P, 0) if t < TT else (NS, T_PROMPT)
                    z = nc.vector.tensor_tensor_reduce(
                        out=prob[s % 4][:, col:col + width], in0=score[b][:, col:col + width],
                        in1=negc[hb][:, row:row + width], scale=1.0, scalar=-3.0e38, op0=ALU.add, op1=ALU.max,
                        accum_out=stat[b][:, n, 0:1])
                z.then_inc(biased[b], 1)
                dve.wait_ge(biased[b], it + 1)
                nt = len(SLOTS[s])
                nc.vector.tensor_scalar(stat[b][:, 0:nt, 1], stat[b][:, 0:nt, 0], -SCALE, None, ALU.mult) \
                    .then_inc(negmax[b], 1)

            def normalize(h, s):
                b, it = s % 2, h * 4 + s // 2
                dve.wait_ge(exped[b], it + 1)
                nt = len(SLOTS[s])
                nc.vector.reciprocal(stat[b][:, 0:nt, 3], stat[b][:, 0:nt, 2]).then_inc(summed[b], 1)
                dve.wait_ge(summed[b], it + 1)
                for n, (t, col) in enumerate(SLOTS[s]):
                    width = (t + 1) * P if t < TT else NS
                    p = nc.vector.tensor_scalar(prob[s % 4][:, col:col + width], prob[s % 4][:, col:col + width],
                                                stat[b][:, n, 3:4], None, ALU.mult)
                p.then_inc(normed[b], 1)

            def low_parts(h, s):
                for n, group in enumerate(GROUPS_OF[s]):
                    gi = first_group[s] + n
                    bank, x = turned[gi % 2], (0 if s < 3 else 1 if s < 7 else 2)
                    dve.wait_ge(hi_done[gi % 2], h * (per_head // 2) + (gi // 2 + 1))
                    for (out, src), (hi, _) in zip(taken(group, pt_lo[x], bank), taken(group, pt_hi[x], bank)):
                        c = nc.vector.tensor_tensor(out, src, hi.bitcast(F32), ALU.subtract)
                    c.then_inc(lo_done[gi % 2], 1)

            def gate_out(h, x, hb, pair=None):
                cols = slice(512 * x, 512 * x + (512 if x < 2 else T_SAMPLE))
                dve.wait_ge(weighed[x], h + 1)
                if x == 0:
                    dve.wait_ge(mix_stored, h * 16)
                    dve.wait_ge(gate_loaded[hb], pair * 16 + 16)
                nc.vector.tensor_tensor(mix[:, cols], att[:, 0:cols.stop - cols.start], gate[hb][:, cols],
                                        ALU.mult).then_inc(gated, 1)

            dve.wait_ge(masks_ready, 1)
            for m in range(3):
                copy_v(0, m)
            low_kc(0, 0)
            bias(0, 0, 0, 0)

            def head(h, hb, i, first=False, last=False):
                for s in range(8):
                    if s < 7:
                        bias(h, s + 1, hb, i)
                    elif not last:
                        bias(h + 1, 0, 1 - hb, i + hb)
                    normalize(h, s)
                    if s > 0:
                        low_parts(h, s - 1)
                    elif not first:
                        low_parts(h - 1, 7)
                    if s == 1 and not first:
                        gate_out(h - 1, 1, 1 - hb)
                    if s == 2 and not first:
                        gate_out(h - 1, 2, 1 - hb)
                    if not last and 3 <= s < 6:
                        copy_v(h + 1, s - 3)
                    if not last and s == 7:
                        low_kc(h + 1, 1 - hb)
                    if s == 6:
                        gate_out(h, 0, hb, i)
            heads(dve, head)
            low_parts(HEADS - 1, 7)
            gate_out(HEADS - 1, 1, 1)
            gate_out(HEADS - 1, 2, 1)



def stage_side(nc, d, G):
    with ExitStack() as ctx:
        sb, ps, sem = allocators(nc, ctx)
        ident = G["ident"]
        WE = Weights(sb, sem, "w_pe_s", KP)
        WG = Weights(sb, sem, "w_glu_s", KS)
        p_in = sb("p_in", [P, TT + 1, D_PLE])
        p_hi, p_lo = (sb(n, [P, KP, T], F32R) for n in ("p_hi", "p_lo"))
        e_out = [sb(f"e_out{b}", [P, T]) for b in range(2)]
        e_sq = [sb(f"e_sq{b}", [P, T]) for b in range(2)]
        e_sum = sb("e_sum", [P, T])
        ones = sb("ones_sq", [P, P])
        y_raw = sb("y_raw", [P, KS, T])
        y_hi, y_lo = (sb(n, [P, KS, T], F32R) for n in ("y_hi", "y_lo"))
        sig = [sb(f"sig{b}", [P, T]) for b in range(2)]
        gs = [sb(f"gs{b}", [P, T]) for b in range(2)]
        out = [sb(f"mix_out{b}", [P, T]) for b in range(2)]
        acc = [ps(f"side_acc{b}", [P, NC, 512]) for b in range(2)]
        p_ps = [ps(f"p_ps{b}", [P, 512]) for b in range(2)]
        p_loaded, p_tail_loaded = sem("p_loaded"), sem("p_tail_loaded")
        gs_loaded, y_loaded = [G["sem"][f"gs_loaded{b}"] for b in range(2)], G["sem"]["y_loaded"]
        y_hi_done, y_split = sem("y_hi_done"), sem("y_split")
        p_turned, p_hi_done, p_lo_done, ones_set = (
            sem(n) for n in ("p_turned", "p_hi_done", "p_lo_done", "ones_set"))
        evacuated = [sem(f"side_evacuated{b}") for b in range(2)]
        e_stored = [sem(f"e_stored{b}") for b in range(2)]
        norm_ready, norm_std, dve_order = (sem(n) for n in ("e_norm_ready", "e_norm_std", "side_order"))
        summed = [sem(f"e_summed{b}") for b in range(2)]
        sig_done, gated_done, mix_stored = ([sem(f"{n}{b}") for b in range(2)]
                                            for n in ("sig_done", "gated_done", "glu_stored"))
        block = ctx.enter_context(nc.Block())
        w_pe = d["w_pe"][0].rearrange("(k p) n -> p k n", p=P)
        w_glu = d["w_glu"][0].rearrange("(k p) n -> p k n", p=P)
        p_rows = d["p_prompt"][0, 0].rearrange("(i p) c -> p i c", p=P)
        yT = d["yT"].rearrange("r k j -> r (k j)")
        uT = d["uT"].rearrange("r k j -> r (k j)")

        @block.sync
        def _(sp):
            sp.dma_start(p_in[:, 0:TT], p_rows).then_inc(p_loaded, 16)
            WE.load(sp, w_pe, 0, 0)
            sp.dma_start(p_in[0:T_SAMPLE, TT], d["p_sample"][0, 0]).then_inc(p_tail_loaded, 16)
            with sp.Fori(1, KD) as m:
                WE.load(sp, w_pe, m * P, m)
            with sp.Fori(0, KS) as m:
                WG.load(sp, w_glu, m * P, m)

        @block.gpsimd
        def _(pool):
            nc.gpsimd.memset(ones[:], 1.0).then_inc(ones_set, 1)
            pool.wait_ge(p_loaded, 16)
            pool.dma_start(y_raw[:], yT.rearrange("(k p) t -> p k t", p=P)).then_inc(y_loaded, 16)
            with pool.Fori(0, KS // 2) as i:
                for b in range(2):
                    pool.wait_ge(gated_done[b], i)
                    pool.dma_start(gs[b][:], uT[bass.ds(i * (2 * P) + (D_SSM + b * P), P)]) \
                        .then_inc(gs_loaded[b], 16)

        @block.tensor
        def _(pe):
            for n in range(TT + 1):
                b, rows = n % 2, (P if n < TT else T_SAMPLE)
                if n in (0, TT):
                    pe.wait_ge(p_tail_loaded if n else p_loaded, 16)
                if n >= 2:
                    pe.wait_ge(p_lo_done, n - 1)
                for k in range(KP):
                    tr = pe.transpose(p_ps[b][:, k * P:k * P + rows], p_in[0:rows, n, k * P:(k + 1) * P],
                                      ident[0:rows, 0:rows])
                tr.then_inc(p_turned, 1)
            pe.wait_ge(p_lo_done, TT + 1)
            with pe.Fori(0, KD // 2) as i:
                for b in range(2):
                    pe.wait_ge(WE.split[1], i * 2 + (b + 1))
                    pe.wait_ge(evacuated[b], i)
                    gemm_tile(pe, acc[b], WE.hi[b], WE.lo[b], p_hi, p_lo, KP).then_inc(WE.gemm_done, 1)

            def glu_tile(m, b, it):
                pe.wait_ge(WG.split[1], m + 1)
                pe.wait_ge(evacuated[b], it + KD // 2)
                gemm_tile(pe, acc[b], WG.hi[b], WG.lo[b], y_hi, y_lo, KS, act_ready=y_split).then_inc(WG.gemm_done, 1)

            glu_tile(0, 0, 0)
            pe.wait_ge(ones_set, 1)
            for b in range(2):
                pe.wait_ge(summed[b], KD // 2)
            for c in range(NC):
                mm = pe.matmul(acc[1][:, c, 0:CH], ones[:], e_sum[:, c * CH:(c + 1) * CH], start=True, stop=True)
            mm.then_inc(norm_ready, 1)
            pe.wait_ge(norm_std, 1)
            glu_tile(1, 1, 0)
            with pe.Fori(1, KS // 2) as i:
                for b in range(2):
                    glu_tile(i * 2 + b, b, i)

        @block.scalar
        def _(act):
            for n in range(TT + 1):
                b, rows = n % 2, (P if n < TT else T_SAMPLE)
                act.wait_ge(p_turned, n + 1)
                nc.scalar.copy(p_hi[:, :, n * P:n * P + rows],
                               p_ps[b][:, 0:2 * P].rearrange("p (k t) -> p k t", k=KP)[:, :, 0:rows]) \
                    .then_inc(p_hi_done, 1)

            def embed(m, b, it):
                act.wait_ge(WE.gemm_done, m + 1)
                act.wait_ge(e_stored[b], it * 16)
                act.wait_ge(summed[b], it)
                nc.scalar.copy(e_out[b].rearrange("p (c t) -> p c t", c=NC), acc[b][:, :, 0:CH])
                nc.scalar.activation(e_sq[b].rearrange("p (c t) -> p c t", c=NC), acc[b][:, :, 0:CH],
                                     ACT.Square).then_inc(evacuated[b], 1)
                act.wait_ge(evacuated[b], it + 1)
                act.dma_start(d["eT"][bass.ds(m * P, P)], e_out[b][:]).then_inc(e_stored[b], 16)

            with act.Fori(0, KD // 4) as i:
                for b in range(2):
                    embed(i * 2 + b, b, i)
            act.wait_ge(y_loaded, 16)
            with act.Fori(KD // 4, KD // 2) as i:
                for b in range(2):
                    embed(i * 2 + b, b, i)
                    k = bass.ds(i * 2 + (b - KD // 2), 1)
                    nc.scalar.copy(y_hi[:, k], y_raw[:, k]).then_inc(y_hi_done, 1)

            def gate(m, b, it):
                act.wait_ge(WG.gemm_done, m + 1)
                act.wait_ge(gated_done[b], it)
                nc.scalar.activation(sig[b].rearrange("p (c t) -> p c t", c=NC), acc[b][:, :, 0:CH],
                                     ACT.Sigmoid).then_inc(evacuated[b], 1)

            def store(m, b, it):
                act.wait_ge(gated_done[b], it + 1)
                act.dma_start(d["mixT"][bass.ds(m * P + D_ATT, P)], out[b][:]).then_inc(mix_stored[b], 16)

            act.wait_ge(norm_ready, 1)
            nc.scalar.activation(e_sum.rearrange("p (c t) -> p c t", c=NC), acc[1][:, :, 0:CH], ACT.Sqrt,
                                 scale=1.0 / D_MODEL, bias=G["eps"][:]).then_inc(norm_std, 1)
            with act.Fori(0, KS // 2) as i:
                for b in range(2):
                    gate(i * 2 + b, b, i)
                    store(i * 2 + b, b, i)
            for b in range(2):
                act.wait_ge(e_stored[b], 16 * KD // 2)
                act.wait_ge(mix_stored[b], 16 * KS // 2)

        @block.vector
        def _(dve):
            chain = Chain(dve, dve_order)
            for n in range(TT + 1):
                b, rows = n % 2, (P if n < TT else T_SAMPLE)
                dve.wait_ge(p_hi_done, n + 1)
                nc.vector.tensor_tensor(p_lo[:, :, n * P:n * P + rows],
                                        p_ps[b][:, 0:2 * P].rearrange("p (k t) -> p k t", k=KP)[:, :, 0:rows],
                                        p_hi[:, :, n * P:n * P + rows].bitcast(F32), ALU.subtract) \
                    .then_inc(p_lo_done, 1)
            chain.link(nc.vector.memset(e_sum[:], 0.0))
            WE.split_tile(dve, nc, 0, 0, False)
            WE.split_tile(dve, nc, 1, 1, False)

            def add_squares(b, it):
                dve.wait_ge(evacuated[b], it + 1)
                nc.vector.tensor_tensor(e_sum[:], e_sum[:], e_sq[b][:], ALU.add).then_inc(summed[b], 1)
                dve.wait_ge(summed[b], it + 1)

            def low_y(k):
                dve.wait_ge(y_hi_done, k + 1)
                one = bass.ds(k, 1)
                nc.vector.tensor_tensor(y_lo[:, one], y_raw[:, one], y_hi[:, one].bitcast(F32), ALU.subtract) \
                    .then_inc(y_split, 1)

            with dve.Fori(0, KD // 4) as i:
                for b in range(2):
                    WE.split_tile(dve, nc, i * 2 + (b + 2), b, True)
                    add_squares(b, i)
            with dve.Fori(KD // 4, KD // 2 - 1) as i:
                for b in range(2):
                    WE.split_tile(dve, nc, i * 2 + (b + 2), b, True)
                    add_squares(b, i)
                    low_y(i * 2 + (b - KD // 2))
            for b in range(2):
                WG.split_tile(dve, nc, b, b, False)
                add_squares(b, KD // 2 - 1)
                low_y(KS - 2 + b)
            dve.wait_ge(norm_std, 1)
            chain.link(nc.vector.reciprocal(G["e_rstd"][:], e_sum[:]))

            def gate_y(m, b, i):
                dve.wait_ge(evacuated[b], i + (KD // 2 + 1))
                dve.wait_ge(gs_loaded[b], i * 16 + 16)
                dve.wait_ge(mix_stored[b], i * 16)
                chain.link(nc.vector.tensor_tensor(sig[b][:], sig[b][:], y_raw[:, bass.ds(m, 1)]
                                                   .rearrange("p a t -> p (a t)"), ALU.mult))
                nc.vector.tensor_tensor(out[b].rearrange("p (j k) -> p k j", k=L),
                                        sig[b].rearrange("p (k j) -> p k j", k=L),
                                        gs[b].rearrange("p (k j) -> p k j", k=L), ALU.mult) \
                    .then_inc(gated_done[b], 1)

            with dve.Fori(0, KS // 2 - 1) as i:
                chain.enter_loop(i, 2)
                for b in range(2):
                    WG.split_tile(dve, nc, i * 2 + (b + 2), b, True)
                    gate_y(i * 2 + b, b, i)
                chain.leave_loop(KS // 2 - 1)
            for b in range(2):
                gate_y(KS - 2 + b, b, KS // 2 - 1)



def stage_output(nc, d, G):
    WIDTH, BASE = (512, T - 512), (0, 512)
    ROWS = ([P] * 4, [P] * 4 + [T_SAMPLE])
    CHUNKS = ([(0, 512)], [(0, 272), (272, 272)])
    WM = max(WIDTH)
    YT = len(ROWS[1])
    RING = 4
    with ExitStack() as ctx:
        sb, ps, sem = allocators(nc, ctx)
        ident = G["ident"]
        W = Weights(sb, sem, "w_post", KD)
        hi, lo, y_tok, g_bc, mix_raw = [], [], [], [], []
        for r in range(2):
            start = (nc.sbuf_base + 31) // 32 * 32
            hi.append(sb(f"region{r}_hi", [P, KD, WM], F32R))
            lo.append(sb(f"region{r}_lo", [P, KD, WM], F32R))
            y_bytes = 4 * YT * D_MODEL
            y_tok.append(nc.alloc_sbuf_tensor_at(f"region{r}_y", [P, YT, D_MODEL], F32, offset=start))
            g_bc.append(nc.alloc_sbuf_tensor_at(f"region{r}_g", [P, D_MODEL], F32, offset=start + y_bytes))
            mix_raw.append(nc.alloc_sbuf_tensor_at(f"region{r}_raw", [P, RING, 2, WM], F32,
                                                   offset=start + y_bytes + 4 * D_MODEL))
            assert y_bytes + 4 * D_MODEL + 4 * RING * 2 * WM <= 2 * 4 * KD * WM
        side, total, sig, h2 = ([sb(f"{n}{b}", [P, WM]) for b in range(2)]
                                for n in ("side", "total", "gate_sig", "h2_"))
        junk = sb("junk", [P, YT, P])
        g_pe = sb("g_pe_s", [P, KD])
        ssq = sb("ssq_y", [P, YT, KD])
        var, std, rstd = (sb(n, [P, YT]) for n in ("var_y", "std_y", "rstd_y"))
        acc = [ps(f"post_acc{b}", [P, 2, 512]) for b in range(2)]
        tr_ps = [ps(f"y_ps{b}", [P, 2 * 512]) for b in range(2)]

        side_loaded, evacuated = ([sem(f"{n}{b}") for b in range(2)] for n in ("side_loaded", "post_evacuated"))
        mix_loaded = [sem(f"mix_loaded{s}") for s in range(RING)]
        mix_hi_done, mix_split, h_hi_done, h_split, total_done, h2_done = (
            sem(n) for n in ("mix_hi_done", "mix_split", "h_hi_done", "h_split", "total_done", "h2_done"))
        e_scaled, e_gated, ssq_zero = sem("e_scaled"), sem("e_gated"), sem("ssq_zero")
        turned, squared, y_filled, gains_loaded, g_loaded = (
            sem(n) for n in ("h2_turned", "h2_squared", "y_filled", "gains_loaded", "g_final_loaded"))
        var_summed, var_done, std_done, rstd_done, dve_scaled, act_scaled = (
            sem(n) for n in ("y_var_summed", "y_var_done", "y_std_done", "y_rstd_done", "dve_scaled", "act_scaled"))
        y_stored = [sem(f"y_stored{t}") for t in range(YT)]
        block = ctx.enter_context(nc.Block())
        w_out, w_pg = (d[n][0].rearrange("(k p) n -> p k n", p=P) for n in ("w_out", "w_pg"))
        mixT = d["mixT"].rearrange("(k p) t -> p k t", p=P)
        y_tiles = d["y_prompt"][0].rearrange("(i p) c -> i p c", p=P)
        ACT_TILES = (1, 3)

        def cols(ap, part):
            return ap[:, 0:WIDTH[part]].rearrange("p (c t) -> p c t", c=len(CHUNKS[part]))

        def acc_cols(b, part):
            return acc[b][:, 0:len(CHUNKS[part]), 0:CHUNKS[part][0][1]]

        def row(regions, part, m):
            return regions[1 - part][:, bass.ds(m, 1), 0:WIDTH[part]].rearrange("p a t -> p (a t)")

        def y_store(eng, part, t):
            rows = ROWS[part][t]
            dst = d["y_sample"][0] if rows < P else y_tiles[BASE[part] // P + t]
            eng.dma_start(dst, y_tok[part][0:rows, t]).then_inc(y_stored[t], 16)

        def stored_count(part, t):
            return 16 * sum(1 for q in range(part + 1) if t < len(ROWS[q]))

        @block.sync
        def _(sp):
            def load(phase, m, b, it):
                part, gate = phase // 2, phase % 2 == 1
                W.load(sp, w_pg if gate else w_out, m * P, m + phase * KD)
                if (gate and not isinstance(m, int)) or (not gate and isinstance(m, int) and part):
                    sp.wait_ge(e_scaled, m + (part * KD - 1))
                else:
                    sp.wait_ge(evacuated[b], it + phase * (KD // 2))
                sp.dma_start(side[b][:, 0:WIDTH[part]],
                             d["eT" if gate else "xT"][bass.ds(m * P, P), BASE[part]:BASE[part] + WIDTH[part]]) \
                  .then_inc(side_loaded[b], 16)

            for phase in range(4):
                for b in range(2):
                    load(phase, b, b, 0)
                with sp.Fori(1, KD // 2) as i:
                    for b in range(2):
                        load(phase, i * 2 + b, b, i)

        @block.gpsimd
        def _(pool):
            with nc.allow_non_contiguous_dma("per-feature columns of the gain"):
                pool.dma_start(g_pe[:], d["g_pe"][0].rearrange("(k p) -> p k", p=P)).then_inc(gains_loaded, 16)

            def load_mix(part, g):
                if g >= RING:
                    pool.wait_ge(mix_split, part * KD + 2 * (g - RING) + 2)
                raw = mix_raw[1 - part][:, g % RING, :, 0:WIDTH[part]]
                pool.dma_start(raw, mixT[:, 2 * g:2 * g + 2, BASE[part]:BASE[part] + WIDTH[part]]) \
                    .then_inc(mix_loaded[g % RING], 16)

            def rejoin(part, m, b):
                nc.gpsimd.tensor_tensor(total[b][:, 0:WIDTH[part]], row(hi, part, m).bitcast(F32),
                                        row(lo, part, m).bitcast(F32), ALU.add).then_inc(total_done, 1)

            for part in range(2):
                for g in range(0 if part == 0 else RING, KD // 2):
                    load_mix(part, g)
                if part == 1:
                    for t in range(len(ROWS[0])):
                        if t not in ACT_TILES:
                            pool.wait_ge(dve_scaled, t // 2 + 1)
                            y_store(pool, 0, t)
                pool.wait_ge(W.gemm_done, part * 2 * KD + KD)
                pool.dma_start(g_bc[part][:], d["g_final"].unsqueeze(0).to_broadcast([P, D_MODEL])) \
                    .then_inc(g_loaded, 16)
                if part == 0:
                    for g in range(RING):
                        load_mix(1, g)
                pool.wait_ge(h_split, part * KD + KD)
                for b in range(2):
                    rejoin(part, b, b)
                with pool.Fori(1, KD // 2) as i:
                    for b in range(2):
                        pool.wait_ge(h2_done, i * 2 + (part * KD + b - 1))
                        rejoin(part, i * 2 + b, b)
            for t in range(YT):
                if t not in ACT_TILES:
                    pool.wait_ge(dve_scaled, 2 + t // 2 + 1)
                    y_store(pool, 1, t)
            for t in range(YT):
                pool.wait_ge(y_stored[t], stored_count(1, t))

        @block.tensor
        def _(pe):
            def turn(part, m, b):
                pe.wait_ge(h2_done, m + (part * KD + 1))
                if part or not isinstance(m, int) or m >= 2:
                    pe.wait_ge(y_filled, m + (part * KD - 1))
                for t, rows in enumerate(ROWS[part]):
                    tr = pe.transpose(tr_ps[b][0:rows, t * P:(t + 1) * P], h2[b][:, t * P:t * P + rows], ident[:])
                tr.then_inc(turned, 1)

            def tile(phase, m, b, it, hook):
                part = phase // 2
                region = part if phase % 2 == 0 else 1 - part
                ready, base = (mix_split, part * KD) if phase % 2 == 0 else (h_split, part * KD)
                pe.wait_ge(W.split[1], m + (phase * KD + 1))
                pe.wait_ge(evacuated[b], it + phase * KD // 2)
                for k in range(KD):
                    pe.wait_ge(ready, base + k + 1)
                    if hook and k == KD // 2:
                        hook()
                    for n, (w, a) in enumerate(((W.hi[b], hi), (W.hi[b], lo), (W.lo[b], hi))):
                        for c, (start, width) in enumerate(CHUNKS[part]):
                            mm = pe.matmul(acc[b][:, c, 0:width], w[:, k, :],
                                           a[region][:, k, start:start + width],
                                           start=(k == 0 and n == 0), stop=(k == KD - 1 and n == 2))
                mm.then_inc(W.gemm_done, 1)

            with pe.Fori(0, KD // 2) as i:
                for b in range(2):
                    tile(0, i * 2 + b, b, i, None)
            for phase in range(1, 4):
                part = phase // 2
                gate = phase % 2 == 1
                tile(phase, 0, 0, 0, None if gate else (lambda: turn(part - 1, KD - 1, 1)))
                tile(phase, 1, 1, 0, (lambda: turn(part, 0, 0)) if gate else None)
                with pe.Fori(1, KD // 2) as i:
                    for b in range(2):
                        tile(phase, i * 2 + b, b, i, (lambda: turn(part, i * 2 + (b - 1), 1 - b)) if gate else None)
            turn(1, KD - 1, 1)

        @block.scalar
        def _(act):
            def high_mix(part, k):
                act.wait_ge(mix_loaded[k // 2 % RING], 16 * (part * 2 + k // 2 // RING + 1))
                if part == 1 and k == 0:
                    act.wait_ge(W.gemm_done, 2 * KD)
                    act.wait_ge(total_done, KD)
                nc.scalar.copy(hi[part][:, k, 0:WIDTH[part]],
                               mix_raw[1 - part][:, k // 2 % RING, k % 2, 0:WIDTH[part]]).then_inc(mix_hi_done, 1)

            def high_h(part, m, b, it):
                act.wait_ge(evacuated[b], it + (part * KD + 1))
                nc.scalar.copy(row(hi, part, m),
                               total[b][:, 0:WIDTH[part]]).then_inc(h_hi_done, 1)

            def sigmoid(part, m, b, it, used=True):
                act.wait_ge(W.gemm_done, m + (part * 2 * KD + KD + 1))
                if used:
                    act.wait_ge(h2_done, m + (part * KD - 1))
                nc.scalar.activation(cols(sig[b], part), acc_cols(b, part), ACT.Sigmoid).then_inc(evacuated[b], 1)

            def squares(part, m, b):
                act.wait_ge(turned, m + (part * KD + 1))
                if part or not isinstance(m, int) or m:
                    act.wait_ge(squared, m + part * KD)
                for t, rows in enumerate(ROWS[part]):
                    s = nc.scalar.activation(junk[0:rows, t], tr_ps[b][0:rows, t * P:(t + 1) * P], ACT.Square,
                                             accum_out=ssq[0:rows, t, bass.ds(m, 1)])
                s.then_inc(squared, 1)

            def tail(part):
                act.wait_ge(var_done, part + 1)
                nc.scalar.activation(std[:], var[:], ACT.Sqrt).then_inc(std_done, 1)
                act.wait_ge(rstd_done, part + 1)
                for t in ACT_TILES:
                    nc.scalar.mul(y_tok[part][:, t], y_tok[part][:, t], rstd[:, t:t + 1]) \
                        .then_inc(act_scaled, 1)
                    act.wait_ge(act_scaled, part * len(ACT_TILES) + ACT_TILES.index(t) + 1)
                    y_store(act, part, t)

            act.wait_ge(ssq_zero, 1)
            for part in range(2):
                if part == 0:
                    for k in range(KD):
                        high_mix(0, k)
                else:
                    for t in range(len(ROWS[0])):
                        act.wait_ge(y_stored[t], stored_count(0, t))
                with act.Fori(0, KD // 2) as i:
                    for b in range(2):
                        high_h(part, i * 2 + b, b, i)
                for m in range(2):
                    sigmoid(part, m, m, 0, used=part > 0)
                    squares(part, m, m)
                with act.Fori(1, KD // 2 - 1) as i:
                    for b in range(2):
                        sigmoid(part, i * 2 + b, b, i)
                        squares(part, i * 2 + b, b)
                sigmoid(part, KD - 2, 0, KD // 2 - 1)
                squares(part, KD - 2, 0)
                if part == 0:
                    for k in range(4):
                        high_mix(1, k)
                sigmoid(part, KD - 1, 1, KD // 2 - 1)
                if part == 0:
                    for k in range(4, KD):
                        high_mix(1, k)
                squares(part, KD - 1, 1)
                tail(part)

        @block.vector
        def _(dve):
            def low_mix(part, k):
                dve.wait_ge(mix_hi_done, part * KD + k + 1)
                w = WIDTH[part]
                nc.vector.tensor_tensor(lo[part][:, k, 0:w], mix_raw[1 - part][:, k // 2 % RING, k % 2, 0:w],
                                        hi[part][:, k, 0:w].bitcast(F32), ALU.subtract).then_inc(mix_split, 1)

            def residual(part, m, b, it):
                w = WIDTH[part]
                dve.wait_ge(W.gemm_done, m + (part * 2 * KD + 1))
                dve.wait_ge(side_loaded[b], it * 16 + 16 * (part * KD + 1))
                nc.vector.tensor_tensor(cols(total[b], part), acc_cols(b, part), cols(side[b], part), ALU.add) \
                    .then_inc(evacuated[b], 1)
                W.split_tile(dve, nc, m + (part * 2 * KD + 2), b, True)
                dve.wait_ge(h_hi_done, m + (part * KD + 1))
                nc.vector.tensor_tensor(row(lo, part, m), total[b][:, 0:w], row(hi, part, m).bitcast(F32),
                                        ALU.subtract).then_inc(h_split, 1)

            def gate(part, m, b, it, first=False):
                w = WIDTH[part]
                dve.wait_ge(side_loaded[b], it * 16 + 16 * (part * KD + KD // 2 + 1))
                if not first:
                    dve.wait_ge(turned, m + (part * KD - 1))
                nc.vector.scalar_tensor_tensor(
                    h2[b][:, 0:w], side[b][:, 0:w], g_pe[:, bass.ds(m, 1)],
                    G["e_rstd"][:, BASE[part]:BASE[part] + w], ALU.mult, ALU.mult).then_inc(e_scaled, 1)
                dve.wait_ge(e_scaled, m + (part * KD + 1))
                dve.wait_ge(evacuated[b], it + (part * KD + KD // 2 + 1))
                nc.vector.tensor_tensor(h2[b][:, 0:w], h2[b][:, 0:w], sig[b][:, 0:w], ALU.mult).then_inc(e_gated, 1)
                dve.wait_ge(e_gated, m + (part * KD + 1))
                dve.wait_ge(total_done, m + (part * KD + 1))
                nc.vector.tensor_tensor(h2[b][:, 0:w], h2[b][:, 0:w], total[b][:, 0:w], ALU.add) \
                    .then_inc(h2_done, 1)

            def fill(part, m, b):
                dve.wait_ge(squared, m + (part * KD + 1))
                dve.wait_ge(g_loaded, 16 * part + 16)
                full = sum(r == P for r in ROWS[part])
                span = bass.ds(m * P, P)
                f = nc.vector.tensor_tensor(y_tok[part][:, 0:full, span],
                                            tr_ps[b][:, 0:full * P].rearrange("p (i c) -> p i c", i=full),
                                            g_bc[part][:, span].unsqueeze(1).to_broadcast([P, full, P]), ALU.mult)
                if part == 1:
                    f = nc.vector.tensor_tensor(y_tok[part][0:T_SAMPLE, full, span],
                                                tr_ps[b][0:T_SAMPLE, full * P:(full + 1) * P],
                                                g_bc[part][0:T_SAMPLE, span], ALU.mult)
                f.then_inc(y_filled, 1)

            def tail(part):
                nc.vector.reduce_sum(var[:], ssq[:], axis=AX_X).then_inc(var_summed, 1)
                dve.wait_ge(var_summed, part + 1)
                nc.vector.tensor_scalar(var[:], var[:], 1.0 / D_MODEL, EPS, ALU.mult, ALU.add).then_inc(var_done, 1)
                dve.wait_ge(std_done, part + 1)
                dve.wait_ge(y_filled, part * KD + KD)
                if part:
                    dve.wait_ge(act_scaled, len(ACT_TILES))
                nc.vector.reciprocal(rstd[:], std[:]).then_inc(rstd_done, 1)
                dve.wait_ge(rstd_done, part + 1)
                for t, rows in enumerate(ROWS[part]):
                    if t not in ACT_TILES:
                        nc.vector.tensor_scalar(y_tok[part][0:rows, t], y_tok[part][0:rows, t], rstd[0:rows, t:t + 1],
                                                None, ALU.mult).then_inc(dve_scaled, 1)

            nc.vector.memset(ssq[:], 0.0).then_inc(ssq_zero, 1)
            dve.wait_ge(gains_loaded, 16)
            W.split_tile(dve, nc, 0, 0, False)
            for k in range(KD):
                low_mix(0, k)
            W.split_tile(dve, nc, 1, 1, False)
            for part in range(2):
                first_pg = part * 2 * KD + KD
                with dve.Fori(0, KD // 2) as i:
                    for b in range(2):
                        residual(part, i * 2 + b, b, i)
                for m in range(2):
                    gate(part, m, m, 0, first=part == 0)
                    W.split_tile(dve, nc, first_pg + m + 2, m, True)
                    fill(part, m, m)
                with dve.Fori(1, KD // 2 - 1) as i:
                    for b in range(2):
                        gate(part, i * 2 + b, b, i)
                        W.split_tile(dve, nc, i * 2 + (first_pg + b + 2), b, True)
                        fill(part, i * 2 + b, b)
                gate(part, KD - 2, 0, KD // 2 - 1)
                if part == 0:
                    W.split_tile(dve, nc, first_pg + KD, 0, True)
                fill(part, KD - 2, 0)
                if part == 0:
                    for k in range(4):
                        low_mix(1, k)
                gate(part, KD - 1, 1, KD // 2 - 1)
                if part == 0:
                    for k in range(4, KD):
                        low_mix(1, k)
                    W.split_tile(dve, nc, first_pg + KD + 1, 1, True)
                fill(part, KD - 1, 1)
                tail(part)



OUTS = [("y_prompt", (1, T_PROMPT, D_MODEL)), ("y_sample", (1, T_SAMPLE, D_MODEL)),
        ("k_prompt", (1, 1, T_PROMPT, HEADS, HD)), ("v_prompt", (1, 1, T_PROMPT, HEADS, HD)),
        ("logf_prompt", (1, 1, T_PROMPT, HEADS)),
        ("ssm_re_prompt", (1, 1, GROUPS, ST)), ("ssm_im_prompt", (1, 1, GROUPS, ST)),
        ("k_sample", (1, 1, T_SAMPLE, HEADS, HD)), ("v_sample", (1, 1, T_SAMPLE, HEADS, HD)),
        ("logf_sample", (1, 1, T_SAMPLE, HEADS)),
        ("ssm_re_sample", (1, 1, GROUPS, ST)), ("ssm_im_sample", (1, 1, GROUPS, ST))]
SCRATCH = [("xT", (D_MODEL, T)),
           ("zT", (4 * D_ATT, T)),
           ("uT", (2 * D_SSM, L, NJ)),
           ("toep", (P, GROUPS, P)),
           ("w_state", (P, GROUPS, P)),
           ("w_read", (P, GROUPS, P)),
           ("yT", (D_SSM, L, NJ)),
           ("negc", (HEADS, T_PROMPT + T_PAST + T_SAMPLE)),
           ("mixT", (D_MODEL, T)),
           ("eT", (D_MODEL, T))]
SCRATCH_KIND = "Internal"


def clear_semaphores(nc, first, free):
    with nc.Block() as block:
        @block.gpsimd
        def _(pool):
            nc.gpsimd.sem_clear(range(first, max(free) + 1))


def program(nc, d, stages=None):
    for name, shape in SCRATCH:
        d[name] = nc.dram_tensor(name, shape, F32, kind=SCRATCH_KIND).ap()
    with ExitStack() as ctx:
        sb, ps, sem = allocators(nc, ctx)
        pool_sems = {n: sem(n) for n in ("xT_stored0", "xT_stored1", "gate_stored", "const_stored",
                                         "v_swapped", "y_stored", "hl_stored", "k_stored", "v_stored", "mix_stored",
                                         "y_loaded", "gs_loaded0", "gs_loaded1")}
        G = {"sem": pool_sems, "passed": sem("passed"), "ident": sb("ident", [P, P]), "ones_col": sb("ones_col", [P, 1]), "eps": sb("eps", [P, 1])}
        first_sem = nc.free_semaphores[0]
        with ExitStack() as ctx_n:
            sb_n, _, _ = allocators(nc, ctx_n)
            G["n_hi"] = sb_n("n_hi", [P, KD, T], F32R)
            G["n_lo"] = sb_n("n_lo", [P, KD, T], F32R)
            stage_norm(nc, d, G)
            stage_project(nc, d, G)
        stage_attention(nc, d, G)
        clear_semaphores(nc, first_sem, nc.free_semaphores)
        G["e_rstd"] = sb("e_rstd", [P, T])
        stage_side(nc, d, G)
        stage_output(nc, d, G)


INS = ("x_prompt", "x_sample", "p_prompt", "p_sample", "cache_k", "cache_v", "cache_logf", "state_ssm_re",
       "state_ssm_im", "g_in", "w_in", "b_f", "a_re", "a_im", "log_dt", "b_re", "b_im", "c_re", "c_im", "d_skip",
       "w_glu", "w_out", "w_pe", "g_pe", "w_pg", "g_final")


def kernel(**inputs):
    import concourse.bacc as bacc
    from concourse.bass_utils import run_bass_kernel_spmd

    nc = bacc.Bacc("TRN2", target_bir_lowering=False, num_devices=1)
    arrays, d = {}, {}
    for name in INS:
        a = np.ascontiguousarray(inputs[name])
        arrays[f"in_{name}_dram"] = a
        d[name] = nc.dram_tensor(f"in_{name}_dram", a.shape, mybir.dt.from_np(a.dtype), kind="ExternalInput").ap()
    for i, (name, shape) in enumerate(OUTS):
        d[name] = nc.dram_tensor(f"out_{i}_dram", shape, F32, kind="ExternalOutput").ap()
    program(nc, d)
    r = run_bass_kernel_spmd(nc, [arrays], core_ids=[0])
    return tuple(r.results[0][f"out_{i}_dram"] for i in range(len(OUTS)))
```
